# Optimizing a Trainium2 kernel written in Bass

```python
import jax
import jax.numpy as jnp
from jax import lax
import numpy as np

D_MODEL = 2048
BATCH = 1
SEQ = 256
DEPTH = 1
DEC_BATCH = 8
DEC_SEQ = 4
PAST_LEN = 2048
PAGE_SIZE = 128

HEAD_DIM = 128
NSA_WIDTH = D_MODEL // 2
NSA_HEADS = NSA_WIDTH // HEAD_DIM
NSA_KV_HEADS = 2
HPG = NSA_HEADS // NSA_KV_HEADS
KV_WIDTH = NSA_KV_HEADS * HEAD_DIM
CMP_BLOCK = 32
CMP_STRIDE = 16
SEL_BLOCK = 64
N_SELECT = 16
WINDOW = 512
FORCE_BONUS = 1e4
SEL_QBLOCK = 32
WIN_QBLOCK = 128
RWKV_WIDTH = D_MODEL - NSA_WIDTH
RWKV_HEAD_DIM = 64
RWKV_HEADS = RWKV_WIDTH // RWKV_HEAD_DIM
DECAY_LORA = 64
ICLR_LORA = 64
GATE_LORA = 128
GN_EPS = 64e-5
MIX_WIDTH = NSA_WIDTH + RWKV_WIDTH
N_GROUPS = 4
EXPERTS_PER_GROUP = 8
N_EXPERTS = N_GROUPS * EXPERTS_PER_GROUP
EXPERT_TOP_K = 2
D_EXPERT = 512
MOE_BLOCK = 64
NORM_EPS = 1e-6
NEG_INF = -1e30
Q_OFF = 0
CMP_OFF = Q_OFF + NSA_WIDTH
SLC_OFF = CMP_OFF + 2 * KV_WIDTH
WIN_OFF = SLC_OFF + 2 * KV_WIDTH
RKV_OFF = WIN_OFF + 2 * KV_WIDTH
GATE_OFF = RKV_OFF + 3 * RWKV_WIDTH
IN_WIDTH = GATE_OFF + 3 * NSA_HEADS

kernel_name = 'hymba_nsa_rwkv7_hmoe_step'

def rmsnorm(x, g):
    xf = x.astype(jnp.float32)
    y = xf * lax.rsqrt(jnp.mean(xf * xf, axis=-1, keepdims=True) + NORM_EPS)
    return (y * g.astype(jnp.float32)).astype(x.dtype)

def alibi_slopes():
    n = jnp.arange(1, NSA_HEADS + 1, dtype=jnp.float32)
    return jnp.exp2(-8.0 * n / NSA_HEADS).reshape(NSA_KV_HEADS, HPG)

def compress_blocks(rows, w1, pe, w2):
    B, L = rows.shape[:2]
    n_chunk = L // CMP_STRIDE
    r = CMP_BLOCK // CMP_STRIDE
    nc = n_chunk - r + 1
    ch = rows.reshape(B, n_chunk, CMP_STRIDE, NSA_KV_HEADS, HEAD_DIM)
    pre = jnp.einsum('pd,pde->e', pe, w1)
    for i in range(r):
        pre = pre + jnp.einsum('bcpgd,pde->bcge', ch[:, i:i + nc], w1[i * CMP_STRIDE:(i + 1) * CMP_STRIDE])
    return jnp.einsum('bcge,ef->bcgf', jax.nn.silu(pre), w2)

def overlap_matrix(nc, ns):
    c_start = jnp.arange(nc) * CMP_STRIDE
    c_end = c_start + CMP_BLOCK - 1
    s_start = jnp.arange(ns) * SEL_BLOCK
    s_end = s_start + SEL_BLOCK - 1
    return ((c_start[:, None] <= s_end[None]) & (c_end[:, None] >= s_start[None])).astype(jnp.float32)

def compressed_branch(qg, pos_q, kc, vc, n_sel, slopes):
    nc = kc.shape[1]
    end_c = jnp.arange(nc) * CMP_STRIDE + CMP_BLOCK - 1
    dist = pos_q[:, None] - end_c[None, :]
    valid = (dist >= 0)[None, :, None, None, :]
    s = jnp.einsum('btghd,bcgd->btghc', qg, kc).astype(jnp.float32) * HEAD_DIM ** -0.5
    s = s - slopes[None, None, :, :, None] * dist.astype(jnp.float32)[None, :, None, None, :]
    p = jax.nn.softmax(jnp.where(valid, s, NEG_INF), axis=-1) * valid
    o = jnp.einsum('btghc,bcgd->btghd', p.astype(vc.dtype), vc)
    imp = jnp.einsum('btghc,cj->btgj', p, overlap_matrix(nc, n_sel))
    blk_t = (pos_q // SEL_BLOCK)[:, None]
    j = jnp.arange(n_sel)[None, :]
    forced = (j == 0) | (j == blk_t) | (j == blk_t - 1)
    imp = jnp.where(forced[None, :, None, :], imp + FORCE_BONUS, imp)
    imp = jnp.where((j <= blk_t)[None, :, None, :], imp, NEG_INF)
    top_val, top_idx = lax.top_k(imp, min(N_SELECT, n_sel))
    return o, top_idx, top_val > 0.5 * NEG_INF

def gather_selected(idx, new_blk, n_past_blk, pool, layer, page_table):
    b_idx = jnp.arange(idx.shape[0])[:, None, None, None]
    g_idx = jnp.arange(NSA_KV_HEADS)[None, None, :, None]
    local = jnp.clip(idx - n_past_blk, 0, new_blk.shape[1] - 1)
    blk = new_blk[b_idx, local, :, :, g_idx]
    if pool is not None:
        sub_per_page = PAGE_SIZE // SEL_BLOCK
        past = jnp.clip(idx, 0, n_past_blk - 1)
        phys = page_table[b_idx, past // sub_per_page]
        pool_r = pool.reshape(pool.shape[0], pool.shape[1], sub_per_page, SEL_BLOCK, 2, NSA_KV_HEADS, HEAD_DIM)
        l_idx = jnp.full_like(phys, layer)
        pblk = pool_r[l_idx, phys, past % sub_per_page, :, :, g_idx]
        blk = jnp.where((idx < n_past_blk)[..., None, None, None], pblk, blk)
    return blk[..., 0, :], blk[..., 1, :]

def selected_branch(qg, pos_q, kb, vb, idx, sel_valid, slopes):
    B, Tq, G, H, _ = qg.shape
    s = jnp.einsum('btghd,btgkpd->btghkp', qg, kb).astype(jnp.float32) * HEAD_DIM ** -0.5
    key_pos = idx[..., None] * SEL_BLOCK + jnp.arange(SEL_BLOCK)
    dist = pos_q[None, :, None, None, None] - key_pos
    mask = ((dist >= 0) & sel_valid[..., None])[:, :, :, None]
    s = s - slopes[None, None, :, :, None, None] * dist.astype(jnp.float32)[:, :, :, None]
    s = jnp.where(mask, s, NEG_INF)
    p = jax.nn.softmax(s.reshape(B, Tq, G, H, -1), axis=-1).reshape(s.shape)
    return jnp.einsum('btghkp,btgkpd->btghd', p.astype(vb.dtype), vb)

def window_attend(qg, pos_q, k, v, key_pos, slopes):
    s = jnp.einsum('btghd,bsgd->btghs', qg, k).astype(jnp.float32) * HEAD_DIM ** -0.5
    dist = pos_q[:, None] - key_pos[None, :]
    mask = ((dist >= 0) & (dist < WINDOW) & (key_pos[None, :] >= 0))[None, :, None, None, :]
    s = s - slopes[None, None, :, :, None] * dist.astype(jnp.float32)[None, :, None, None, :]
    p = jax.nn.softmax(jnp.where(mask, s, NEG_INF), axis=-1)
    return jnp.einsum('btghs,bsgd->btghd', p.astype(v.dtype), v)

def nsa_group(proj, pos_q, lp, layer, pool_cmp, pool_slc, page_table, win_buf):
    B, T = proj.shape[:2]
    G, dh = NSA_KV_HEADS, HEAD_DIM
    slopes = alibi_slopes()
    qg = proj[..., Q_OFF:CMP_OFF].reshape(B, T, G, HPG, dh)
    cmp_new = proj[..., CMP_OFF:SLC_OFF].reshape(B, T, 2, G, dh)
    slc_new = proj[..., SLC_OFF:WIN_OFF].reshape(B, T, 2, G, dh)
    win_new = proj[..., WIN_OFF:RKV_OFF].reshape(B, T, 2, G, dh)
    gates = jax.nn.sigmoid(proj[..., GATE_OFF:IN_WIDTH].astype(jnp.float32)).reshape(B, T, 3, G, HPG, 1)

    if pool_cmp is None:
        n_past = 0
        cmp_rows = cmp_new
    else:
        n_past = page_table.shape[1] * PAGE_SIZE
        past_rows = pool_cmp[layer, page_table].reshape(B, -1, 2, G, dh)
        cmp_rows = jnp.concatenate([past_rows, cmp_new], axis=1)
    l16 = (cmp_rows.shape[1] // CMP_STRIDE) * CMP_STRIDE
    kc = compress_blocks(cmp_rows[:, :l16, 0], lp['cmp_k_w1'], lp['cmp_k_pe'], lp['cmp_k_w2'])
    vc = compress_blocks(cmp_rows[:, :l16, 1], lp['cmp_v_w1'], lp['cmp_v_pe'], lp['cmp_v_w2'])
    n_sel = -(-(n_past + T) // SEL_BLOCK)
    o_cmp, idx, sel_valid = compressed_branch(qg, pos_q, kc, vc, n_sel, slopes)

    n_past_blk = n_past // SEL_BLOCK
    n_new_blk = -(-T // SEL_BLOCK)
    new_blk = jnp.pad(slc_new, ((0, 0), (0, n_new_blk * SEL_BLOCK - T), (0, 0), (0, 0), (0, 0)))
    new_blk = new_blk.reshape(B, n_new_blk, SEL_BLOCK, 2, G, dh)

    def sel_block(args):
        q_b, pos_b, idx_b, valid_b = args
        kb, vb = gather_selected(idx_b, new_blk, n_past_blk, pool_slc, layer, page_table)
        return selected_branch(q_b, pos_b, kb, vb, idx_b, valid_b, slopes)

    if T > SEL_QBLOCK and T % SEL_QBLOCK == 0:
        nqb = T // SEL_QBLOCK

        def blocks(a):
            return a.reshape((B, nqb, SEL_QBLOCK) + a.shape[2:]).swapaxes(0, 1)

        o_sel = lax.map(sel_block, (blocks(qg), pos_q.reshape(nqb, SEL_QBLOCK), blocks(idx), blocks(sel_valid)))
        o_sel = o_sel.swapaxes(0, 1).reshape(B, T, G, HPG, dh)
    else:
        o_sel = sel_block((qg, pos_q, idx, sel_valid))

    win_len = min(WINDOW, PAST_LEN)
    if win_buf is None:
        nq = T // WIN_QBLOCK
        n_pre = -(-WINDOW // WIN_QBLOCK)
        kp = jnp.pad(win_new, ((0, 0), (n_pre * WIN_QBLOCK, 0), (0, 0), (0, 0), (0, 0)))
        kp = kp.reshape(B, nq + n_pre, WIN_QBLOCK, 2, G, dh)
        band = jnp.concatenate([kp[:, i:i + nq] for i in range(n_pre + 1)], axis=2)
        key_pos = (jnp.arange(nq)[:, None] - n_pre) * WIN_QBLOCK + jnp.arange((n_pre + 1) * WIN_QBLOCK)[None]
        o_win = jax.vmap(window_attend, in_axes=(1, 0, 1, 1, 0, None), out_axes=1)(
            qg.reshape(B, nq, WIN_QBLOCK, G, HPG, dh), pos_q.reshape(nq, WIN_QBLOCK),
            band[:, :, :, 0], band[:, :, :, 1], key_pos, slopes).reshape(B, T, G, HPG, dh)
        pad_rows = jnp.zeros((B, win_len, 2, G, dh), win_new.dtype)
        win_state = jnp.concatenate([pad_rows, win_new], axis=1)[:, -win_len:]
    else:
        keys = jnp.concatenate([win_buf, win_new], axis=1)
        key_pos = n_past - win_buf.shape[1] + jnp.arange(keys.shape[1])
        o_win = window_attend(qg, pos_q, keys[:, :, 0], keys[:, :, 1], key_pos, slopes)
        win_state = keys[:, -win_buf.shape[1]:]

    o = gates[:, :, 0] * o_cmp + gates[:, :, 1] * o_sel + gates[:, :, 2] * o_win
    return o.reshape(B, T, NSA_WIDTH).astype(proj.dtype), cmp_new, slc_new, win_state

def rwkv_group(h, h_shift, p_rkv, p_rkv_prev, wkv0, lp):
    B, T, _ = h.shape
    f32 = jnp.float32
    rkv = (p_rkv + lp['mu_rkv'] * (p_rkv_prev - p_rkv)).astype(f32)
    r, k, v = jnp.split(rkv, 3, axis=-1)
    xx = h_shift - h
    xw = h + xx * lp['mu_wag'][0]
    xa = h + xx * lp['mu_wag'][1]
    xg = h + xx * lp['mu_wag'][2]
    w_log = -jax.nn.softplus(-(lp['decay_w0'] + jnp.tanh(xw @ lp['decay_w1']) @ lp['decay_w2']).astype(f32)) - 0.5
    decay = jnp.exp(-jnp.exp(w_log))
    a = jax.nn.sigmoid((lp['iclr_a0'] + (xa @ lp['iclr_a1']) @ lp['iclr_a2']).astype(f32))
    g = (jax.nn.sigmoid(xg @ lp['gate_g1']) @ lp['gate_g2']).astype(f32)

    def heads(t):
        return t.reshape(B, T, RWKV_HEADS, RWKV_HEAD_DIM)

    kk = heads(k * lp['k_k'])
    kk = kk / jnp.maximum(jnp.sqrt(jnp.sum(kk * kk, axis=-1, keepdims=True)), 1e-12)
    k = k * (1.0 + (a - 1.0) * lp['k_a'])
    r_h, k_h, v_h, w_h, a_h = heads(r), heads(k), heads(v), heads(decay), heads(a)

    def step(S, inp):
        r_t, w_t, k_t, v_t, kk_t, a_t = inp
        sa = jnp.einsum('bhij,bhj->bhi', S, -kk_t)
        S = S * w_t[:, :, None, :] + sa[..., None] * (kk_t * a_t)[:, :, None, :] + v_t[..., None] * k_t[:, :, None, :]
        return S, jnp.einsum('bhij,bhj->bhi', S, r_t)

    seq = tuple(jnp.moveaxis(t, 1, 0) for t in (r_h, w_h, k_h, v_h, kk, a_h))
    S_T, ys = lax.scan(step, wkv0.astype(f32), seq)
    y = jnp.moveaxis(ys, 0, 1)
    mu = jnp.mean(y, axis=-1, keepdims=True)
    var = jnp.mean(jnp.square(y - mu), axis=-1, keepdims=True)
    y = ((y - mu) * lax.rsqrt(var + GN_EPS)).reshape(B, T, RWKV_WIDTH) * lp['ln_x_w'] + lp['ln_x_b']
    bonus = (jnp.sum(r_h * k_h * lp['r_k'], axis=-1, keepdims=True) * v_h).reshape(B, T, RWKV_WIDTH)
    return (y + bonus) * g, S_T

def hier_route(h, w_rg, b_rg, w_re, b_re):
    n = h.shape[0]
    pg = jax.nn.softmax((h @ w_rg + b_rg).astype(jnp.float32), axis=-1)
    g_val, g_sel = lax.top_k(pg, 1)
    le = (h @ w_re + b_re).astype(jnp.float32).reshape(n, N_GROUPS, EXPERTS_PER_GROUP)
    le_g = jnp.take_along_axis(le, g_sel[:, :, None], axis=1)[:, 0]
    e_val, e_sel = lax.top_k(le_g, EXPERT_TOP_K)
    weights = jax.nn.softmax(e_val, axis=-1) * g_val
    return g_sel * EXPERTS_PER_GROUP + e_sel, weights

def moe_ffn(h, eid, ew, w_gate, w_up, w_down):
    n, d = h.shape
    a_tot = n * EXPERT_TOP_K
    flat_e = eid.reshape(-1)
    flat_t = jnp.arange(a_tot) // EXPERT_TOP_K
    flat_w = ew.reshape(-1)
    order = jnp.argsort(flat_e)
    se, st, sw = flat_e[order], flat_t[order], flat_w[order]
    counts = jnp.bincount(flat_e, length=N_EXPERTS)
    padded = (counts + MOE_BLOCK - 1) // MOE_BLOCK * MOE_BLOCK
    pad_end = jnp.cumsum(padded)
    pad_start = pad_end - padded
    start = jnp.cumsum(counts) - counts
    dest = pad_start[se] + jnp.arange(a_tot) - start[se]
    n_blk = (a_tot + N_EXPERTS * (MOE_BLOCK - 1) + MOE_BLOCK - 1) // MOE_BLOCK
    tok_buf = jnp.full((n_blk * MOE_BLOCK,), n, jnp.int32).at[dest].set(st)
    h_pad = jnp.concatenate([h, jnp.zeros((1, d), h.dtype)], axis=0)
    xb = h_pad[tok_buf].reshape(n_blk, MOE_BLOCK, d)
    blk_e = jnp.clip(jnp.searchsorted(pad_end, jnp.arange(n_blk) * MOE_BLOCK, side='right'), 0, N_EXPERTS - 1)

    def expert_block(args):
        xblk, e = args
        return (jax.nn.silu(xblk @ w_gate[e]) * (xblk @ w_up[e])) @ w_down[e]

    yb = lax.map(expert_block, (xb, blk_e)).reshape(n_blk * MOE_BLOCK, d)
    out = jnp.zeros((n, d), jnp.float32).at[st].add(yb[dest].astype(jnp.float32) * sw[:, None])
    return out.astype(h.dtype)

def decoder_layer(x, c, pos_q, lp, layer, pool_cmp, pool_slc, page_table, win_buf, wkv0, shift0):
    B, T, D = x.shape
    mod = jax.nn.silu(c) @ lp['w_ada'] + lp['b_ada']
    sh1, sc1, gt1, sh2, sc2, gt2 = jnp.split(mod[:, None, :], 6, axis=-1)
    h = rmsnorm(x, lp['norm1']) * (1.0 + sc1) + sh1
    proj = h @ lp['w_in']
    shift0 = shift0.astype(h.dtype)
    h_shift = jnp.concatenate([shift0[:, None], h[:, :-1]], axis=1)
    p_rkv = proj[..., RKV_OFF:GATE_OFF]
    p_rkv_prev = jnp.concatenate([(shift0 @ lp['w_in'][:, RKV_OFF:GATE_OFF])[:, None], p_rkv[:, :-1]], axis=1)
    o_nsa, cmp_new, slc_new, win_state = nsa_group(proj, pos_q, lp, layer, pool_cmp, pool_slc, page_table, win_buf)
    o_rwkv, wkv_T = rwkv_group(h, h_shift, p_rkv, p_rkv_prev, wkv0, lp)
    mixed = jnp.concatenate([o_nsa, o_rwkv.astype(o_nsa.dtype)], axis=-1) @ lp['w_out']
    x = x + gt1 * mixed
    h2 = (rmsnorm(x, lp['norm2']) * (1.0 + sc2) + sh2).reshape(B * T, D)
    eid, ew = hier_route(h2, lp['w_router_group'], lp['b_router_group'], lp['w_router_expert'], lp['b_router_expert'])
    ffn = moe_ffn(h2, eid, ew, lp['w_gate'], lp['w_up'], lp['w_down']).reshape(B, T, D)
    x = x + gt2 * ffn
    return x, cmp_new, slc_new, win_state, wkv_T, h[:, -1]

def setup_inputs(seed: int = 0) -> dict:
    key = jax.random.key(seed)
    keys = iter(jax.random.split(key, 64))

    def nrm(shape, scale=1.0):
        return jax.random.normal(next(keys), shape, jnp.float32) * scale

    def gain(shape):
        return 1.0 + nrm(shape, 0.02)

    def unif(shape):
        return jax.random.uniform(next(keys), shape, jnp.float32)

    n_pages = PAST_LEN // PAGE_SIZE
    n_phys = (DEC_BATCH * n_pages * 5) // 4
    win_len = min(WINDOW, PAST_LEN)
    row = (2, NSA_KV_HEADS, HEAD_DIM)
    perm = jax.random.permutation(next(keys), n_phys)
    page_table = perm[:DEC_BATCH * n_pages].reshape(DEC_BATCH, n_pages).astype(jnp.int32)
    L = DEPTH
    D = D_MODEL
    return {
        'x_prompt': nrm((BATCH, SEQ, D)),
        'x_sample': nrm((DEC_BATCH, DEC_SEQ, D)),
        'c_prompt': nrm((BATCH, D)),
        'c_sample': nrm((DEC_BATCH, D)),
        'cache_cmp_kv': nrm((L, n_phys, PAGE_SIZE) + row),
        'cache_slc_kv': nrm((L, n_phys, PAGE_SIZE) + row),
        'page_table': page_table,
        'state_win_kv': nrm((L, DEC_BATCH, win_len) + row),
        'state_wkv': nrm((L, DEC_BATCH, RWKV_HEADS, RWKV_HEAD_DIM, RWKV_HEAD_DIM), 0.5),
        'state_shift': nrm((L, DEC_BATCH, D)),
        'w_ada': nrm((L, D, 6 * D), 0.5 * D ** -0.5),
        'b_ada': nrm((L, 6 * D), 0.02),
        'norm1': gain((L, D)),
        'w_in': nrm((L, D, IN_WIDTH), D ** -0.5),
        'cmp_k_w1': nrm((L, CMP_BLOCK, HEAD_DIM, HEAD_DIM), (CMP_BLOCK * HEAD_DIM) ** -0.5),
        'cmp_k_pe': nrm((L, CMP_BLOCK, HEAD_DIM), 0.5),
        'cmp_k_w2': nrm((L, HEAD_DIM, HEAD_DIM), HEAD_DIM ** -0.5),
        'cmp_v_w1': nrm((L, CMP_BLOCK, HEAD_DIM, HEAD_DIM), (CMP_BLOCK * HEAD_DIM) ** -0.5),
        'cmp_v_pe': nrm((L, CMP_BLOCK, HEAD_DIM), 0.5),
        'cmp_v_w2': nrm((L, HEAD_DIM, HEAD_DIM), HEAD_DIM ** -0.5),
        'mu_rkv': unif((L, 3 * RWKV_WIDTH)),
        'mu_wag': unif((L, 3, D)),
        'decay_w0': nrm((L, RWKV_WIDTH), 0.5),
        'decay_w1': nrm((L, D, DECAY_LORA), D ** -0.5),
        'decay_w2': nrm((L, DECAY_LORA, RWKV_WIDTH), 0.5 * DECAY_LORA ** -0.5),
        'iclr_a0': nrm((L, RWKV_WIDTH), 0.5),
        'iclr_a1': nrm((L, D, ICLR_LORA), D ** -0.5),
        'iclr_a2': nrm((L, ICLR_LORA, RWKV_WIDTH), 0.5 * ICLR_LORA ** -0.5),
        'gate_g1': nrm((L, D, GATE_LORA), D ** -0.5),
        'gate_g2': nrm((L, GATE_LORA, RWKV_WIDTH), GATE_LORA ** -0.5),
        'k_k': 0.85 + nrm((L, RWKV_WIDTH), 0.05),
        'k_a': gain((L, RWKV_WIDTH)),
        'r_k': nrm((L, RWKV_HEADS, RWKV_HEAD_DIM), 0.1),
        'ln_x_w': gain((L, RWKV_WIDTH)),
        'ln_x_b': nrm((L, RWKV_WIDTH), 0.02),
        'w_out': nrm((L, MIX_WIDTH, D), MIX_WIDTH ** -0.5),
        'norm2': gain((L, D)),
        'w_router_group': nrm((L, D, N_GROUPS), D ** -0.5),
        'b_router_group': nrm((L, N_GROUPS), 0.01),
        'w_router_expert': nrm((L, D, N_EXPERTS), D ** -0.5),
        'b_router_expert': nrm((L, N_EXPERTS), 0.01),
        'w_gate': nrm((L, N_EXPERTS, D, D_EXPERT), D ** -0.5),
        'w_up': nrm((L, N_EXPERTS, D, D_EXPERT), D ** -0.5),
        'w_down': nrm((L, N_EXPERTS, D_EXPERT, D), D_EXPERT ** -0.5),
        'norm_f': gain((D,)),
    }

def reference(x_prompt, x_sample, c_prompt, c_sample, cache_cmp_kv, cache_slc_kv, page_table,
              state_win_kv, state_wkv, state_shift, w_ada, b_ada, norm1, w_in,
              cmp_k_w1, cmp_k_pe, cmp_k_w2, cmp_v_w1, cmp_v_pe, cmp_v_w2,
              mu_rkv, mu_wag, decay_w0, decay_w1, decay_w2, iclr_a0, iclr_a1, iclr_a2,
              gate_g1, gate_g2, k_k, k_a, r_k, ln_x_w, ln_x_b, w_out, norm2,
              w_router_group, b_router_group, w_router_expert, b_router_expert,
              w_gate, w_up, w_down, norm_f):
    bp, tp = x_prompt.shape[:2]
    bs, ts = x_sample.shape[:2]
    pos_p = jnp.arange(tp)
    pos_s = page_table.shape[1] * PAGE_SIZE + jnp.arange(ts)
    hp, hs = x_prompt, x_sample
    cmp_p, cmp_s, slc_p, slc_s, win_p, win_s = [], [], [], [], [], []
    wkv_p, wkv_s, sft_p, sft_s = [], [], [], []
    for l in range(DEPTH):
        lp = dict(w_ada=w_ada[l], b_ada=b_ada[l], norm1=norm1[l], w_in=w_in[l],
                  cmp_k_w1=cmp_k_w1[l], cmp_k_pe=cmp_k_pe[l], cmp_k_w2=cmp_k_w2[l],
                  cmp_v_w1=cmp_v_w1[l], cmp_v_pe=cmp_v_pe[l], cmp_v_w2=cmp_v_w2[l],
                  mu_rkv=mu_rkv[l], mu_wag=mu_wag[l], decay_w0=decay_w0[l], decay_w1=decay_w1[l],
                  decay_w2=decay_w2[l], iclr_a0=iclr_a0[l], iclr_a1=iclr_a1[l], iclr_a2=iclr_a2[l],
                  gate_g1=gate_g1[l], gate_g2=gate_g2[l], k_k=k_k[l], k_a=k_a[l], r_k=r_k[l],
                  ln_x_w=ln_x_w[l], ln_x_b=ln_x_b[l], w_out=w_out[l], norm2=norm2[l],
                  w_router_group=w_router_group[l], b_router_group=b_router_group[l],
                  w_router_expert=w_router_expert[l], b_router_expert=b_router_expert[l],
                  w_gate=w_gate[l], w_up=w_up[l], w_down=w_down[l])
        wkv_zero = jnp.zeros((bp, RWKV_HEADS, RWKV_HEAD_DIM, RWKV_HEAD_DIM), jnp.float32)
        shift_zero = jnp.zeros((bp, D_MODEL), x_prompt.dtype)
        hp, a1, a2, a3, a4, a5 = decoder_layer(hp, c_prompt, pos_p, lp, l, None, None, None, None, wkv_zero, shift_zero)
        hs, b1, b2, b3, b4, b5 = decoder_layer(hs, c_sample, pos_s, lp, l, cache_cmp_kv, cache_slc_kv, page_table,
                                               state_win_kv[l], state_wkv[l], state_shift[l])
        cmp_p.append(a1); slc_p.append(a2); win_p.append(a3); wkv_p.append(a4); sft_p.append(a5)
        cmp_s.append(b1); slc_s.append(b2); win_s.append(b3); wkv_s.append(b4); sft_s.append(b5)
    y_prompt = rmsnorm(hp, norm_f)
    y_sample = rmsnorm(hs, norm_f)
    return (y_prompt, y_sample,
            jnp.stack(cmp_p), jnp.stack(cmp_s), jnp.stack(slc_p), jnp.stack(slc_s),
            jnp.stack(win_p), jnp.stack(win_s), jnp.stack(wkv_p), jnp.stack(wkv_s),
            jnp.stack(sft_p), jnp.stack(sft_s))


_drawn_inputs = setup_inputs


def setup_inputs(seed=0):
    import zlib

    import numpy as np

    out = dict(_drawn_inputs(seed))
    spreads = {}
    factors = {'cmp_k_w1': 4.412,
     'cmp_k_pe': 8.0,
     'cmp_k_w2': 4.134,
     'k_k': 3.877,
     'k_a': 2.747,
     'ln_x_w': 8.0,
     'ln_x_b': 8.0,
     'norm2': 4.165,
     'b_router_group': 8.0,
     'b_router_expert': 8.0,
     'norm_f': 2.869}
    for name, (base, spread) in spreads.items():
        noise = np.random.default_rng([zlib.crc32(name.encode()), seed]).standard_normal(out[name].shape)
        drawn = base * np.exp(spread * noise) if base else spread * noise
        out[name] = jnp.asarray(drawn.astype(out[name].dtype))
    for name, factor in factors.items():
        out[name] = (out[name] * factor).astype(out[name].dtype)
    return out
```

```python
from contextlib import ExitStack

import concourse.bass as bass
from concourse import mybir

F32 = mybir.dt.float32
I32 = mybir.dt.int32
U32 = mybir.dt.uint32
ALU = mybir.AluOpType
ACT = mybir.ActivationFunctionType
AX = mybir.AxisListType

P = 128
D = 2048
KT = D // P
TP = 256
NB = 8
TS = 4
NS = NB * TS
NT = TP + NS
NX = NT + NB
ROWS = ((0, 128), (128, 128), (256, NS))
IN_W = 5656
IN_TILES = 44
GATE_OFF = IN_TILES * P
HEADS, GROUPS, HPG = 8, 2, 4
RKV_TILE = 20
RT = 8
NC = 1 + NB
EPS = 1e-6
NEG = -1.0e30
SCALE = 128.0 ** -0.5

(C_NORM1, C_NORM2, C_MUWAG, C_MURKV, C_W0, C_A0, C_KK, C_KA, C_RK, C_LNW, C_LNB, C_NORMF, C_BADA) = (
    0, 16, 32, 80, 104, 112, 120, 128, 136, 144, 152, 160, 176)
N_PAR = C_BADA + 96


class Step:
    pass


class Steps:

    def __init__(self, sem):
        self.sem, self.last = sem, None

    def chain(self, eng):
        self.last = Chain(eng, self.sem, self.last.base + self.last.n if self.last else 0)
        return self.last


class Chain:

    def __init__(self, eng, sem, base=0):
        self.eng, self.sem, self.base, self.n = eng, sem, base, 0

    def __call__(self, ins):
        ins.then_inc(self.sem, 1)
        self.n += 1
        self.eng.wait_ge(self.sem, self.base + self.n)

    def enter(self, i, per):
        assert self.n == 0
        self.start, self.per = self.base, per
        self.base = self.start + i * per

    def leave(self, count):
        assert self.n == self.per, self.n
        self.base, self.n = self.start + count * self.per, 0

    def settle(self):
        self.base, self.n = self.base + self.n, 0


def persistent(nc, ctx):
    k = Step()
    k.nc = nc
    k.sb = lambda name, shape, dt=F32, c=ctx: c.enter_context(nc.sbuf_tensor("sb_" + name, shape, dt))
    k.sem = lambda name: ctx.enter_context(nc.semaphore(name))
    k.bank = [ctx.enter_context(nc.psum_tensor(f"bank{i}", [P, 512], F32)) for i in range(8)]
    k.steps = Steps(k.sem("dve_step"))
    k.ident = k.sb("ident", [P, P])
    k.ones = k.sb("ones", [P, P])
    k.headones = k.sb("headones", [P, P])
    k.par = k.sb("par", [P, N_PAR])
    k.eps = k.sb("eps", [P, 4])
    k.mod = k.sb("mod", [P, 96, NC])
    k.xT = k.sb("xT", [P, KT, NT])
    k.mixT = k.sb("mixT", [P, KT, NT])
    k.peb = k.sb("pe_bias", [P, 2])
    return k


def phase_start(k, A):
    nc = k.nc
    CH = 512
    HK = KT // 2
    RING = 3
    PER = 6 * D // CH // NB
    PG = 4
    with ExitStack() as c:
        sb = lambda name, shape, dt=F32: k.sb(name, shape, dt, c)
        xf, mf = (v[:, :, :].rearrange("p a n -> p (a n)") for v in (k.xT, k.mixT))
        c_rows, c_act = xf[0:NC, 0:D], mf[0:NC, 0:D]
        stage = [xf[:, D + i * P:D + (i + 1) * P] for i in range(3)]
        stack = xf[:, D + 3 * P:D + 3 * P + 32]
        sil = mf[:, D:D + 4 * NCS].rearrange("p (i n) -> p i n", i=2)
        at = D + 4 * NCS
        cT = mf[:, at:at + KT * 32].rearrange("p (t m) -> p t m", t=KT)
        w = [sb(f"w_ada{i}", [P, HK, CH]) for i in range(RING)]
        mrows = sb("mod_rows", [P, CH])
        w1, w2 = sb("cmp_w1", [P, 2, CB, P]), sb("cmp_w2", [P, 2, P])
        pe_rows, peT = sb("pe_rows", [CB, 2, P]), sb("peT", [P, 2, CB])
        raw = [sb(f"cmp_raw{i}", [P, PG, ROW]) for i in range(N_PAGES // PG)]
        xt = sb("cmp_xT", [P, 4, PAST])
        table = sb("cmp_table", [1, NB * N_PAGES], I32)
        kcT, vc = sb("kcT_made", [P, NB, 2 * NCS]), sb("vc_made", [P, NB, KVW])
        s_const = k.sem("a_const")
        s_par = k.sem("a_par_rows")
        s_c = k.sem("a_c_rows")
        s_w = [k.sem(f"a_w_landed{i}") for i in range(RING)]
        s_silu = k.sem("a_silu")
        s_parT = k.sem("a_par_transposed")
        s_cT = k.sem("a_c_transposed")
        s_ready = k.sem("a_operands_ready")
        s_half = k.sem("a_half_multiplied")
        s_rows = k.sem("a_chunk_copied")
        s_tr = k.sem("a_chunk_transposed")
        s_mod = k.sem("a_chunk_done")
        s_wl, s_tab = k.sem("l_weights"), k.sem("l_table")
        s_raw = [k.sem(f"l_pages{i}") for i in range(len(raw))]
        s_t = k.sem("l_page_transposed")
        s_pc = [k.sem("l_even_page_copied"), k.sem("l_odd_page_copied")]
        s_pre, s_sil, s_out, s_kv = (k.sem(n) for n in ("l_pre", "l_silu", "l_multiplied", "l_done"))
        s_pe0, s_pe1 = k.sem("l_pe_stage"), k.sem("l_pe_copied")

        w_view = A["w_ada"][0].rearrange("(k p) n -> p k n", p=P)
        with nc.Block() as block:
            @block.sync
            def _(sp):
                sp.dma_start(c_rows[0:1, :], A["c_prompt"]).then_inc(s_c, 16)
                sp.dma_start(c_rows[1:NC, :], A["c_sample"]).then_inc(s_c, 16)
                sp.dma_start(table[:, :], A["page_table"].rearrange("b n -> (b n)").rearrange("(o n) -> o n", o=1))\
                    .then_inc(s_tab, 16)
                sp.wait_ge(s_tab, 16)

                def turn(b, first):
                    def ada(i):
                        n = b * 2 * PER + i
                        if not (first and i < RING):
                            sp.wait_ge(s_half, n - RING + 1)
                        hf = i % 2
                        col = (b * PER + i // 2) * CH
                        sp.dma_start(w[i % RING][:, :, :], w_view[:, hf * HK:(hf + 1) * HK, bass.ds(col, CH)])\
                            .then_inc(s_w[i % RING], 16)

                    def pages(r):
                        if not first:
                            sp.wait_ge(s_t, (b - 1) * N_PAGES + PG * (r + 1))
                        for j in range(PG):
                            page = sp.value_load(table[0:1, bass.ds(b * N_PAGES + r * PG + j, 1)], min_val=0,
                                                 max_val=A["cache_cmp_kv"].shape[1] - 1)
                            sp.dma_start(raw[r][:, j, :], A["cache_cmp_kv"][0, bass.ds(page, 1)]
                                         .rearrange("o s kv g d -> (o s) (kv g d)")).then_inc(s_raw[r], 16)
                    ada(0)
                    ada(1)
                    pages(0)
                    ada(2)
                    pages(1)
                    pages(2)
                    pages(3)
                    ada(3)
                    ada(4)
                    ada(5)
                turn(0, True)
                with sp.Fori(1, NB) as b:
                    turn(b, False)
                sp.wait_ge(s_kv, 2 * NB)
                sp.dma_start(k.kc_dram[:, :, :], kcT[:, :, :]).then_inc(s_tab, 16)
                sp.dma_start(k.vc_dram[:, :, :], vc[0:NCS, :, :]).then_inc(s_tab, 16)
                sp.wait_ge(s_tab, 48)

            def copies(eng, copy, parity, b, lo, hi):
                for pg in range(lo + parity, hi, 2):
                    eng.wait_ge(s_t, b * N_PAGES + pg + 1)
                    copy(xt[:, :, pg * PAGE:(pg + 1) * PAGE], k.bank[2 + parity][:, :].rearrange("p (j s) -> p j s", j=4))\
                        .then_inc(s_pc[parity], 1)

            @block.scalar
            def _(act):
                def rows(tile, at, n, src):
                    act.dma_start(tile[at:at + n, :], src).then_inc(s_par, 16)
                r1 = lambda v: v.rearrange("a (r p) -> (a r) p", p=P)
                rows(stage[0], C_NORM1, 16, r1(A["norm1"]))
                rows(stage[0], C_NORM2, 16, r1(A["norm2"]))
                rows(stage[0], C_MUWAG, 48, A["mu_wag"][0].rearrange("a (r p) -> (a r) p", p=P))
                rows(stage[0], C_MURKV, 24, r1(A["mu_rkv"]))
                for col, v in ((C_W0, A["decay_w0"]), (C_A0, A["iclr_a0"]), (C_KK, A["k_k"]), (C_KA, A["k_a"]),
                               (C_RK, A["r_k"].rearrange("a h d -> a (h d)")), (C_LNW, A["ln_x_w"]),
                               (C_LNB, A["ln_x_b"])):
                    rows(stage[1], col - C_W0, 8, r1(v))
                rows(stage[1], C_NORMF - C_W0, 16, A["norm_f"].rearrange("(r p) -> r p", p=P))
                rows(stage[2], 0, 96, r1(A["b_ada"]))
                for i, (a, b2, pe_) in enumerate(((A["cmp_k_w1"], A["cmp_k_w2"], A["cmp_k_pe"]),
                                                  (A["cmp_v_w1"], A["cmp_v_w2"], A["cmp_v_pe"]))):
                    act.dma_start(pe_rows[:, i, :], pe_[0]).then_inc(s_wl, 16)
                    act.dma_start(w1[:, i, :, :], a[0].rearrange("s d e -> d s e")).then_inc(s_wl, 16)
                    act.dma_start(w2[:, i, :], b2[0]).then_inc(s_wl, 16)
                act.wait_ge(s_c, 32)
                act.activation(c_act[:, :], c_rows[:, :], ACT.Silu).then_inc(s_silu, 1)
                act.wait_ge(s_pe1, 2)
                with act.Fori(0, NB) as b:
                    copies(act, act.copy, 0, b, 0, N_PAGES)
                    for i in range(2):
                        act.wait_ge(s_pre, 2 * b + 1 + i)
                        act.activation(sil[:, i, :], k.bank[4 + i][:, 0:2 * NCS], ACT.Silu, bias=k.peb[:, i:i + 1])\
                            .then_inc(s_sil, 1)

            @block.gpsimd
            def _(pool):
                pool.memset(k.ident[:, :], 0.0).then_inc(s_const, 1)
                pool.memset(k.ones[:, :], 1.0).then_inc(s_const, 1)
                pool.memset(k.headones[:, :], 1.0).then_inc(s_const, 1)
                pool.memset(k.eps[:, 0:1], EPS).then_inc(s_const, 1)
                pool.memset(k.eps[:, 1:2], 64e-5).then_inc(s_const, 1)
                pool.memset(k.eps[:, 2:4], 0.0).then_inc(s_const, 1)
                pool.memset(cT[:, :, :], 0.0).then_inc(s_const, 1)
                pool.wait_ge(s_const, 7)
                pool.affine_select(out=k.ident[:, :], in_=k.ident[:, :], compare_op=ALU.not_equal, fill=1.0,
                                   base=0, pattern=[[-1, P]], channel_multiplier=1).then_inc(s_const, 1)
                pool.affine_select(out=k.headones[:, 0:64], in_=k.headones[:, 0:64], compare_op=ALU.is_ge, fill=0.0,
                                   base=63, pattern=[[0, 64]], channel_multiplier=-1).then_inc(s_const, 1)
                pool.affine_select(out=k.headones[:, 64:128], in_=k.headones[:, 64:128], compare_op=ALU.is_ge,
                                   fill=0.0, base=-64, pattern=[[0, 64]], channel_multiplier=1).then_inc(s_const, 1)

            @block.tensor
            def _(pe):
                pe.wait_ge(s_const, 10)
                pe.wait_ge(s_par, 16 * 13)
                pe.transpose(k.bank[0][:, 0:104], stage[0][0:104, :], k.ident[0:104, 0:104])
                pe.transpose(k.bank[0][:, 104:176], stage[1][0:72, :], k.ident[0:72, 0:72])
                pe.transpose(k.bank[0][:, 176:272], stage[2][0:96, :], k.ident[0:96, 0:96]).then_inc(s_parT, 1)
                pe.wait_ge(s_silu, 1)
                for t in range(KT):
                    ins = pe.transpose(k.bank[1][:, t * NC:(t + 1) * NC], c_act[:, t * P:(t + 1) * P],
                                       k.ident[0:NC, 0:NC])
                ins.then_inc(s_cT, 1)
                pe.wait_ge(s_wl, 16 * 6)
                for i in range(2):
                    ins = pe.transpose(k.bank[6][:, i * CB:(i + 1) * CB], pe_rows[:, i, :], k.ident[0:CB, 0:CB])
                ins.then_inc(s_pe0, 1)
                pe.wait_ge(s_pe1, 1)
                for i in range(2):
                    for s in range(CB):
                        ins = pe.matmul(k.bank[7][:, i:i + 1], w1[:, i, s, :], peT[:, i, s:s + 1], start=(s == 0),
                                        stop=(s == CB - 1))
                ins.then_inc(s_pe0, 1)
                pe.wait_ge(s_ready, 3)
                pe.wait_ge(s_pe1, 2)

                def chunk(b, r):
                    for hf in range(2):
                        i = 2 * r + hf
                        pe.wait_ge(s_w[i % RING], (b * 2 + i // RING + 1) * 16)
                        for t in range(HK):
                            j = t % 4
                            ins = pe.matmul(k.bank[0][32 * j:32 * j + 32, :], cT[:, hf * HK + t, :], w[i % RING][:, t, :],
                                            start=(hf == 0 and t < 4), stop=(hf == 1 and t >= HK - 4))
                        ins.then_inc(s_half, 1)

                def turned(b, r):
                    pe.wait_ge(s_rows, b * PER + r + 1)
                    for j in range(4):
                        ins = pe.matmul(k.bank[1][:, 32 * j:32 * j + 32], mrows[:, j * P:(j + 1) * P], stack, start=True,
                                        stop=True)
                    ins.then_inc(s_tr, 1)

                def pages(b, lo, hi):
                    for pg in range(lo, hi):
                        if pg % PG == 0:
                            pe.wait_ge(s_raw[pg // PG], (b + 1) * 16 * PG)
                        if pg >= 2:
                            pe.wait_ge(s_pc[pg % 2], b * (N_PAGES // 2) + pg // 2)
                        for j in range(4):
                            ins = pe.transpose(k.bank[2 + pg % 2][:, j * P:(j + 1) * P],
                                               raw[pg // PG][:, pg % PG, j * P:(j + 1) * P], k.ident[:, :])
                        ins.then_inc(s_t, 1)

                def turn(b, first):
                    pages(b, 0, 3)
                    chunk(b, 0)
                    pages(b, 3, 8)
                    turned(b, 0)
                    chunk(b, 1)
                    pages(b, 8, 12)
                    turned(b, 1)
                    chunk(b, 2)
                    pages(b, 12, N_PAGES)
                    turned(b, 2)
                    for i in range(2):
                        pe.wait_ge(s_pc[i], (b + 1) * (N_PAGES // 2))
                    if not first:
                        pe.wait_ge(s_kv, 2 * b)
                    compress_project(k, pe, NCS, w1, w2, sil, lambda i, s: xt[:, 2 * i:2 * i + 2, s:s + CS * (NCS - 1) + 1:CS],
                                     s_pre, lambda: pe.wait_ge(s_sil, 2 * b + 2), s_out)
                turn(0, True)
                with pe.Fori(1, NB) as b:
                    turn(b, False)

            @block.vector
            def _(dve):
                dve.wait_ge(s_const, 10)
                dve.wait_ge(s_parT, 1)
                dve.tensor_copy(k.par[:, :], k.bank[0][:, 0:N_PAR]).then_inc(s_ready, 1)
                dve.wait_ge(s_cT, 1)
                dve.tensor_copy(cT[:, :, 0:NC], k.bank[1][:, 0:KT * NC].rearrange("p (t m) -> p t m", m=NC))\
                   .then_inc(s_ready, 1)
                dve.wait_ge(s_pe0, 1)
                dve.tensor_copy(peT[:, :, :], k.bank[6][:, 0:2 * CB].rearrange("p (i s) -> p i s", i=2)).then_inc(s_pe1, 1)
                dve.wait_ge(s_pe0, 2)
                dve.tensor_copy(k.peb[:, :], k.bank[7][:, 0:2]).then_inc(s_pe1, 1)
                dve.wait_ge(s_ready, 2)
                dve.tensor_reduce(stack, k.ident[:, :].rearrange("p (j m) -> p m j", j=4), AX.X, ALU.add).then_inc(s_ready, 1)

                def rows(b, r):
                    dve.wait_ge(s_half, (b * PER + r) * 2 + 2)
                    dve.tensor_copy(mrows[:, :], k.bank[0][:, :]).then_inc(s_rows, 1)

                def done(b, r):
                    n = b * PER + r
                    dve.wait_ge(s_tr, n + 1)
                    bada = k.par[:, bass.ds(C_BADA + 4 * n, 4)].unsqueeze(2).to_broadcast([P, 4, NC])
                    dve.tensor_tensor(k.mod[:, bass.ds(4 * n, 4), :],
                                      k.bank[1][:, 0:P].rearrange("p (j m) -> p j m", m=32)[:, :, 0:NC],
                                      bada, ALU.add).then_inc(s_mod, 1)

                with dve.Fori(0, NB) as b:
                    copies(dve, dve.tensor_copy, 1, b, 0, 2)
                    rows(b, 0)
                    copies(dve, dve.tensor_copy, 1, b, 2, 8)
                    done(b, 0)
                    rows(b, 1)
                    copies(dve, dve.tensor_copy, 1, b, 8, 12)
                    done(b, 1)
                    rows(b, 2)
                    copies(dve, dve.tensor_copy, 1, b, 12, N_PAGES)
                    done(b, 2)
                    dve.wait_ge(s_out, b + 1)
                    dve.tensor_scalar(kcT[:, bass.ds(b, 1), :].rearrange("p o n -> p (o n)"), k.bank[6][:, 0:2 * NCS], 1.0,
                                      None, ALU.mult).then_inc(s_kv, 1)
                    dve.tensor_scalar(vc[0:NCS, bass.ds(b, 1), :].rearrange("p o n -> p (o n)"),
                                      k.bank[7][0:NCS, 0:KVW], 1.0, None, ALU.mult).then_inc(s_kv, 1)


def compress_project(k, pe, n, w1, w2, sil, rhs, s_pre, silu_made, s_out):
    for i in range(2):
        for s in range(CB):
            ins = pe.matmul(k.bank[4 + i][:, 0:2 * n].rearrange("p (g c) -> p g c", g=2), w1[:, i, s, :],
                            rhs(i, s), start=(s == 0), stop=(s == CB - 1))
        ins.then_inc(s_pre, 1)
    silu_made()
    pe.matmul(k.bank[6][:, 0:2 * n], w2[:, 0, :], sil[:, 0, 0:2 * n], start=True, stop=True)
    for g in range(2):
        ins = pe.matmul(k.bank[7][0:n, g * P:(g + 1) * P], sil[:, 1, g * n:(g + 1) * n], w2[:, 1, :],
                        start=True, stop=True)
    ins.then_inc(s_out, 1)


def phase_norm1(k, A):
    nc = k.nc
    with ExitStack() as c:
        sb = lambda name, shape, dt=F32: k.sb(name, shape, dt, c)
        rows = [sb("x_rows0", [P, D]), sb("x_rows1", [P, D]), sb("x_rows2", [NS, D]), sb("s_rows", [NB, D])]
        s_x = [k.sem(f"b_rows_landed{i}") for i in range(4)]
        s_t = k.sem("b_tile_transposed")
        s_c = k.sem("b_tile_copied")
        with nc.Block() as block:
            @block.sync
            def _(sp):
                sp.dma_start(rows[0][:, :], A["x_prompt"][0, 0:128, :]).then_inc(s_x[0], 16)
                sp.dma_start(rows[1][:, :], A["x_prompt"][0, 128:256, :]).then_inc(s_x[1], 16)
                sp.dma_start(rows[2][:, :], A["x_sample"].rearrange("b t d -> (b t) d")).then_inc(s_x[2], 16)
                sp.dma_start(rows[3][:, :], A["state_shift"][0]).then_inc(s_x[3], 16)

            @block.tensor
            def _(pe):
                for i in range(4):
                    pe.wait_ge(s_x[i], 16)
                for t in range(KT):
                    if t >= 4:
                        pe.wait_ge(s_c, 2 * (t - 3))
                    for i, (at, n) in enumerate(ROWS + ((NT, NB),)):
                        ins = pe.transpose(k.bank[t % 4][:, at:at + n], rows[i][0:n, t * P:(t + 1) * P],
                                           k.ident[0:n, 0:n])
                    ins.then_inc(s_t, 1)

            @block.scalar
            def _(act):
                for t in range(KT):
                    act.wait_ge(s_t, t + 1)
                    act.copy(k.xT[:, t, :], k.bank[t % 4][:, 0:NT]).then_inc(s_c, 1)
                    act.copy(k.hT[:, t, NT:NX], k.bank[t % 4][:, NT:NX]).then_inc(s_c, 1)
    norm_block(k, "b1", k.xT, k.hT, C_NORM1, 0, 16)
    with ExitStack() as c:
        last = k.sb("last_cols", [P, KT, NC], F32, c)
        last_rows = k.sb("last_rows", [NC, D], F32, c)
        s_l, s_t, s_r, s_o = k.sem("b_last_cols"), k.sem("b_last_transposed"), k.sem("b_last_rows"), k.sem("b_last_out")
        with nc.Block() as block:
            @block.vector
            def _(dve):
                dve.tensor_copy(last[:, :, 0:1], k.hT[:, :, TP - 1:TP]).then_inc(s_l, 1)
                dve.tensor_copy(last[:, :, 1:NC], k.hT[:, :, TP + TS - 1:NT:TS]).then_inc(s_l, 1)
                for q in range(4):
                    dve.wait_ge(s_t, q + 1)
                    dve.tensor_copy(last_rows[:, q * 512:(q + 1) * 512], k.bank[q][0:NC, :]).then_inc(s_r, 1)

            @block.tensor
            def _(pe):
                pe.wait_ge(s_l, 2)
                for t in range(KT):
                    ins = pe.transpose(k.bank[t // 4][0:NC, (t % 4) * P:(t % 4 + 1) * P], last[:, t, :], k.ident[:, :])
                    if t % 4 == 3:
                        ins.then_inc(s_t, 1)

            @block.sync
            def _(sp):
                sp.wait_ge(s_r, 4)
                sp.dma_start(A["shift_prompt"][0], last_rows[0:1, :]).then_inc(s_o, 16)
                sp.dma_start(A["shift_sample"][0], last_rows[1:NC, :]).then_inc(s_o, 16)
                sp.wait_ge(s_o, 32)


def norm_block(k, pfx, src, dst, gain_col, shift, scale):
    nc = k.nc
    with ExitStack() as c:
        sb = lambda name, shape: k.sb(pfx + name, shape, F32, c)
        tmp, rstd, sd, g = sb("tmp", [P, KT, NT]), sb("rstd", [P, NT]), sb("sd", [P, NT]), sb("gain", [P, KT, NC])
        s_q, s_s = k.sem(pfx + "_squared"), k.sem(pfx + "_summed")
        s_sd = k.sem(pfx + "_root")
        with nc.Block() as block:
            @block.vector
            def _(dve):
                step = k.steps.chain(dve)
                for t in range(KT):
                    dve.tensor_tensor(tmp[:, t, :], src[:, t, :], src[:, t, :], ALU.mult).then_inc(s_q, 1)
                gain = k.par[:, gain_col:gain_col + KT].unsqueeze(2).to_broadcast([P, KT, NC])
                step(dve.scalar_tensor_tensor(out=g[:, :, :], in0=k.mod[:, scale:scale + KT, :], scalar=1.0, in1=gain,
                                              op0=ALU.add, op1=ALU.mult))
                dve.wait_ge(s_sd, 1)
                step(dve.reciprocal(rstd[:, :], sd[:, :]))
                step(dve.tensor_tensor(tmp[:, :, :], src[:, :, 0:NT], rstd[:, :].unsqueeze(1).to_broadcast([P, KT, NT]),
                                       ALU.mult))
                for t in range(KT):
                    dve.tensor_scalar(dst[:, t, 0:TP], tmp[:, t, 0:TP], g[:, t, 0:1], k.mod[:, shift + t, 0:1],
                                      ALU.mult, ALU.add)
                by_t = lambda v: v.unsqueeze(3).to_broadcast([P, KT, NB, TS])
                samples = lambda v: v[:, :, TP:NT].rearrange("p k (b t) -> p k b t", t=TS)
                step(dve.tensor_tensor(samples(tmp), samples(tmp), by_t(g[:, :, 1:NC]), ALU.mult))
                step(dve.tensor_tensor(samples(dst), samples(tmp), by_t(k.mod[:, shift:shift + KT, 1:NC]), ALU.add))

            @block.tensor
            def _(pe):
                for t in range(KT):
                    pe.wait_ge(s_q, t + 1)
                    ins = pe.matmul(k.bank[0][:, 0:NT], k.ones[:, :], tmp[:, t, :], start=(t == 0), stop=(t == KT - 1))
                ins.then_inc(s_s, 1)

            @block.scalar
            def _(act):
                act.wait_ge(s_s, 1)
                act.activation(sd[:, :], k.bank[0][:, 0:NT], ACT.Sqrt, bias=k.eps[:, 0:1], scale=1.0 / D)\
                   .then_inc(s_sd, 1)


def phase_in(k, A):
    nc = k.nc
    CH, N_CH, RING = 512, IN_TILES * P // 512, 2
    NG = 24
    with ExitStack() as c:
        sb = lambda name, shape, dt=F32: k.sb(name, shape, dt, c)
        w = [sb(f"w_in{i}", [P, KT, CH]) for i in range(RING)]
        wg = sb("w_in_gate", [P, KT, NG])
        s_w = [k.sem(f"c_w_landed{i}") for i in range(RING)]
        s_wg = k.sem("c_wg_landed")
        s_tile = k.sem("c_tile_multiplied")
        s_copy = [k.sem("c_even_copied"), k.sem("c_odd_copied")]
        s_g = k.sem("c_gates_multiplied")
        s_gc = k.sem("c_gates_done")
        w_view = A["w_in"][0].rearrange("(k p) n -> p k n", p=P)
        FULL = N_CH // RING

        with nc.Block() as block:
            @block.sync
            def _(sp):
                def load(r, n, used):
                    if used is not None:
                        sp.wait_ge(s_tile, used)
                    sp.dma_start(w[r][:, :, :], w_view[:, :, bass.ds(n * CH, CH)]).then_inc(s_w[r], 16)
                load(0, 0, None)
                load(1, 1, None)
                sp.dma_start(wg[:, :, :], w_view[:, :, GATE_OFF:IN_W]).then_inc(s_wg, 16)
                with sp.Fori(1, FULL) as it:
                    for r in range(RING):
                        load(r, it * RING + r, (it * RING + r - RING + 1) * 4)
                load(0, FULL * RING, (FULL * RING - RING + 1) * 4)

            @block.tensor
            def _(pe):
                def chunk(r, n, landed, first=False):
                    pe.wait_ge(s_w[r], landed)
                    for m in range(4):
                        if not first:
                            pe.wait_ge(s_copy[m % 2], 2 * n - 1 + m // 2)
                        for t in range(KT):
                            ins = pe.matmul(k.bank[m][:, 0:NX], w[r][:, t, m * P:(m + 1) * P], k.hT[:, t, :],
                                            start=(t == 0), stop=(t == KT - 1))
                        ins.then_inc(s_tile, 1)
                chunk(0, 0, 16, True)
                chunk(1, 1, 16)
                with pe.Fori(1, FULL) as it:
                    for r in range(RING):
                        chunk(r, it * RING + r, (it + 1) * 16)
                chunk(0, FULL * RING, (FULL + 1) * 16)
                pe.wait_ge(s_wg, 16)
                for i, (at, n) in enumerate(ROWS):
                    for t in range(KT):
                        ins = pe.matmul(k.bank[4 + i][0:n, 0:NG], k.hT[:, t, at:at + n], wg[:, t, :],
                                        start=(t == 0), stop=(t == KT - 1))
                    ins.then_inc(s_g, 1)

            def copies(eng, copy, parity):
                def chunk(n, dst, first):
                    for h in range(2):
                        m = 2 * h + parity
                        eng.wait_ge(s_tile, 4 * n + m + 1)
                        copy(dst[:, bass.ds(4 * n + m - first, 1), :].rearrange("p a n -> p (a n)"), k.bank[m][:, 0:NX])\
                            .then_inc(s_copy[parity], 1)
                with eng.Fori(0, RKV_TILE // 4) as n:
                    chunk(n, k.pT, 0)
                with eng.Fori(RKV_TILE // 4, N_CH) as n:
                    chunk(n, k.rkvT, RKV_TILE)

            @block.scalar
            def _(act):
                copies(act, act.copy, 0)
                for i, (at, n) in enumerate(ROWS):
                    act.wait_ge(s_g, i + 1)
                    act.activation(k.gates[0:n, i, :], k.bank[4 + i][0:n, 0:NG], ACT.Sigmoid).then_inc(s_gc, 1)

            @block.vector
            def _(dve):
                copies(dve, lambda out, in_: dve.tensor_scalar(out, in_, 1.0, None, ALU.mult), 1)


HT = 16
CL = 32
N_CHUNK = TP // CL
LW, LA, LG = 64, 64, 128


def shift_differences(dve, step, out, cur, tiles):
    samples = lambda v: v[:, :, TP:NT].rearrange("p k (b t) -> p k b t", t=TS)
    dve.tensor_tensor(out[:, :, 1:TP], cur[:, tiles, 0:TP - 1], cur[:, tiles, 1:TP], ALU.subtract)
    dve.tensor_scalar(out[:, :, 0:1], cur[:, tiles, 0:1], -1.0, None, ALU.mult)
    c = cur[:, tiles, :]
    dve.tensor_tensor(samples(out)[:, :, :, 1:TS], samples(c)[:, :, :, 0:TS - 1], samples(c)[:, :, :, 1:TS], ALU.subtract)
    step(dve.tensor_tensor(out[:, :, TP:NT:TS], c[:, :, NT:NX], c[:, :, TP:NT:TS], ALU.subtract))


def phase_lora(k, A):
    nc = k.nc
    with ExitStack() as c:
        sb = lambda name, shape, dt=F32: k.sb(name, shape, dt, c)
        w1 = [sb("lora_w1", [P, KT, LW]), sb("lora_a1", [P, KT, LA]), sb("lora_g1", [P, KT, LG])]
        w2 = [sb("lora_w2", [LW, RT * P]), sb("lora_a2", [LA, RT * P]), sb("lora_g2", [LG, RT * P])]
        dx = sb("dx", [P, KT, NT])
        XR = 8
        xm = sb("xm", [P, XR, NT])
        low = [sb("low_w", [LW, NT]), sb("low_a", [LA, NT]), sb("low_g", [LG, NT])]
        s_w, s_v, s_x = k.sem("f_lora_weights"), k.sem("f_lora_dve"), k.sem("f_mixed_input")
        s_used, s_act, s_hi, s_out = k.sem("f_tile_used"), k.sem("f_low_activated"), k.sem("f_high"), k.sem("f_high_done")
        dst = [k.dec, k.a, k.g]
        with nc.Block() as block:
            @block.sync
            def _(sp):
                for w, src in ((w1, (A["decay_w1"], A["iclr_a1"], A["gate_g1"])),):
                    for tile, s in zip(w, src):
                        sp.dma_start(tile[:, :, :], s[0].rearrange("(k p) n -> p k n", p=P)).then_inc(s_w, 16)
                for tile, s in zip(w2, (A["decay_w2"], A["iclr_a2"], A["gate_g2"])):
                    sp.dma_start(tile[:, :], s[0]).then_inc(s_w, 16)

            @block.vector
            def _(dve):
                step = Chain(dve, s_v)
                shift_differences(dve, step, dx, k.hT, slice(0, KT))
                for i in range(3):
                    for t in range(KT):
                        m = i * KT + t
                        if m >= XR:
                            dve.wait_ge(s_used, m - XR + 1)
                        mu = k.par[:, C_MUWAG + i * KT + t:C_MUWAG + i * KT + t + 1]
                        dve.scalar_tensor_tensor(out=xm[:, m % XR, :], in0=dx[:, t, :], scalar=mu, in1=k.hT[:, t, 0:NT],
                                                 op0=ALU.mult, op1=ALU.add).then_inc(s_x, 1)

            @block.tensor
            def _(pe):
                pe.wait_ge(s_w, 16 * 6)
                for i in range(3):
                    n = (LW, LA, LG)[i]
                    for t in range(KT):
                        pe.wait_ge(s_x, i * KT + t + 1)
                        ins = pe.matmul(k.bank[i][0:n, 0:NT], w1[i][:, t, :], xm[:, t % XR, :], start=(t == 0),
                                        stop=(t == KT - 1))
                        ins.then_inc(s_used, 1)
                for i in range(3):
                    pe.wait_ge(s_act, i + 1)
                    for t in range(RT):
                        m = i * RT + t
                        if m >= 4:
                            pe.wait_ge(s_out, m - 3)
                        pe.matmul(k.bank[4 + m % 4][:, 0:NT], w2[i][:, t * P:(t + 1) * P], low[i][:, :], start=True,
                                  stop=True).then_inc(s_hi, 1)

            @block.scalar
            def _(act):
                for i, fn in enumerate((ACT.Tanh, ACT.Copy, ACT.Sigmoid)):
                    n = (LW, LA, LG)[i]
                    act.wait_ge(s_used, (i + 1) * KT)
                    act.activation(low[i][:, :], k.bank[i][0:n, 0:NT], fn).then_inc(s_act, 1)
                for m in range(3 * RT):
                    i, t = m // RT, m % RT
                    act.wait_ge(s_hi, m + 1)
                    ps = k.bank[4 + m % 4][:, 0:NT]
                    if i == 2:
                        act.copy(dst[i][:, t, :], ps).then_inc(s_out, 1)
                    else:
                        col = (C_W0, C_A0)[i] + t
                        act.activation(dst[i][:, t, :], ps, ACT.Sigmoid, bias=k.par[:, col:col + 1]).then_inc(s_out, 1)
                act.wait_ge(s_out, 3 * RT)
                act.activation(k.dec[:, :, :], k.dec[:, :, :], ACT.Exp, scale=-0.6065306597126334).then_inc(s_out, 1)


def phase_rkv(k, A):
    nc = k.nc
    r, kx, v = (slice(i * RT, (i + 1) * RT) for i in range(3))
    with ExitStack() as c:
        sb = lambda name, shape, dt=F32: k.sb(name, shape, dt, c)
        d = sb("rkv_diff", [P, 3 * RT, NT])
        t1 = d[:, 0:RT, :]
        t2 = d[:, RT:2 * RT, :]
        one = sb("one_minus_ka", [P, RT])
        s_v, s_q, s_n, s_r = k.sem("g_dve"), k.sem("g_squares"), k.sem("g_head_sums"), k.sem("g_roots")
        with nc.Block() as block:
            @block.vector
            def _(dve):
                step = Chain(dve, s_v)
                shift_differences(dve, step, d, k.rkvT, slice(0, 3 * RT))
                for t in range(3 * RT):
                    mu = k.par[:, C_MURKV + t:C_MURKV + t + 1]
                    cur = k.rkvT[:, t, 0:NT]
                    ins = dve.scalar_tensor_tensor(out=cur, in0=d[:, t, :], scalar=mu, in1=cur, op0=ALU.mult,
                                                   op1=ALU.add)
                step(ins)
                bc = lambda col: k.par[:, col:col + RT].unsqueeze(2).to_broadcast([P, RT, NT])
                R, K, V = (k.rkvT[:, s, 0:NT] for s in (r, kx, v))
                step(dve.tensor_tensor(k.kk[:, :, :], K, bc(C_KK), ALU.mult))
                dve.tensor_tensor(t1, k.kk[:, :, :], k.kk[:, :, :], ALU.mult).then_inc(s_q, 1)
                step(dve.tensor_scalar(one[:, :], k.par[:, C_KA:C_KA + RT], -1.0, 1.0, ALU.mult, ALU.add))
                step(dve.tensor_tensor(t2, k.a[:, :, :], bc(C_KA), ALU.mult))
                step(dve.tensor_tensor(t2, t2, one[:, :].unsqueeze(2).to_broadcast([P, RT, NT]), ALU.add))
                step(dve.tensor_tensor(K, K, t2, ALU.mult))
                for t in range(RT):
                    dve.wait_ge(s_n, t + 1)
                    step(dve.tensor_scalar(t2[:, t, :], k.bank[t % 4][:, 0:NT], 1e-24, None, ALU.max))
                step(dve.tensor_tensor(k.bonus[:, :, :], R, K, ALU.mult))
                dve.tensor_tensor(k.bonus[:, :, :], k.bonus[:, :, :], bc(C_RK), ALU.mult).then_inc(s_q, 1)
                dve.wait_ge(s_r, 1)
                step(dve.reciprocal(t1, t2))
                step(dve.tensor_tensor(k.kk[:, :, :], k.kk[:, :, :], t1, ALU.mult))
                step(dve.tensor_tensor(k.a[:, :, :], k.a[:, :, :], k.kk[:, :, :], ALU.mult))
                for t in range(RT):
                    dve.wait_ge(s_n, RT + t + 1)
                    step(dve.tensor_tensor(k.bonus[:, t, :], k.bank[4 + t % 4][:, 0:NT], V[:, t, :], ALU.mult))

            @block.tensor
            def _(pe):
                BEFORE = 7
                pe.wait_ge(s_q, 1)
                for t in range(RT):
                    if t >= 4:
                        pe.wait_ge(s_v, BEFORE + t - 3)
                    pe.matmul(k.bank[t % 4][:, 0:NT], k.headones[:, :], t1[:, t, :], start=True, stop=True)\
                        .then_inc(s_n, 1)
                pe.wait_ge(s_q, 2)
                for t in range(RT):
                    if t >= 4:
                        pe.wait_ge(s_v, BEFORE + RT + 1 + 3 + t - 3)
                    pe.matmul(k.bank[4 + t % 4][:, 0:NT], k.headones[:, :], k.bonus[:, t, :], start=True, stop=True)\
                        .then_inc(s_n, 1)

            @block.scalar
            def _(act):
                act.wait_ge(s_v, 7 + RT)
                act.activation(t2, t2, ACT.Sqrt).then_inc(s_r, 1)


def phase_scan(k, A):
    nc = k.nc
    with ExitStack() as c:
        sb = lambda name, shape, dt=F32: k.sb(name, shape, dt, c)
        Q = HT // 4
        masks = []
        for name in ("prompt", "sample"):
            m = Step()
            m.up, m.low, m.incl4 = (sb(f"m_{what}_{name}", [P, 4, CL]) for what in ("up", "low", "incl4"))
            m.incl = sb("m_incl_" + name, [P, CL])
            masks.append(m)
        rowb4 = sb("m_row4", [P, 4, NB])
        rowb = sb("m_row", [P, NB])
        colb = sb("m_col", [P, NB, CL])
        d0, d1, pc = sb("decay_in", [P, RT, CL]), sb("decay_first", [P, RT, CL]), sb("decay_prod", [P, RT, CL])
        pinv, pprev = sb("decay_inv", [P, RT, CL]), sb("decay_prev", [P, RT, CL])
        ar, bh, kh, vc = (sb("ahat_rhat", [P, 2, RT, CL]), sb("bhat", [P, RT, CL]), sb("khat", [P, RT, CL]),
                          sb("v_chunk", [P, RT, CL]))
        lt, mk, pt_ = sb("LT", [P, Q, P]), sb("MK", [P, Q, P]), sb("invT", [P, Q, P])
        a_ = [sb("pow0", [P, Q, P]), sb("pow1", [P, Q, P])]
        at = [lt, sb("powT1", [P, Q, P])]
        rbk = sb("RBK", [P, Q, 2, CL])
        rows = sb("bkv_rows", [P, 3, Q, 64])
        x, sa = sb("X", [P, Q, 64]), sb("SA", [P, Q, 64])
        st = sb("state", [P, RT, 64])
        s0 = sb("sample_state", [P, RT, NB, 64])
        ahm = sb("ahat_by_sample", [P, RT, NB, CL])
        flat = lambda tile: k.rkvT[:, tile:tile + 7, :].rearrange("p a n -> p (a n)")[:, 0:Q * NB * 64]\
            .rearrange("p (q b i) -> p q b i", q=Q, b=NB)
        sam, vm = flat(0), flat(RT)
        s_m, s_st = k.sem("h_masks"), k.sem("h_states_landed")
        s_pe, s_v, s_o = k.sem("h_pe_stage"), k.sem("h_dve_stage"), k.sem("h_states_written")
        VST, PST = 12, 9
        bank = k.bank

        def head(h):
            pb, rb = 64 * (h % 2), 64 * (h % 2) + 32 * (h // 2 % 2)
            return h // 2, slice(pb, pb + 64), h // 4, slice(rb, rb + 32)

        def pe_chunk(pe, v, sample):
            pe.wait_ge(s_st, 16 * NB)
            v(1)
            g = bank[0][:, :].rearrange("p (q m a t) -> p q m a t", q=Q, m=2, a=2)
            for h in range(HT):
                t, pb, q, rb = head(h)
                pe.matmul(bank[1][rb, P + q * 64:P + (q + 1) * 64], vc[:, t, :], k.ident[:, pb], start=True, stop=True)
            for h in range(HT):
                t, pb, q, rb = head(h)
                pe.matmul(g[rb, q, 0, :, :], bh[pb, t, :], ar[pb, :, t, :], start=True, stop=True)
                pe.matmul(g[rb, q, 1, :, :], kh[pb, t, :], ar[pb, :, t, :], start=True, stop=True)
                pe.matmul(bank[1][rb, q * CL:(q + 1) * CL], ar[pb, 0, t, :], bh[pb, t, :], start=True, stop=True)
            for h in range(HT):
                t, pb, q, rb = head(h)
                for i, src in enumerate((bh, kh)):
                    ins = pe.matmul(bank[2][rb, i * 256 + q * 64:i * 256 + (q + 1) * 64], src[pb, t, :], k.ident[pb, pb],
                                    start=True, stop=True)
            ins.then_inc(s_pe, 1)
            v(3)
            for q in range(Q):
                pe.matmul(bank[6][:, q * 64:(q + 1) * 64], mk[:, q, :], rows[:, 2, q, :], start=True, stop=False)
                for h in range(4 * q, 4 * q + 4):
                    t, pb, _, rb = head(h)
                    out = bank[6][rb, q * 64:(q + 1) * 64]
                    if sample:
                        for b in range(NB):
                            ins = pe.matmul(out, ahm[pb, t, b, :], s0[pb, t, b, :], start=False,
                                            stop=(b == NB - 1))
                    else:
                        ins = pe.matmul(out, ar[pb, 0, t, :], st[pb, t, :], start=False, stop=True)
            ins.then_inc(s_pe, 1)
            for level in range(5):
                if level > 0:
                    v(4 + level)
                src, dst = (level + 1) % 2, level % 2
                for q in range(Q):
                    cols = slice(q * P, (q + 1) * P)
                    if level < 4:
                        ins = pe.matmul(bank[3][:, cols], at[dst][:, q, :], a_[dst][:, q, :], start=True, stop=True)
                        if level < 3:
                            ins = pe.matmul(bank[4][:, cols], a_[dst][:, q, :], at[dst][:, q, :], start=True, stop=True)
                    if level > 0:
                        ins = pe.matmul(bank[5][:, cols], a_[dst][:, q, :], pt_[:, q, :], start=True, stop=True)
                ins.then_inc(s_pe, 1)
            v(9)
            for q in range(Q):
                ins = pe.matmul(bank[6][:, 256 + q * 64:256 + (q + 1) * 64], pt_[:, q, :], x[:, q, :], start=True,
                                stop=True)
            ins.then_inc(s_pe, 1)
            v(10)
            for h in range(HT):
                t, pb, q, rb = head(h)
                y_bank, at_ = bank[3 + t % 2], t // 2 * CL
                out = y_bank[pb, at_:at_ + CL]
                pe.matmul(out, sa[rb, q, :], rbk[rb, q, 0, :], start=True, stop=False)
                pe.matmul(out, rows[rb, 2, q, :], rbk[rb, q, 1, :], start=False, stop=sample)
                if sample:
                    for b in range(NB):
                        ins = pe.matmul(y_bank[pb, at_ + b * TS:at_ + (b + 1) * TS], s0[pb, t, b, :],
                                        ar[pb, 1, t, b * TS:(b + 1) * TS], start=False, stop=True,
                                        skip_group_check=True)
                else:
                    ins = pe.matmul(out, st[pb, t, :], ar[pb, 1, t, :], start=False, stop=True)
            if not sample:
                for h in range(HT):
                    t, pb, q, rb = head(h)
                    out = bank[(7, 5)[t % 2]][pb, t // 2 * 64:(t // 2 + 1) * 64]
                    pe.matmul(out, rows[rb, 0, q, :], sa[rb, q, :], start=True, stop=False)
                    ins = pe.matmul(out, rows[rb, 1, q, :], rows[rb, 2, q, :], start=False, stop=True)
            ins.then_inc(s_pe, 1)

        def dve_chunk(dve, step, p, cols, mask, first_step, sample):
            R, K, V = (k.rkvT[:, i * RT:(i + 1) * RT, cols] for i in range(3))
            seg = slice(0, CL, first_step)
            inner = Chain(dve, s_in, step.base_in)
            inner(dve.tensor_scalar(d0[:, :, :], k.dec[:, :, cols], 1.0, None, ALU.mult))
            dve.tensor_scalar(d1[:, :, seg], k.dec[:, :, cols][:, :, seg], 1.0, None, ALU.mult)
            inner(dve.memset(d0[:, :, seg], 0.0))
            fl = lambda v: v[:, :, :].rearrange("p k t -> p (k t)")
            inner(dve.tensor_tensor_scan(fl(pc), fl(d0), fl(d1), 0.0, ALU.mult, ALU.add))
            inner(dve.tensor_copy(fl(pprev)[:, 1:RT * CL], fl(pc)[:, 0:RT * CL - 1]))
            inner(dve.memset(pprev[:, :, seg], 1.0))
            inner(dve.reciprocal(pinv[:, :, :], pc[:, :, :]))
            ins = dve.scalar_tensor_tensor(out=ar[:, 0, :, :], in0=k.kk[:, :, cols], scalar=-1.0, in1=pprev[:, :, :],
                                           op0=ALU.mult, op1=ALU.mult)
            if sample:
                inner(ins)
                for t in range(RT):
                    dve.tensor_tensor(ahm[:, t, :, :], ar[:, 0, t, :].unsqueeze(1).to_broadcast([P, NB, CL]),
                                      colb[:, :, :], ALU.mult)
            dve.tensor_tensor(ar[:, 1, :, :], R, pc[:, :, :], ALU.mult)
            dve.tensor_tensor(bh[:, :, :], k.a[:, :, cols], pinv[:, :, :], ALU.mult)
            dve.tensor_tensor(kh[:, :, :], K, pinv[:, :, :], ALU.mult)
            step(dve.tensor_scalar(vc[:, :, :], V, 1.0, None, ALU.mult))
            p(1)
            g = bank[0][:, :].rearrange("p (q m a t) -> p q m a t", q=Q, m=2, a=2)
            spread = lambda v: v.unsqueeze(2).to_broadcast([P, Q, 4, CL])
            over_q = lambda m: m[:, :, :].unsqueeze(1).to_broadcast([P, Q, 4, CL])
            out4 = lambda v: v[:, :, :].rearrange("p q (h t) -> p q h t", t=CL)
            dve.tensor_tensor(out4(a_[0]), spread(bank[1][:, 0:P].rearrange("p (q t) -> p q t", q=Q)), over_q(mask.low),
                              ALU.mult)
            step(dve.tensor_tensor(out4(lt), spread(g[:, :, 0, 0, :]), over_q(mask.up), ALU.mult))
            dve.tensor_tensor(out4(mk), spread(g[:, :, 1, 0, :]), over_q(mask.up), ALU.mult)
            dve.tensor_tensor(pt_[:, :, :], lt[:, :, :], k.ident[:, :].unsqueeze(1).to_broadcast([P, Q, P]), ALU.add)
            for i in range(2):
                dve.tensor_tensor(rbk[:, :, i, :], g[:, :, i, 1, :], mask.incl[:, :].unsqueeze(1).to_broadcast([P, Q, CL]),
                                  ALU.mult)
            fr = rows[:, :, :, :].rearrange("p m q i -> p (m q i)")
            dve.tensor_copy(fr[:, 0:512], bank[2][:, :])
            step(dve.tensor_copy(fr[:, 512:768], bank[1][:, P:P + 256]))
            p(2)
            step(dve.tensor_copy(x[:, :, :].rearrange("p q i -> p (q i)"), bank[6][:, 0:256]))
            full = lambda v: v[:, :, :].rearrange("p q i -> p (q i)")
            for level in range(5):
                p(3 + level)
                dst = (level + 1) % 2
                if level > 0:
                    ins = dve.tensor_tensor(full(pt_), full(pt_), bank[5][:, :], ALU.add)
                if level < 4:
                    if level < 3:
                        dve.tensor_copy(full(at[dst]), bank[4][:, :])
                    ins = dve.tensor_copy(full(a_[dst]), bank[3][:, :])
                step(ins)
            p(8)
            step(dve.tensor_copy(full(sa), bank[6][:, 256:512]))
            p(9)
            for i in range(2):
                ins = dve.tensor_scalar(k.y[:, i:RT:2, cols], bank[3 + i][:, 0:RT // 2 * CL].rearrange("p (k t) -> p k t", t=CL),
                                        1.0, None, ALU.mult)
            step(ins)
            if not sample:
                for i in range(2):
                    ins = dve.tensor_tensor(st[:, i:RT:2, :], st[:, i:RT:2, :],
                                            bank[(7, 5)[i]][:, 0:RT // 2 * 64].rearrange("p (k i) -> p k i", i=64), ALU.add)
                inner(ins)
                step(dve.tensor_tensor(st[:, :, :], st[:, :, :], pc[:, :, CL - 1:CL].to_broadcast([P, RT, 64]),
                                       ALU.mult))
            assert inner.n == 7

        s_in = k.sem("h_dve_inner")
        s_sp, s_sv = k.sem("h_state_pe"), k.sem("h_state_dve")
        raw = sb("state_rows", [P, RT * P])
        x_rows = sb("prompt_state_rows", [64, RT * P])
        with nc.Block() as block:
            @block.gpsimd
            def _(pool):
                n = [0]

                def select(m, in_, op, base, pattern, cm):
                    pool.affine_select(out=m, in_=in_, compare_op=op, fill=0.0, base=base, pattern=pattern,
                                       channel_multiplier=cm).then_inc(s_m, 1)
                    n[0] += 1
                    pool.wait_ge(s_m, n[0])
                for i, m in enumerate(masks):
                    w = CL if i == 0 else TS
                    blk = [P // w, w]
                    for tile, op, s in ((m.up, ALU.is_gt, 1), (m.low, ALU.is_gt, -1), (m.incl4, ALU.is_ge, 1)):
                        t = tile[:, :, :].rearrange("p a t -> p (a t)")
                        one = k.ones[:, :]
                        select(t, one, op, 0, [[s, P]], -s)
                        tb = t.rearrange("p (a t) -> p a t", t=w)
                        if s == 1:
                            select(tb, tb, ALU.is_ge, 0, [[-w, blk[0]], [0, w]], 1)
                        else:
                            select(tb, tb, ALU.is_ge, w - 1, [[w, blk[0]], [0, w]], -1)
                r4 = rowb4[:, :, :].rearrange("p a b -> p (a b)")
                select(r4, k.ones[:, 0:32], ALU.is_ge, 0, [[-TS, 32]], 1)
                select(r4, r4, ALU.is_ge, TS - 1, [[TS, 32]], -1)
                select(colb[:, :, :], k.ones[:, 0:CL].unsqueeze(1).to_broadcast([P, NB, CL]), ALU.is_ge, 0, [[-TS, NB], [1, CL]], 0)
                select(colb[:, :, :], colb[:, :, :], ALU.is_ge, TS - 1, [[TS, NB], [-1, CL]], 0)

            @block.sync
            def _(sp):
                for pair in range(NB // 2):
                    if pair > 0:
                        sp.wait_ge(s_sp, pair)
                    for b in range(2):
                        sp.dma_start(raw[64 * b:64 * b + 64, :].rearrange("i (h j) -> i h j", j=64),
                                     A["state_wkv"][0, 2 * pair + b].rearrange("h i j -> i h j")).then_inc(s_st, 16)

            @block.tensor
            def _(pe):
                for pair in range(NB // 2):
                    pe.wait_ge(s_st, 32 * (pair + 1))
                    if pair > 0:
                        pe.wait_ge(s_sv, 2 * pair)
                    for t in range(RT):
                        ins = pe.transpose(bank[t // 4][:, (t % 4) * P:(t % 4 + 1) * P], raw[:, t * P:(t + 1) * P],
                                           k.ident[:, :])
                    ins.then_inc(s_sp, 1)

            @block.vector
            def _(dve):
                dve.wait_ge(s_m, 16)
                for m in masks:
                    dve.tensor_reduce(m.incl[:, :], m.incl4[:, :, :].rearrange("p a t -> p t a"), AX.X, ALU.add)
                dve.tensor_reduce(rowb[:, :], rowb4[:, :, :].rearrange("p a b -> p b a"), AX.X, ALU.add)
                dve.memset(st[:, :, :], 0.0)
                dve.memset(d1[:, :, :], 0.0)
                for pair in range(NB // 2):
                    dve.wait_ge(s_sp, pair + 1)
                    for i in range(2):
                        dve.tensor_copy(s0[:, 4 * i:4 * i + 4, 2 * pair:2 * pair + 2, :].rearrange("p t b i -> p t (b i)"),
                                        bank[i][:, :].rearrange("p (t n) -> p t n", t=4)).then_inc(s_sv, 1)
        with nc.Block() as block:
            @block.tensor
            def _(pe):
                with pe.Fori(0, N_CHUNK) as n:
                    pe_chunk(pe, lambda i: pe.wait_ge(s_v, n * VST + i), False)
                pe_chunk(pe, lambda i: pe.wait_ge(s_v, N_CHUNK * VST + i), True)
                pe.wait_ge(s_v, N_CHUNK * VST + VST)
                for t in range(RT):
                    if t >= 2:
                        pe.wait_ge(s_sv, NB + t - 1)
                    for h in (2 * t, 2 * t + 1):
                        _, pb, q, rb = head(h)
                        fold = lambda v: v[rb, q, :, :].rearrange("p b i -> p (b i)")
                        pe.matmul(bank[t % 2][pb, :], rows[rb, 0, q, :], fold(sam), start=True, stop=False)
                        ins = pe.matmul(bank[t % 2][pb, :], rows[rb, 1, q, :], fold(vm), start=False, stop=True)
                    ins.then_inc(s_sp, 1)
                for t in range(RT):
                    ins = pe.transpose(bank[2 + t // 4][0:64, (t % 4) * P:(t % 4 + 1) * P], st[:, t, :], k.ident[:, :])
                ins.then_inc(s_sp, 1)
                pe.wait_ge(s_sv, NB + RT)
                for pair in range(NB // 2):
                    if pair > 0:
                        pe.wait_ge(s_sv, NB + RT + 2 + 2 * pair)
                    for t in range(RT):
                        ins = pe.transpose(bank[4 + t // 4][:, (t % 4) * P:(t % 4 + 1) * P],
                                           s0[:, t, 2 * pair:2 * pair + 2, :].rearrange("p b i -> p (b i)"), k.ident[:, :])
                    ins.then_inc(s_sp, 1)

            @block.vector
            def _(dve):
                step = Chain(dve, s_v)
                with dve.Fori(0, N_CHUNK) as n:
                    step.enter(n, VST)
                    step.base_in = n * 7
                    dve_chunk(dve, step, lambda i: dve.wait_ge(s_pe, n * PST + i), bass.ds(n * CL, CL), masks[0], CL, False)
                step.leave(N_CHUNK)
                step.base_in = N_CHUNK * 7
                base = N_CHUNK * PST

                def p(i):
                    dve.wait_ge(s_pe, base + i)
                dve_chunk(dve, step, p, slice(TP, NT), masks[1], TS, True)
                for src, dst in ((sa, sam), (rows[:, 2, :, :], vm)):
                    for q in range(Q):
                        ins = dve.tensor_tensor(dst[:, q, :, :], src[:, q, :].unsqueeze(1).to_broadcast([P, NB, 64]),
                                                rowb[:, :].unsqueeze(2).to_broadcast([P, NB, 64]), ALU.mult)
                step(ins)
                for t in range(RT):
                    dve.wait_ge(s_sp, NB // 2 + t + 1)
                    s0t = s0[:, t, :, :].rearrange("p b i -> p (b i)")
                    step(dve.tensor_tensor(s0t, s0t, bank[t % 2][:, :], ALU.add))
                    dve.tensor_tensor(s0[:, t, :, :], s0[:, t, :, :], pc[:, t, TS - 1:CL:TS].unsqueeze(2)
                                      .to_broadcast([P, NB, 64]), ALU.mult).then_inc(s_sv, 1)
                dve.wait_ge(s_sp, NB // 2 + RT + 1)
                for i in range(2):
                    dve.tensor_copy(x_rows[0:64, i * 512:(i + 1) * 512], bank[2 + i][0:64, :]).then_inc(s_sv, 1)
                for pair in range(NB // 2):
                    dve.wait_ge(s_sp, NB // 2 + RT + 2 + pair)
                    if pair > 0:
                        dve.wait_ge(s_o, 16 + 32 * pair)
                    for i in range(2):
                        dve.tensor_copy(raw[:, i * 512:(i + 1) * 512], bank[4 + i][:, :]).then_inc(s_sv, 1)

            @block.sync
            def _(sp):
                sp.wait_ge(s_sv, NB + RT + 2)
                sp.dma_start(A["wkv_prompt"][0, 0].rearrange("h i j -> i h j"),
                             x_rows[0:64, :].rearrange("i (h j) -> i h j", j=64)).then_inc(s_o, 16)
                for pair in range(NB // 2):
                    sp.wait_ge(s_sv, NB + RT + 4 + 2 * pair)
                    for b in range(2):
                        sp.dma_start(A["wkv_sample"][0, 2 * pair + b].rearrange("h i j -> i h j"),
                                     raw[64 * b:64 * b + 64, :].rearrange("i (h j) -> i h j", j=64)).then_inc(s_o, 16)
                sp.wait_ge(s_o, 16 + 32 * (NB // 2))


def phase_groupnorm(k, A):
    nc = k.nc
    with ExitStack() as c:
        sb = lambda name, shape, dt=F32: k.sb(name, shape, dt, c)
        sq, sd = sb("gn_square", [P, RT, NT]), sb("gn_root", [P, RT, NT])
        s_m, s_c, s_q, s_n, s_r, s_v = (k.sem(n) for n in ("i_means", "i_centred", "i_squared", "i_variances",
                                                            "i_roots", "i_dve"))
        with nc.Block() as block:
            @block.tensor
            def _(pe):
                for t in range(RT):
                    if t >= 4:
                        pe.wait_ge(s_c, t - 3)
                    pe.matmul(k.bank[t % 4][:, 0:NT], k.headones[:, :], k.y[:, t, :], start=True, stop=True)\
                        .then_inc(s_m, 1)
                for t in range(RT):
                    pe.wait_ge(s_q, t + 1)
                    if t >= 4:
                        pe.wait_ge(s_r, t - 3)
                    pe.matmul(k.bank[4 + t % 4][:, 0:NT], k.headones[:, :], sq[:, t, :], start=True, stop=True)\
                        .then_inc(s_n, 1)

            @block.scalar
            def _(act):
                for t in range(RT):
                    act.wait_ge(s_n, t + 1)
                    act.activation(sd[:, t, :], k.bank[4 + t % 4][:, 0:NT], ACT.Sqrt, bias=k.eps[:, 1:2],
                                   scale=1.0 / 64).then_inc(s_r, 1)

            @block.vector
            def _(dve):
                step = Chain(dve, s_v)
                for t in range(RT):
                    dve.wait_ge(s_m, t + 1)
                    dve.scalar_tensor_tensor(out=k.y[:, t, :], in0=k.bank[t % 4][:, 0:NT], scalar=-1.0 / 64,
                                             in1=k.y[:, t, :], op0=ALU.mult, op1=ALU.add).then_inc(s_c, 1)
                    dve.wait_ge(s_c, t + 1)
                    dve.tensor_tensor(sq[:, t, :], k.y[:, t, :], k.y[:, t, :], ALU.mult).then_inc(s_q, 1)
                dve.wait_ge(s_r, RT)
                step(dve.reciprocal(sd[:, :, :], sd[:, :, :]))
                step(dve.tensor_tensor(k.y, k.y, sd[:, :, :], ALU.mult))
                for t in range(RT):
                    ins = dve.tensor_scalar(k.y[:, t, :], k.y[:, t, :], k.par[:, C_LNW + t:C_LNW + t + 1],
                                            k.par[:, C_LNB + t:C_LNB + t + 1], ALU.mult, ALU.add)
                step(ins)
                step(dve.tensor_tensor(k.y, k.y, k.bonus, ALU.add))
                step(dve.tensor_tensor(k.mixT[:, RT:KT, :], k.y, k.g[:, :, :], ALU.mult))


CB, CS = 32, 16
PAST, PAGE = 2048, 128
N_PAGES = PAST // PAGE
NCP = TP // CS - 1
NCS = PAST // CS - 1
CMP_T, SLC_T, WIN_T = 8, 12, 16
SELB, TOPK = 64, 16
NSEL = PAST // SELB + 1
WINL = 512
ROW = 512
KVW = 256
FAR = 1.0e33


def phase_rows(k, A):
    nc = k.nc
    with ExitStack() as c:
        zero = k.zero_rows
        s_t, s_c, s_z, s_o = k.sem("j_transposed"), k.sem("j_copied"), k.sem("j_zero"), k.sem("j_written")
        s_gate = k.sem("j_gates_written")
        k.rows_written = s_o
        k.s_cw = k.sem("q_weights")
        n_out = [0]
        with nc.Block() as block:
            @block.gpsimd
            def _(pool):
                pool.memset(zero[:, :], 0.0).then_inc(s_z, 1)

            @block.scalar
            def _(act):
                for i, (a, b) in enumerate(((A["cmp_k_w1"], A["cmp_k_w2"]), (A["cmp_v_w1"], A["cmp_v_w2"]))):
                    act.dma_start(k.cp_w1[:, i, :, :], a[0].rearrange("s d e -> d s e")).then_inc(k.s_cw, 16)
                    act.dma_start(k.cp_w2[:, i, :], b[0]).then_inc(k.s_cw, 16)

            @block.tensor
            def _(pe):
                for i, (at, n) in enumerate(ROWS):
                    for q in range(3):
                        m = 3 * i + q
                        if m >= 6:
                            pe.wait_ge(s_c, m - 5)
                        for j in range(4):
                            ins = pe.transpose(k.bank[m % 6][0:n, j * P:(j + 1) * P],
                                               k.pT[:, CMP_T + 4 * q + j, at:at + n], k.ident[:, :])
                        ins.then_inc(s_t, 1)

            @block.vector
            def _(dve):
                for i, (at, n) in enumerate(ROWS):
                    for q in range(3):
                        m = 3 * i + q
                        dve.wait_ge(s_t, m + 1)
                        dve.tensor_copy(k.kvrows[0:n, i, q * ROW:(q + 1) * ROW], k.bank[m % 6][0:n, :]).then_inc(s_c, 1)

            @block.sync
            def _(sp):
                def out(dst, src, **how):
                    sp.dma_start(dst, src, **how).then_inc(s_o, 16)
                    n_out[0] += 1
                r = lambda v: v.rearrange("s kv g d -> s (kv g d)")
                sp.dma_start(k.gate_dram[:, :], k.gates[0:NS, 2, :]).then_inc(s_gate, 16)
                sp.wait_ge(s_gate, 16)
                for h in range(HEADS):
                    for j in range(3):
                        out(k.sgates[TS * h:TS * h + TS, :, j],
                            k.gate_dram[:, j * HEADS + h].rearrange("(b t) -> t b", t=TS),
                            allow_slow_non_contiguous=True)
                out(A["win_kv_sample"][0, :, 0:WINL - TS].rearrange("b s kv g d -> b (s kv g d)"),
                    A["state_win_kv"][0, :, TS:WINL].rearrange("b s kv g d -> b (s kv g d)"))
                sp.wait_ge(s_z, 1)
                for i in range(2):
                    out(r(A["win_kv_prompt"][0, 0, i * P:(i + 1) * P]), zero[:, :])
                sp.wait_ge(s_c, 9)
                for i in range(2):
                    out(r(A["cmp_kv_prompt"][0, 0, i * P:(i + 1) * P]), k.kvrows[:, i, 0:ROW])
                    out(r(A["slc_kv_prompt"][0, 0, i * P:(i + 1) * P]), k.kvrows[:, i, ROW:2 * ROW])
                    out(r(A["win_kv_prompt"][0, 0, TP + i * P:TP + (i + 1) * P]), k.kvrows[:, i, 2 * ROW:3 * ROW])
                out(A["cmp_kv_sample"][0].rearrange("b t kv g d -> (b t) (kv g d)"), k.kvrows[0:NS, 2, 0:ROW])
                out(A["slc_kv_sample"][0].rearrange("b t kv g d -> (b t) (kv g d)"), k.kvrows[0:NS, 2, ROW:2 * ROW])
                for b in range(NB):
                    out(r(A["win_kv_sample"][0, b, WINL - TS:WINL]), k.kvrows[TS * b:TS * b + TS, 2, 2 * ROW:3 * ROW])
        k.n_rows_written = 16 * n_out[0]


def phase_compress_prompt(k, A):
    nc = k.nc
    with ExitStack() as c:
        sb = lambda name, shape: k.sb(name, shape, F32, c)
        w1, w2, sil = k.cp_w1, k.cp_w2, sb("cp_silu", [P, 2, 2 * NCP])
        s_w = k.s_cw
        s_pre, s_sil, s_out, s_kv = (k.sem(n) for n in ("q_pre", "q_silu", "q_multiplied", "q_done"))
        with nc.Block() as block:
            @block.tensor
            def _(pe):
                pe.wait_ge(s_w, 64)
                compress_project(k, pe, NCP, w1, w2, sil,
                                 lambda i, s: k.pT[:, CMP_T + 2 * i:CMP_T + 2 * i + 2, s:s + CS * (NCP - 1) + 1:CS],
                                 s_pre, lambda: pe.wait_ge(s_sil, 2), s_out)

            @block.scalar
            def _(act):
                for i in range(2):
                    act.wait_ge(s_pre, i + 1)
                    act.activation(sil[:, i, :], k.bank[4 + i][:, 0:2 * NCP], ACT.Silu, bias=k.peb[:, i:i + 1])\
                        .then_inc(s_sil, 1)

            @block.vector
            def _(dve):
                dve.wait_ge(s_out, 1)
                dve.tensor_copy(k.kcTp[:, :], k.bank[6][:, 0:2 * NCP]).then_inc(s_kv, 1)
                dve.tensor_copy(k.vcp[0:NCP, :], k.bank[7][0:NCP, 0:KVW]).then_inc(s_kv, 1)


def phase_attend_prompt(k, A):
    nc = k.nc
    with ExitStack() as c:
        sb = lambda name, shape, dt=F32: k.sb(name, shape, dt, c)
        dtok, dcmp = sb("d_tok", [P, TP]), sb("d_cmp", [P, 2, NCP])
        far = sb("d_far", [P, TP])
        slope = sb("neg_slopes", [P, HEADS])
        rowok = sb("row_has_block", [P, 1])
        q = sb("q_head", [P, TP])
        NK = (P, TP)
        s_ = [sb(f"scores{i}", [P, 16 + 2 * NK[i]]) for i in range(2)]
        mx, sm, fac = sb("neg_max", [P, 2, 3]), sb("exp_sums", [P, 2, 3]), sb("factors", [P, 2, 3])
        pt = [sb(f"probsT{i}", [P, 2 * NK[i]]) for i in range(2)]
        ptc = sb("probsT_cmp", [16, 2, P])
        s_i, s_i2, s_v, s_p, s_a, s_in = (k.sem(n) for n in ("m_iota", "m_setup", "m_dve_stage", "m_pe_stage",
                                                             "m_exp_stage", "m_dve_inner"))
        VST, PST, AST, IN = 8, 5, 2, 6
        with nc.Block() as block:
            @block.gpsimd
            def _(pool):
                pool.iota(dtok[:, :], pattern=[[-1, TP]], base=P, channel_multiplier=1,
                          allow_small_or_imprecise_dtypes=True).then_inc(s_i, 1)
                pool.iota(dcmp[:, :, :], pattern=[[P, 2], [-CS, NCP]], base=-(CB - 1), channel_multiplier=1,
                          allow_small_or_imprecise_dtypes=True).then_inc(s_i, 1)
                for h in range(HEADS):
                    ins = pool.memset(slope[:, h:h + 1], -2.0 ** (-8.0 * (h + 1) / HEADS))
                ins.then_inc(s_i, 1)
                pool.affine_select(out=rowok[:, :], in_=k.ones[:, 0:1], compare_op=ALU.is_ge, fill=0.0, base=-(CB - 1),
                                   pattern=[[0, 1]], channel_multiplier=1).then_inc(s_i, 1)

            @block.vector
            def _(dve):
                dve.wait_ge(s_i, 4)
                step = Chain(dve, s_i2)
                step(dve.tensor_scalar(far[:, :], dtok[:, :], 0.0, FAR, ALU.is_lt, ALU.mult))
                step(dve.tensor_tensor(dtok[:, :], dtok[:, :], far[:, :], ALU.add))
                fl = dcmp[:, :, :].rearrange("p a b -> p (a b)")
                step(dve.tensor_scalar(far[:, 0:2 * NCP], fl, 0.0, FAR, ALU.is_lt, ALU.mult))
                step(dve.tensor_tensor(fl, fl, far[:, 0:2 * NCP], ALU.add))
        with nc.Block() as block:
            @block.sync
            def _(sp):
                sp.wait_ge(k.rows_written, k.n_rows_written)

            def each_head(eng, body):
                for g in range(GROUPS):
                    with eng.Fori(0, HPG) as hh:
                        body(g, hh, hh + HPG * g)

            @block.tensor
            def _(pe):
                def body(g, hh, n):
                    v = lambda i: pe.wait_ge(s_v, n * VST + i)
                    v(1)
                    for t in range(2):
                        qt = q[:, t * P:(t + 1) * P]
                        pe.matmul(k.bank[t][:, TP:TP + NCP], qt, k.kcTp[:, g * NCP:(g + 1) * NCP], start=True, stop=True)
                        pe.matmul(k.bank[t][:, 0:NK[t]], qt, k.pT[:, SLC_T + g, 0:NK[t]], start=True, stop=True)
                        pe.matmul(k.bank[2 + t][:, 0:NK[t]], qt, k.pT[:, WIN_T + g, 0:NK[t]], start=True, stop=True)\
                            .then_inc(s_p, 1)
                    for t in range(2):
                        v(4 + t)
                        out_c = (k.bank[4][0:NCP, 2 * P:3 * P], k.bank[7][0:NCP, 0:P])[t]
                        pe.transpose(out_c, s_[t][:, 0:NCP], k.ident[:, :])
                        for j in range(2 * NK[t] // P):
                            ins = pe.transpose(k.bank[4 + t][:, j * P:(j + 1) * P], s_[t][:, 16 + j * P:16 + (j + 1) * P],
                                               k.ident[:, :])
                        ins.then_inc(s_p, 1)
                    for t in range(2):
                        v(6 + t)
                        out = k.bank[6][:, t * P:(t + 1) * P]
                        pe.matmul(out, k.vcp[0:NCP, g * P:(g + 1) * P], ptc[0:NCP, t, :], start=True, stop=False)
                        for j in range(2 * NK[t] // P):
                            per = NK[t] // P
                            col = (1 + j // per) * ROW + KVW + g * P
                            ins = pe.matmul(out, k.kvrows[:, j % per, col:col + P], pt[t][:, j * P:(j + 1) * P],
                                            start=False, stop=(j == 2 * per - 1))
                    ins.then_inc(s_p, 1)
                each_head(pe, body)

            @block.scalar
            def _(act):
                def body(g, hh, n):
                    for t in range(2):
                        act.wait_ge(s_v, n * VST + 2 + t)
                        for i, (a, b) in enumerate(((0, NCP), (16, 16 + NK[t]), (16 + NK[t], 16 + 2 * NK[t]))):
                            ins = act.activation(s_[t][:, a:b], s_[t][:, a:b], ACT.Exp, bias=mx[:, t, i:i + 1],
                                                 accum_out=sm[:, t, i:i + 1])
                        ins.then_inc(s_a, 1)
                each_head(act, body)

            @block.vector
            def _(dve):
                def body(g, hh, n):
                    step = Chain(dve, s_v, n * VST)
                    inner = Chain(dve, s_in, n * IN)
                    p = lambda i: dve.wait_ge(s_p, n * PST + i)
                    step(dve.tensor_scalar(q[:, :], k.pT[:, bass.ds(n, 1), 0:TP].rearrange("p o n -> p (o n)"), SCALE,
                                           None, ALU.mult))
                    sl = slope[:, bass.ds(n, 1)]
                    for t in range(2):
                        p(1 + t)
                        nk = NK[t]
                        dist = dtok[:, TP - nk:TP]
                        for o, ps, dd in ((0, k.bank[t][:, TP:TP + NCP], dcmp[:, t, :]), (16, k.bank[t][:, 0:nk], dist),
                                          (16 + nk, k.bank[2 + t][:, 0:nk], dist)):
                            w = NCP if o == 0 else nk
                            ins = dve.scalar_tensor_tensor(out=s_[t][:, o:o + w], in0=dd, scalar=sl, in1=ps, op0=ALU.mult,
                                                           op1=ALU.add)
                        inner(ins)
                        dve.tensor_reduce(mx[:, t, 0:1], s_[t][:, 0:NCP], AX.X, ALU.max, negate=True)
                        step(dve.tensor_reduce(mx[:, t, 1:3], s_[t][:, 16:16 + 2 * nk].rearrange("p (a n) -> p a n", a=2),
                                               AX.X, ALU.max, negate=True))
                    for t in range(2):
                        nk = NK[t]
                        dve.wait_ge(s_a, n * AST + 1 + t)
                        inner(dve.reciprocal(fac[:, t, :], sm[:, t, :]))
                        gate = k.gates[:, t, :].rearrange("p (r h) -> p r h", h=HEADS)[:, :, bass.ds(n, 1)]\
                            .rearrange("p r o -> p (r o)")
                        ins = dve.tensor_tensor(fac[:, t, :], fac[:, t, :], gate, ALU.mult)
                        inner(ins)
                        if t == 0:
                            dve.tensor_scalar(s_[t][:, 0:NCP], s_[t][:, 0:NCP], fac[:, t, 0:1], rowok[:, :], ALU.mult, ALU.mult)
                        else:
                            dve.tensor_scalar(s_[t][:, 0:NCP], s_[t][:, 0:NCP], fac[:, t, 0:1], None, ALU.mult)
                        for i in range(2):
                            part = s_[t][:, 16 + i * nk:16 + (i + 1) * nk]
                            ins = dve.tensor_scalar(part, part, fac[:, t, 1 + i:2 + i], None, ALU.mult)
                        step(ins)
                    for t in range(2):
                        p(3 + t)
                        dve.tensor_copy(ptc[0:NCP, t, :], (k.bank[4][0:NCP, 2 * P:3 * P], k.bank[7][0:NCP, 0:P])[t])
                        step(dve.tensor_copy(pt[t][:, :], k.bank[4 + t][:, 0:2 * NK[t]]))
                    p(5)
                    step(dve.tensor_scalar(k.mixT[:, bass.ds(n, 1), 0:TP].rearrange("p o n -> p (o n)"),
                                           k.bank[6][:, 0:TP], 1.0, None, ALU.mult))
                    assert step.n == VST and inner.n == IN, (step.n, inner.n)
                each_head(dve, body)


def phase_attend_samples(k, A):
    nc = k.nc
    R = HEADS * TS
    with ExitStack() as c:
        sb = lambda name, shape, dt=F32: k.sb(name, shape, dt, c)
        k.kcT, k.vc = sb("kcT", [P, NB, 2 * NCS]), sb("vc", [P, NB, KVW])
        PG = 4
        NQ = N_PAGES // PG
        kraw = [sb(f"slc_k{i}", [P, PG, KVW]) for i in range(NQ)]
        vraw = [sb(f"slc_v{i}", [P, N_PAGES, KVW]) for i in range(2)]
        wraw = [sb(f"win_raw{i}", [P, WINL // P, ROW]) for i in range(2)]
        vnew = [sb(f"v_new{i}", [TS, 2, KVW]) for i in range(2)]
        kt = sb("slc_kT", [P, GROUPS, PAST])
        wt = sb("win_kT", [P, GROUPS, WINL])
        qz = sb("q_padded", [P, GROUPS, R])
        vcb = sb("vc_sample", [NCS, KVW])
        S, W = PAST + TS, WINL + TS
        s_s, s_w, s_c = sb("s_slc", [R, S]), sb("s_win", [R, W]), sb("s_cmp", [R, NCS + 1])
        p_c = sb("p_cmp", [R, NCS + 1])
        b_s, b_w, b_c = sb("bias_slc", [R, S]), sb("bias_win", [R, W]), sb("bias_cmp", [R, NCS + 1])
        cmpx = sb("compare", [R, NSEL, NSEL])
        cmpe = sb("compare_eq", [R, NSEL, NSEL])
        before = k.pT[0:R, CMP_T:CMP_T + 4, :].rearrange("p a n -> p (a n)")[:, 0:NSEL * NSEL]\
            .rearrange("p (i j) -> p i j", i=NSEL)
        imp, drop = sb("importance", [R, NSEL]), sb("dropped", [R, NSEL])
        forced = sb("forced", [R, NSEL])
        over = sb("overlap", [NCS, NSEL])
        mx, sm, fac = sb("s_negmax", [R, 3]), sb("s_sums", [R, 3]), sb("s_factors", [R, 3])
        rowi, tstep, nslope = sb("row_index", [R, 4], I32), sb("row_step", [R, 1]), sb("row_slope", [R, 1])
        pts = sb("s_probsT", [P, N_PAGES, R])
        pto = sb("s_probsT_rest", [P, 8, R])
        psg, psb = sb("p_group", [P, 8]), sb("p_group_rows", [P, GROUPS, HPG, TS])
        table = sb("slc_table", [1, NB * N_PAGES], I32)
        s_i, s_tab = k.sem("n_iota"), k.sem("n_table")
        s_k = [k.sem(f"n_k_pages{i}") for i in range(NQ)]
        s_vr = [k.sem(f"n_v_pages{i}") for i in range(2)]
        s_wr = [k.sem(f"n_window{i}") for i in range(2)]
        s_v, s_p, s_a, s_in = k.sem("n_dve_stage"), k.sem("n_pe_stage"), k.sem("n_exp_stage"), k.sem("n_dve_inner")
        s_kt = k.sem("n_k_transposed")
        s_kc = k.sem("n_k_copied")
        NKT = N_PAGES // 2 + 2
        with nc.Block() as block:
            @block.gpsimd
            def _(pool):
                f = dict(allow_small_or_imprecise_dtypes=True)
                pool.iota(b_s[:, :], pattern=[[-1, S]], base=PAST, channel_multiplier=0, **f).then_inc(s_i, 1)
                pool.iota(b_w[:, :], pattern=[[-1, W]], base=WINL, channel_multiplier=0, **f).then_inc(s_i, 1)
                pool.iota(b_c[:, 0:NCS], pattern=[[-CS, NCS]], base=PAST - (CB - 1), channel_multiplier=0, **f).then_inc(s_i, 1)
                pool.iota(rowi[:, 0:1], pattern=[[0, 1]], base=0, channel_multiplier=1).then_inc(s_i, 1)
                pool.memset(qz[:, :, :], 0.0).then_inc(s_i, 1)
                pool.memset(forced[:, :], 0.0).then_inc(s_i, 1)
                pool.wait_ge(s_i, 6)
                pool.memset(forced[:, 0:1], 1.0e4).then_inc(s_i, 1)
                pool.memset(forced[:, NSEL - 2:NSEL], 1.0e4).then_inc(s_i, 1)
                pool.affine_select(out=before[:, :, :], in_=k.ones[0:R, 0:1].unsqueeze(2).to_broadcast([R, NSEL, NSEL]),
                                   compare_op=ALU.is_gt, fill=0.0, base=0, pattern=[[1, NSEL], [-1, NSEL]],
                                   channel_multiplier=0).then_inc(s_i, 1)
                pool.affine_select(out=over[:, :], in_=k.ones[0:NCS, 0:NSEL], compare_op=ALU.is_ge, fill=0.0,
                                   base=SELB - 1, pattern=[[SELB, NSEL]], channel_multiplier=-CS).then_inc(s_i, 1)
                pool.wait_ge(s_i, 10)
                pool.affine_select(out=over[:, :], in_=over[:, :], compare_op=ALU.is_ge, fill=0.0, base=CB - 1,
                                   pattern=[[-SELB, NSEL]], channel_multiplier=CS).then_inc(s_i, 1)

            @block.vector
            def _(dve):
                step = k.steps.chain(dve)
                dve.wait_ge(s_i, 11)
                step(dve.tensor_scalar(rowi[:, 1:2], rowi[:, 0:1], TS - 1, None, ALU.bitwise_and))
                step(dve.tensor_scalar(rowi[:, 2:3], rowi[:, 0:1], 2, None, ALU.logical_shift_right))
                step(dve.tensor_copy(tstep[:, :], rowi[:, 1:2]))
                step(dve.tensor_scalar(rowi[:, 3:4], rowi[:, 2:3], -1.0, 126.0, ALU.mult, ALU.add))
                step(dve.tensor_scalar(rowi[:, 0:1], rowi[:, 3:4], 23, None, ALU.logical_shift_left))
                step(dve.tensor_scalar(nslope[:, :], rowi[:, 0:1].bitcast(F32), -1.0, None, ALU.mult))
                for tile, lo in ((b_s, PAST), (b_w, WINL)):
                    step(dve.tensor_scalar(tile[:, :], tile[:, :], tstep[:, 0:1], None, ALU.add))
                    new = tile[:, lo:lo + TS]
                    step(dve.tensor_scalar(cmpx[:, 0, 0:TS], new, 0.0, FAR, ALU.is_lt, ALU.mult))
                    step(dve.tensor_tensor(new, new, cmpx[:, 0, 0:TS], ALU.add))
                old = b_w[:, 0:TS]
                step(dve.tensor_scalar(cmpx[:, 0, 0:TS], old, float(WINL), FAR, ALU.is_ge, ALU.mult))
                step(dve.tensor_tensor(old, old, cmpx[:, 0, 0:TS], ALU.add))
                step(dve.tensor_scalar(b_c[:, 0:NCS], b_c[:, 0:NCS], tstep[:, 0:1], None, ALU.add))
                for tile in (b_s[:, :], b_w[:, :], b_c[:, 0:NCS]):
                    step(dve.tensor_scalar(tile, tile, nslope[:, 0:1], None, ALU.mult))

            @block.sync
            def _(sp):
                sp.dma_start(table[:, :], A["page_table"].rearrange("b n -> (b n)").rearrange("(o n) -> o n", o=1))\
                    .then_inc(s_tab, 16)
                sp.dma_start(k.kcT[:, :, :], k.kc_dram[:, :, :]).then_inc(s_tab, 16)
                sp.dma_start(k.vc[0:NCS, :, :], k.vc_dram[:, :, :]).then_inc(s_tab, 16)
                sp.wait_ge(s_tab, 48)

        VST, PST, AST, IN = 12, 7, 3, 14
        kv2 = lambda v: v.rearrange("s kv g d -> s (kv g d)")
        with nc.Block() as block:
            @block.sync
            def _(sp):
                def load(b, u, keys_used, buffers_used):
                    if buffers_used:
                        sp.wait_ge(s_p, (b - 1) * PST)
                    row = lambda v: v.rearrange("o t kv g d -> (o t) (kv g d)")
                    sp.dma_start(vnew[u][:, 0, :], row(A["slc_kv_sample"][0, bass.ds(b, 1)])[:, KVW:]).then_inc(s_wr[u], 16)
                    sp.dma_start(vnew[u][:, 1, :], row(A["win_kv_sample"][0, bass.ds(b, 1), WINL - TS:WINL])[:, KVW:])\
                        .then_inc(s_wr[u], 16)
                    sp.dma_start(wraw[u][:, :, :], A["state_win_kv"][0, bass.ds(b, 1)]
                                 .rearrange("o (n p) kv g d -> p (o n) (kv g d)", p=P)).then_inc(s_wr[u], 16)
                    for r in range(NQ):
                        if keys_used:
                            sp.wait_ge(s_kt, (b - 1) * NKT + 2 * (r + 1))
                        for j in range(PG):
                            page = sp.value_load(table[0:1, bass.ds(b * N_PAGES + r * PG + j, 1)], min_val=0,
                                                 max_val=A["cache_slc_kv"].shape[1] - 1)
                            src = A["cache_slc_kv"][0, bass.ds(page, 1)].rearrange("o s kv g d -> (o s) (kv g d)")
                            sp.dma_start(kraw[r][:, j, :], src[:, 0:KVW]).then_inc(s_k[r], 16)
                            sp.dma_start(vraw[u][:, r * PG + j, :], src[:, KVW:]).then_inc(s_vr[u], 16)
                load(0, 0, False, False)
                load(1, 1, True, False)
                with sp.Fori(1, NB // 2) as it:
                    for u in range(2):
                        load(it * 2 + u, u, True, True)

            @block.tensor
            def _(pe):
                def body(b, u, it):
                    v = lambda i: pe.wait_ge(s_v, b * VST + i)
                    v(1)
                    for g in range(2):
                        ins = pe.matmul(k.bank[0][0:R, 0:NCS], qz[:, g, :], kc(b, g), start=(g == 0), stop=(g == 1))
                    for br in range(2):
                        for g in range(2):
                            ins = pe.matmul(k.bank[0][0:R, 128 + TS * br:128 + TS * (br + 1)], qz[:, g, :],
                                            knew(b, (SLC_T, WIN_T)[br] + g), start=(g == 0), stop=(g == 1))
                    ins.then_inc(s_p, 1)

                    def turned(m, tiles):
                        if m >= 2:
                            pe.wait_ge(s_kc, b * NKT + m - 1)
                        for j, src in enumerate(tiles):
                            ins = pe.transpose(k.bank[1 + m % 2][:, j * P:(j + 1) * P], src, k.ident[:, :])
                        ins.then_inc(s_kt, 1)
                    for m in range(N_PAGES // 2):
                        r = m // 2
                        if m % 2 == 0:
                            pe.wait_ge(s_k[r], (b + 1) * 16 * PG)
                        turned(m, [kraw[r][:, (2 * m + i) % PG, g * P:(g + 1) * P] for g in range(2) for i in range(2)])
                    pe.wait_ge(s_wr[u], (it + 1) * 48)
                    for m in range(2):
                        turned(N_PAGES // 2 + m, [wraw[u][:, 2 * m + i, g * P:(g + 1) * P] for g in range(2) for i in range(2)])
                    pe.wait_ge(s_kc, (b + 1) * NKT)
                    for ch in range(4):
                        if ch >= 2:
                            v(3 + ch - 2)
                        for g in range(2):
                            ins = pe.matmul(k.bank[3 + ch % 2][0:R, :], qz[:, g, :], kt[:, g, ch * 512:(ch + 1) * 512],
                                            start=(g == 0), stop=(g == 1))
                        if ch == 1:
                            for g in range(2):
                                ins = pe.matmul(k.bank[5][0:R, :], qz[:, g, :], wt[:, g, :], start=(g == 0), stop=(g == 1))
                            ins.then_inc(s_p, 1)
                        if ch == 3:
                            ins.then_inc(s_p, 1)
                    v(7)
                    pe.matmul(k.bank[7][0:NCS, 0:R], p_c[:, 0:NCS], k.ident[0:R, 0:R], start=True, stop=True)
                    pe.transpose(k.bank[7][0:NCS, R:2 * R], s_c[:, 0:NCS], k.ident[0:R, 0:R]).then_inc(s_p, 1)
                    v(8)
                    pe.matmul(k.bank[0][0:R, 160:160 + NSEL], psb[0:NCS, :, :, :].rearrange("p g h t -> p (g h t)"),
                              over[:, :], start=True, stop=True).then_inc(s_p, 1)
                    v(10)
                    pe.matmul(k.bank[6][:, 0:R], s_s[:, 0:P], k.ident[0:R, 0:R], start=True, stop=True)
                    for j in range(1, N_PAGES):
                        pe.transpose(k.bank[6][:, j * R:(j + 1) * R], s_s[:, j * P:(j + 1) * P], k.ident[0:R, 0:R])
                    pe.transpose(k.bank[7][0:TS, 2 * R:3 * R], s_s[:, PAST:S], k.ident[0:R, 0:R])
                    pe.transpose(k.bank[7][0:TS, 3 * R:4 * R], s_w[:, WINL:W], k.ident[0:R, 0:R])
                    for j in range(WINL // P):
                        ins = pe.transpose(k.bank[7][:, (4 + j) * R:(5 + j) * R], s_w[:, j * P:(j + 1) * P], k.ident[0:R, 0:R])
                    ins.then_inc(s_p, 1)
                    pe.wait_ge(s_vr[u], (it + 1) * 16 * N_PAGES)
                    v(11)
                    for g in range(2):
                        cols, d = slice(16 * g, 16 * g + 16), slice(g * P, (g + 1) * P)
                        out = k.bank[5][:, cols]
                        pe.matmul(out, vcb[:, d], pto[0:NCS, 1, cols], start=True, stop=False)
                        for br in range(2):
                            pe.matmul(out, vnew[u][:, br, d], pto[0:TS, 2 + br, cols], start=False, stop=False)
                        for j in range(WINL // P):
                            pe.matmul(out, wraw[u][:, j, KVW + g * P:KVW + (g + 1) * P], pto[:, 4 + j, cols], start=False,
                                      stop=False)
                        for j in range(N_PAGES):
                            ins = pe.matmul(out, vraw[u][:, j, d], pts[:, j, cols], start=False, stop=(j == N_PAGES - 1))
                    ins.then_inc(s_p, 1)
                kc = lambda b, g: k.kcT[:, bass.ds(b, 1), g * NCS:(g + 1) * NCS].rearrange("p o n -> p (o n)")
                knew = lambda b, t: k.pT[:, t, bass.ds(TP + b * TS, TS)]
                with pe.Fori(0, NB // 2) as it:
                    for u in range(2):
                        body(it * 2 + u, u, it)

            @block.scalar
            def _(act):
                def body(b):
                    for m in range(NKT):
                        act.wait_ge(s_kt, b * NKT + m + 1)
                        bank = k.bank[1 + m % 2][:, :].rearrange("p (g n) -> p g n", g=2)
                        dst = kt[:, :, m * 256:(m + 1) * 256] if m < N_PAGES // 2 else \
                            wt[:, :, (m - N_PAGES // 2) * 256:(m - N_PAGES // 2 + 1) * 256]
                        act.copy(dst, bank).then_inc(s_kc, 1)
                    for i, (tile, n, at) in enumerate(((s_c, NCS, 2), (s_w, W, 6), (s_s, S, 9))):
                        act.wait_ge(s_v, b * VST + at)
                        act.activation(tile[:, 0:n], tile[:, 0:n], ACT.Exp, bias=mx[:, i:i + 1], accum_out=sm[:, i:i + 1])\
                            .then_inc(s_a, 1)
                with act.Fori(0, NB) as b:
                    body(b)

            @block.vector
            def _(dve):
                def body(b):
                    step = Chain(dve, s_v, b * VST)
                    inner = Chain(dve, s_in, b * IN)
                    p = lambda i: dve.wait_ge(s_p, b * PST + i)
                    for g in range(2):
                        dve.tensor_scalar(qz[:, g, 16 * g:16 * g + 16].rearrange("p (h t) -> p h t", t=TS),
                                          k.pT[:, HPG * g:HPG * (g + 1), bass.ds(TP + b * TS, TS)], SCALE, None, ALU.mult)
                    step(dve.tensor_scalar(vcb[:, :], k.vc[0:NCS, bass.ds(b, 1), :].rearrange("p o n -> p (o n)"), 1.0,
                                           None, ALU.mult))
                    p(1)
                    ps = k.bank[0][0:R, :]
                    dve.tensor_tensor(s_s[:, PAST:S], ps[:, 128:128 + TS], b_s[:, PAST:S], ALU.add)
                    dve.tensor_tensor(s_w[:, WINL:W], ps[:, 128 + TS:128 + 2 * TS], b_w[:, WINL:W], ALU.add)
                    inner(dve.tensor_tensor(s_c[:, 0:NCS], ps[:, 0:NCS], b_c[:, 0:NCS], ALU.add))
                    step(dve.tensor_reduce(mx[:, 0:1], s_c[:, 0:NCS], AX.X, ALU.max, negate=True))
                    p(2)
                    for ch in range(4):
                        if ch == 2:
                            p(3)
                        ins = dve.tensor_tensor(s_s[:, ch * 512:(ch + 1) * 512], k.bank[3 + ch % 2][0:R, :],
                                                b_s[:, ch * 512:(ch + 1) * 512], ALU.add)
                        if ch < 3:
                            step(ins)
                        else:
                            inner(dve.tensor_tensor(s_w[:, 0:WINL], k.bank[5][0:R, :], b_w[:, 0:WINL], ALU.add))
                            step(dve.tensor_reduce(mx[:, 1:2], s_w[:, :], AX.X, ALU.max, negate=True))
                    dve.wait_ge(s_a, b * 3 + 1)
                    inner(dve.reciprocal(fac[:, 0:1], sm[:, 0:1]))
                    inner(dve.tensor_scalar(p_c[:, 0:NCS], s_c[:, 0:NCS], fac[:, 0:1], None, ALU.mult))
                    gate = lambda r: k.sgates[:, bass.ds(b, 1), r:r + 1].rearrange("p o r -> p (o r)")
                    step(dve.tensor_scalar(s_c[:, 0:NCS], p_c[:, 0:NCS], gate(0), None, ALU.mult))
                    p(4)
                    inner(dve.tensor_copy(pto[0:NCS, 0:2, :].rearrange("p a r -> p (a r)"), k.bank[7][0:NCS, 0:2 * R]))
                    inner(dve.tensor_reduce(psg[0:NCS, :].rearrange("p (g t) -> p g t", g=2),
                                            pto[0:NCS, 0, :].rearrange("p (g h t) -> p g t h", g=2, h=HPG), AX.X, ALU.add))
                    step(dve.tensor_copy(psb[0:NCS, :, :, :], psg[0:NCS, :].rearrange("p (g t) -> p g t", g=2).unsqueeze(2)
                                         .to_broadcast([NCS, GROUPS, HPG, TS])))
                    p(5)
                    inner(dve.tensor_tensor(imp[:, :], ps[:, 160:160 + NSEL], forced[:, :], ALU.add))
                    mine = imp[:, :].unsqueeze(2).to_broadcast([R, NSEL, NSEL])
                    other = imp[:, :].unsqueeze(1).to_broadcast([R, NSEL, NSEL])
                    dve.tensor_tensor(cmpx[:, :, :], other, mine, ALU.is_gt)
                    inner(dve.tensor_tensor(cmpe[:, :, :], other, mine, ALU.is_equal))
                    inner(dve.tensor_tensor(cmpe[:, :, :], cmpe[:, :, :], before[:, :, :], ALU.mult))
                    inner(dve.tensor_tensor(cmpx[:, :, :], cmpx[:, :, :], cmpe[:, :, :], ALU.add))
                    inner(dve.tensor_reduce(drop[:, :], cmpx[:, :, :], AX.X, ALU.add))
                    inner(dve.tensor_scalar(drop[:, :], drop[:, :], TOPK - 0.5, NEG, ALU.is_gt, ALU.mult))
                    past = s_s[:, 0:PAST].rearrange("p (j s) -> p j s", s=SELB)
                    inner(dve.tensor_tensor(past, past, drop[:, 0:NSEL - 1].unsqueeze(2).to_broadcast([R, NSEL - 1, SELB]),
                                            ALU.add))
                    step(dve.tensor_reduce(mx[:, 2:3], s_s[:, :], AX.X, ALU.max, negate=True))
                    dve.wait_ge(s_a, b * 3 + 3)
                    dve.reciprocal(fac[:, 1:2], sm[:, 1:2])
                    inner(dve.reciprocal(fac[:, 2:3], sm[:, 2:3]))
                    dve.tensor_scalar(s_w[:, :], s_w[:, :], fac[:, 1:2], gate(2), ALU.mult, ALU.mult)
                    step(dve.tensor_scalar(s_s[:, :], s_s[:, :], fac[:, 2:3], gate(1), ALU.mult, ALU.mult))
                    p(6)
                    dve.tensor_copy(pts[:, :, :].rearrange("p j r -> p (j r)"), k.bank[6][:, :])
                    dve.tensor_copy(pto[0:TS, 2:4, :].rearrange("p a r -> p (a r)"), k.bank[7][0:TS, 2 * R:4 * R])
                    step(dve.tensor_copy(pto[:, 4:8, :].rearrange("p a r -> p (a r)"), k.bank[7][:, 4 * R:8 * R]))
                    p(7)
                    step(dve.tensor_scalar(k.mixT[:, 0:HEADS, bass.ds(TP + b * TS, TS)],
                                           k.bank[5][:, 0:R].rearrange("p (h t) -> p h t", t=TS), 1.0, None, ALU.mult))
                    assert (step.n, inner.n) == (VST, IN), (step.n, inner.n)
                with dve.Fori(0, NB) as b:
                    body(b)


def phase_out(k, A):
    nc = k.nc
    CH = 512
    N_CH = D // CH
    with ExitStack() as c:
        w = [k.sb(f"w_out{i}", [P, KT, CH], F32, c) for i in range(2)]
        part = k.sb("gated", [P, 2, NS], F32, c)
        s_w = [k.sem(f"o_w_landed{i}") for i in range(2)]
        s_tile = k.sem("o_tile_multiplied")
        s_add = k.sem("o_tile_added")
        w_view = A["w_out"][0].rearrange("(k p) n -> p k n", p=P)
        with nc.Block() as block:
            @block.sync
            def _(sp):
                for n in range(N_CH):
                    if n >= 2:
                        sp.wait_ge(s_tile, 4 * (n - 1))
                    sp.dma_start(w[n % 2][:, :, :], w_view[:, :, n * CH:(n + 1) * CH]).then_inc(s_w[n % 2], 16)

            @block.tensor
            def _(pe):
                for m in range(KT):
                    n = m // 4
                    if m % 4 == 0:
                        pe.wait_ge(s_w[n % 2], 16 * (n // 2 + 1))
                    if m >= 4:
                        pe.wait_ge(s_add, m - 3)
                    for t in range(KT):
                        ins = pe.matmul(k.bank[m % 4][:, 0:NT], w[n % 2][:, t, (m % 4) * P:(m % 4 + 1) * P],
                                        k.mixT[:, t, :], start=(t == 0), stop=(t == KT - 1))
                    ins.then_inc(s_tile, 1)

            @block.vector
            def _(dve):
                inner = k.steps.chain(dve)
                for m in range(KT):
                    dve.wait_ge(s_tile, m + 1)
                    ps = k.bank[m % 4]
                    add_gated(k, dve, inner, m, ps[:, 0:TP], ps[:, TP:NT], 32, part[:, m % 2, :]).then_inc(s_add, 1)


def add_gated(k, dve, inner, m, prompt, sample, gate, part):
    by_t = lambda v: v.rearrange("p (b t) -> p b t", t=TS)
    dve.scalar_tensor_tensor(out=k.xT[:, m, 0:TP], in0=prompt, scalar=k.mod[:, gate + m, 0:1], in1=k.xT[:, m, 0:TP],
                             op0=ALU.mult, op1=ALU.add)
    inner(dve.tensor_tensor(by_t(part), by_t(sample), k.mod[:, gate + m, 1:NC].unsqueeze(2).to_broadcast([P, NB, TS]),
                            ALU.mult))
    return dve.tensor_tensor(k.xT[:, m, TP:NT], k.xT[:, m, TP:NT], part, ALU.add)


NGRP, NEXP, EPG = 4, 32, 8
SLOTS = 64
N_OVER = 2 * NT // SLOTS - 1
N_BLK = NEXP + N_OVER
NTT = len(ROWS)


def phase_route(k, A):
    nc = k.nc
    NL = NGRP + NEXP
    with ExitStack() as c:
        sb = lambda name, shape, dt=F32: k.sb(name, shape, dt, c)
        w = sb("w_router", [P, KT, NL])
        bias = sb("router_bias", [P, NL])
        L = sb("logits", [P, NTT, NL])
        tri = sb("earlier", [P, P])
        im = sb("expert_minus_99", [P, NEXP])
        cand, oh, oh2 = sb("candidates", [P, NTT, NEXP]), sb("one_hot1", [P, NTT, NEXP]), sb("one_hot2", [P, NTT, NEXP])
        le, M = sb("expert_logits", [P, NTT, NEXP]), sb("chosen", [P, NTT, NEXP])
        gd, goh = sb("group_logits", [P, NTT, NGRP]), sb("group_one_hot", [P, NTT, NGRP])
        r1 = sb("route_scalars", [P, NTT, 8])
        rank, wt = sb("rank", [P, NTT, NEXP]), sb("route_weights", [P, NTT, NEXP])
        nb, cum, excl = sb("extra_blocks", [P, NEXP]), sb("extra_cum", [P, NEXP]), sb("extra_tmp", [P, NEXP])
        ind, pick = sb("extra_ind", [P, NEXP]), sb("extra_pick", [P, NEXP])
        tmp3 = sb("extra_tmp3", [P, NTT, NEXP])
        ex = sb("extra_scalars", [P, 8])
        ef = sb("expert_float", [P, N_BLK + 1])
        s_w, s_i, s_rows = k.sem("r_weights_landed"), k.sem("r_constants"), k.sem("r_rows_copied")
        s_l, s_e, s_rank, s_p = (k.sem("r_logits"), k.sem("r_exps"), k.sem("r_ranks"),
                                      k.sem("r_rows_transposed"))
        s_v1, s_v2, s_m = k.sem("r_group_max"), k.sem("r_best_two"), k.sem("r_chosen")
        with nc.Block() as block:
            @block.sync
            def _(sp):
                with nc.allow_non_contiguous_dma(reason="small router weights"):
                    sp.dma_start(w[:, :, 0:NGRP], A["w_router_group"][0].rearrange("(k p) n -> p k n", p=P)).then_inc(s_w, 16)
                    sp.dma_start(w[:, :, NGRP:NL], A["w_router_expert"][0].rearrange("(k p) n -> p k n", p=P)).then_inc(s_w, 16)
                sp.wait_ge(s_i, 1)
                sp.dma_start(bias[0:1, 0:NGRP], A["b_router_group"]).then_inc(s_w, 16)
                sp.dma_start(bias[0:1, NGRP:NL], A["b_router_expert"]).then_inc(s_w, 16)

            @block.gpsimd
            def _(pool):
                f = dict(allow_small_or_imprecise_dtypes=True)
                pool.memset(bias[:, :], 0.0).then_inc(s_i, 1)
                pool.memset(L[:, :, :], 0.0).then_inc(s_i, 1)
                pool.memset(rank[:, :, :], 0.0).then_inc(s_i, 1)
                pool.memset(k.slot[:, :, N_BLK:N_BLK + 2], 0.0).then_inc(s_i, 1)
                pool.memset(k.weight[:, :, N_BLK:N_BLK + 2], 0.0).then_inc(s_i, 1)
                pool.iota(im[:, :], pattern=[[1, NEXP]], base=-99, channel_multiplier=0, **f).then_inc(s_i, 1)
                pool.iota(k.slots[:, :], pattern=[[1, SLOTS]], base=0, channel_multiplier=0, **f).then_inc(s_i, 1)
                pool.iota(ef[:, 0:NEXP], pattern=[[1, NEXP]], base=0, channel_multiplier=0, **f).then_inc(s_i, 1)
                pool.affine_select(out=tri[:, :], in_=k.ones[:, :], compare_op=ALU.is_gt, fill=0.0, base=0,
                                   pattern=[[1, P]], channel_multiplier=-1).then_inc(s_i, 1)

            @block.tensor
            def _(pe):
                for n in range(4 * NTT):
                    i, q = divmod(n, 4)
                    at, r = ROWS[i]
                    if n >= 4:
                        pe.wait_ge(s_rows, n - 3)
                    for j in range(4):
                        ins = pe.transpose(k.bank[4 + n % 4][0:r, j * P:(j + 1) * P], k.h2T[:, 4 * q + j, at:at + r],
                                           k.ident[:, :])
                    ins.then_inc(s_p, 1)
                pe.wait_ge(s_w, 64)
                for i, (at, r) in enumerate(ROWS):
                    pe.matmul(k.bank[i][0:r, 0:NL], k.ones[:, 0:r], bias[:, :], start=True, stop=False)
                    for t in range(KT):
                        ins = pe.matmul(k.bank[i][0:r, 0:NL], k.h2T[:, t, at:at + r], w[:, t, :], start=False,
                                        stop=(t == KT - 1))
                    ins.then_inc(s_l, 1)
                pe.wait_ge(s_m, 1)
                for i, (_, r) in enumerate(ROWS):
                    out = k.bank[3][0:r, i * NEXP:(i + 1) * NEXP]
                    for j in range(i):
                        pe.matmul(out, k.ones[:, 0:r], M[:, j, :], start=(j == 0), stop=False)
                    pe.matmul(out, tri[0:r, 0:r], M[0:r, i, :], start=(i == 0), stop=True)
                for i, (_, r) in enumerate(ROWS):
                    ins = pe.matmul(k.bank[0][:, 64:64 + NEXP], k.ones[0:r, :], M[0:r, i, :], start=(i == 0),
                                    stop=(i == NTT - 1))
                ins.then_inc(s_rank, 1)

            @block.scalar
            def _(act):
                for n in range(4 * NTT):
                    i, q = divmod(n, 4)
                    r = ROWS[i][1]
                    act.wait_ge(s_p, n + 1)
                    act.copy(k.h2rows[0:r, i, q * 512:(q + 1) * 512], k.bank[4 + n % 4][0:r, :]).then_inc(s_rows, 1)
                act.wait_ge(s_v1, 1)
                act.activation(cand[:, :, 0:NGRP], gd[:, :, :], ACT.Exp).then_inc(s_e, 1)
                act.wait_ge(s_v2, 1)
                act.activation(r1[:, :, 4:5], r1[:, :, 3:4], ACT.Exp).then_inc(s_e, 1)

            @block.vector
            def _(dve):
                step = k.steps.chain(dve)
                tt = lambda out, a, b, op: step(dve.tensor_tensor(out, a, b, op))
                ts = lambda out, a, s1, s2, o1, o2=None: step(dve.tensor_scalar(out, a, s1, s2, o1, o2) if o2 else
                                                              dve.tensor_scalar(out, a, s1, s2, o1))
                red = lambda out, a, op: step(dve.tensor_reduce(out, a, AX.X, op))
                wide = lambda col, n: col.to_broadcast([P, NTT, n])
                imw = lambda n: im[:, 0:n].unsqueeze(1).to_broadcast([P, NTT, n])

                def first_best(src, out, n, best, at):
                    tt(out, src, wide(best, n), ALU.is_equal)
                    tt(out, out, imw(n), ALU.mult)
                    red(r1[:, :, at:at + 1], out, ALU.min)
                    tt(out, imw(n), wide(r1[:, :, at:at + 1], n), ALU.is_equal)
                dve.wait_ge(s_i, 9)
                for i, (_, r) in enumerate(ROWS):
                    dve.wait_ge(s_l, i + 1)
                    step(dve.tensor_copy(L[0:r, i, :], k.bank[i][0:r, 0:NL]))
                red(r1[:, :, 0:1], L[:, :, 0:NGRP], ALU.max)
                dve.tensor_tensor(gd[:, :, :], L[:, :, 0:NGRP], wide(r1[:, :, 0:1], NGRP), ALU.subtract).then_inc(s_v1, 1)
                first_best(L[:, :, 0:NGRP], goh[:, :, :], NGRP, r1[:, :, 0:1], 1)
                ts(goh[:, :, :], goh[:, :, :], -NEG, NEG, ALU.mult, ALU.add)
                by_g = lambda v: v.rearrange("p i (g e) -> p i g e", e=EPG)
                for i in range(NTT):
                    tt(le[:, i, :].rearrange("p (g e) -> p g e", e=EPG), L[:, i, NGRP:NL].rearrange("p (g e) -> p g e", e=EPG),
                       goh[:, i, :].unsqueeze(2).to_broadcast([P, NGRP, EPG]), ALU.add)
                red(r1[:, :, 2:3], le[:, :, :], ALU.max)
                first_best(le[:, :, :], oh[:, :, :], NEXP, r1[:, :, 2:3], 1)
                step(dve.scalar_tensor_tensor(out=le[:, :, :], in0=oh[:, :, :], scalar=2.0 * NEG, in1=le[:, :, :],
                                              op0=ALU.mult, op1=ALU.add))
                red(r1[:, :, 3:4], le[:, :, :], ALU.max)
                first_best(le[:, :, :], oh2[:, :, :], NEXP, r1[:, :, 3:4], 1)
                dve.tensor_tensor(r1[:, :, 3:4], r1[:, :, 3:4], r1[:, :, 2:3], ALU.subtract).then_inc(s_v2, 1)
                dve.tensor_tensor(M[:, :, :], oh[:, :, :], oh2[:, :, :], ALU.add).then_inc(s_m, 1)
                dve.wait_ge(s_e, 2)
                red(r1[:, :, 5:6], cand[:, :, 0:NGRP], ALU.add)
                ts(r1[:, :, 6:7], r1[:, :, 4:5], 1.0, None, ALU.add)
                tt(r1[:, :, 5:6], r1[:, :, 5:6], r1[:, :, 6:7], ALU.mult)
                step(dve.reciprocal(r1[:, :, 6:7], r1[:, :, 5:6]))
                tt(r1[:, :, 7:8], r1[:, :, 6:7], r1[:, :, 4:5], ALU.mult)
                tt(oh[:, :, :], oh[:, :, :], wide(r1[:, :, 6:7], NEXP), ALU.mult)
                tt(oh2[:, :, :], oh2[:, :, :], wide(r1[:, :, 7:8], NEXP), ALU.mult)
                tt(wt[:, :, :], oh[:, :, :], oh2[:, :, :], ALU.add)
                dve.wait_ge(s_rank, 1)
                for i, (_, r) in enumerate(ROWS):
                    step(dve.scalar_tensor_tensor(out=rank[0:r, i, :], in0=k.bank[3][0:r, i * NEXP:(i + 1) * NEXP],
                                                  scalar=1.0, in1=M[0:r, i, :], op0=ALU.add, op1=ALU.mult))
                ts(rank[:, :, :], rank[:, :, :], 1.0, None, ALU.subtract)
                step(dve.tensor_copy(k.slot[:, :, 0:NEXP], rank[:, :, :]))
                step(dve.tensor_copy(k.weight[:, :, 0:NEXP], wt[:, :, :]))
                cnt = k.bank[0][:, 64:64 + NEXP]
                ts(nb[:, :], cnt, SLOTS + 0.5, None, ALU.is_gt)
                for j in range(2, (NT - 1) // SLOTS + 1):
                    step(dve.scalar_tensor_tensor(out=nb[:, :], in0=cnt, scalar=j * SLOTS + 0.5, in1=nb[:, :], op0=ALU.is_gt,
                                                  op1=ALU.add))
                step(dve.tensor_copy(cum[:, :], nb[:, :]))
                for s in (1, 2, 4, 8, 16):
                    step(dve.tensor_copy(excl[:, :], cum[:, :]))
                    tt(cum[:, s:NEXP], excl[:, s:NEXP], excl[:, 0:NEXP - s], ALU.add)
                step(dve.tensor_copy(ef[:, N_BLK:N_BLK + 1], cum[:, NEXP - 1:NEXP]))
                for o in range(N_OVER):
                    b = NEXP + o
                    ts(ind[:, :], cum[:, :], o + 0.5, None, ALU.is_lt)
                    red(ex[:, 0:1], ind[:, :], ALU.add)
                    tt(pick[:, :], ind[:, :], nb[:, :], ALU.mult)
                    red(ex[:, 1:2], pick[:, :], ALU.add)
                    ts(ex[:, 2:3], ex[:, 0:1], NEXP - 0.5, 1.0e3, ALU.is_gt, ALU.mult)
                    ts(ex[:, 3:4], ex[:, 1:2], -float(SLOTS), float(SLOTS * (1 + o)), ALU.mult, ALU.add)
                    tt(ex[:, 3:4], ex[:, 3:4], ex[:, 2:3], ALU.add)
                    ts(ef[:, b:b + 1], ex[:, 0:1], float(NEXP - 1), None, ALU.min)
                    ts(pick[:, :], ef[:, 0:NEXP], ef[:, b:b + 1], None, ALU.is_equal)
                    pw = pick[:, :].unsqueeze(1).to_broadcast([P, NTT, NEXP])
                    tt(tmp3[:, :, :], rank[:, :, :], pw, ALU.mult)
                    red(k.slot[:, :, b:b + 1], tmp3[:, :, :], ALU.add)
                    ts(k.slot[:, :, b:b + 1], k.slot[:, :, b:b + 1], ex[:, 3:4], None, ALU.subtract)
                    tt(tmp3[:, :, :], wt[:, :, :], pw, ALU.mult)
                    red(k.weight[:, :, b:b + 1], tmp3[:, :, :], ALU.add)
                step(dve.tensor_copy(k.expert[:, :], ef[0:1, :]))


def phase_moe(k, A):
    nc = k.nc
    DE = 512
    CK = 8
    with ExitStack() as c:
        sb = lambda name, shape, dt=F32: k.sb(name, shape, dt, c)
        wg = [sb(f"gate_w{i}", [P, CK, DE]) for i in range(2)]
        wu = [sb(f"up_w{i}", [P, CK, DE]) for i in range(2)]
        wd = [sb(f"down_w{i}", [P, 2, D]) for i in range(2)]
        sel = sb("select", [P, NTT, 2, SLOTS])
        give = sb("give", [P, NTT, 2, 2, SLOTS])
        giveT = sb("giveT", [P, 2, NT])
        x = sb("x_picked", [P, KT, P])
        h = sb("hidden", [P, 2, 256])
        hT = sb("hiddenT", [P, 2, 2, P])
        y = sb("y_rows", [P, 2, D // 2])
        s_w = [k.sem(f"u_w_landed{i}") for i in range(6)]
        s_half = k.sem("u_half_gate_up")
        s_gu = k.sem("u_gate_up")
        s_yh = k.sem("u_half_y")
        s_y = k.sem("u_y_made")
        s_sel = k.sem("u_selected")
        s_x, s_xc = k.sem("u_x_picked"), k.sem("u_x_copied")
        s_silu, s_h = k.sem("u_silu"), k.sem("u_hidden")
        s_ht, s_htc = k.sem("u_hidden_transposed"), k.sem("u_hiddenT_copied")
        s_gt, s_gtc = k.sem("u_give_transposed"), k.sem("u_giveT_copied")
        s_yc = k.sem("u_y_copied")
        s_c, s_cc = k.sem("u_given_back"), k.sem("u_added")
        bank = k.bank
        XB = (7, 3)
        YB = ((5, 6), (3, 4))
        GB = ((5, 6), (3, 4))
        WB = (0, 7)

        def both(eng, turn, last=None):
            def run(lo, hi):
                turn(lo, lo == 0, False)
                with eng.Fori(lo + 1, hi) as n:
                    turn(n, False, True)
                if last:
                    last(hi)
            run(0, NEXP // 2)
            with eng.If(eng.value_load(k.expert[0:1, N_BLK:N_BLK + 1], min_val=0, max_val=N_OVER) > 0):
                run(NEXP // 2, N_BLK // 2)

        with nc.Block() as block:
            @block.sync
            def _(sp):
                def turn(n, fresh, before):
                    for b in range(2):
                        e = sp.value_load(k.expert[0:1, bass.ds(2 * n + b, 1)], min_val=0, max_val=NEXP - 1)
                        g_v, u_v, d_v = (v[0, bass.ds(e, 1)].rearrange("o (k p) n -> p (o k) n", p=P)
                                         for v in (A["w_gate"], A["w_up"], A["w_down"]))
                        for i in range(2):
                            if not (fresh and b == 0):
                                sp.wait_ge((s_half, s_gu)[i], 2 * n + b)
                            sp.dma_start(wg[i][:, :, :], g_v[:, i * CK:(i + 1) * CK, :]).then_inc(s_w[2 * i], 16)
                            sp.dma_start(wu[i][:, :, :], u_v[:, i * CK:(i + 1) * CK, :]).then_inc(s_w[2 * i + 1], 16)
                        for i in range(2):
                            if not (fresh and b == 0):
                                sp.wait_ge((s_yh, s_y)[i], 2 * n + b)
                            sp.dma_start(wd[i][:, :, :], d_v[:, 2 * i:2 * i + 2, :]).then_inc(s_w[4 + i], 16)
                both(sp, turn)

            @block.tensor
            def _(pe):
                def give_back(n):
                    pe.wait_ge(s_yc, 4 * n + 4)
                    for s in range(8):
                        if s >= 2:
                            pe.wait_ge(s_cc, 16 * n + 2 * (s - 1))
                        for b in range(2):
                            for dh in range(2):
                                rows = slice(64 * dh, 64 * dh + 64)
                                ins = pe.matmul(bank[GB[s % 2][dh]][:, 0:NT], y[rows, b, s * P:(s + 1) * P],
                                                giveT[rows, b, :], start=(b == 0), stop=(b == 1))
                        ins.then_inc(s_c, 1)

                def pick(m, fresh):
                    pe.wait_ge(s_sel, m + 1)
                    if not fresh:
                        pe.wait_ge(s_gtc, 2 * m)
                    for q in range(4):
                        if q >= 2:
                            pe.wait_ge(s_xc, 4 * m + q - 1)
                        for j in range(4):
                            t = 4 * q + j
                            for i, (_, r) in enumerate(ROWS):
                                ins = pe.matmul(bank[XB[q % 2]][:, j * P:(j + 1) * P], k.h2rows[0:r, i, t * P:(t + 1) * P],
                                                sel[0:r, i, :, :].rearrange("p b s -> p (b s)"), start=(i == 0),
                                                stop=(i == NTT - 1))
                        ins.then_inc(s_x, 1)

                def gate_up(n, b):
                    for t in range(KT):
                        i = t // CK
                        if b == 0 and t % 4 == 0:
                            pe.wait_ge(s_xc, 4 * n + t // 4 + 1)
                        if t % CK == 0:
                            for w in range(2):
                                pe.wait_ge(s_w[2 * i + w], 16 * (2 * n + b + 1))
                        for w, col in ((wg, 0), (wu, 256)):
                            for half in range(2):
                                ins = pe.matmul(bank[b][64 * half:64 * half + 64, col:col + 256],
                                                x[:, t, b * 64:b * 64 + 64],
                                                w[i][:, t % CK, half * 256:half * 256 + 256],
                                                start=(t == 0 and w is wg), stop=(t == KT - 1 and w is wu))
                        if t == CK - 1:
                            ins.then_inc(s_half, 1)
                        if t == KT - 1:
                            ins.then_inc(s_gu, 1)

                def turn_hidden(n, b):
                    pe.wait_ge(s_h, 2 * n + b + 1)
                    for cc in range(2):
                        ins = pe.transpose(bank[2][:, (2 * b + cc) * P:(2 * b + cc + 1) * P], h[:, b, cc * P:(cc + 1) * P],
                                           k.ident[:, :])
                    ins.then_inc(s_ht, 1)

                def down(n, b):
                    pe.wait_ge(s_htc, 2 * n + b + 1)
                    for f in range(4):
                        half, cc = divmod(f, 2)
                        if cc == 0:
                            pe.wait_ge(s_w[4 + half], 16 * (2 * n + b + 1))
                        for j in range(2):
                            for dh in range(2):
                                at = dh * (D // 2) + j * 512
                                ins = pe.matmul(bank[YB[b][j]][64 * dh:64 * dh + 64, :],
                                                hT[:, b, cc, half * 64:half * 64 + 64], wd[half][:, cc, at:at + 512],
                                                start=(f == 0), stop=(f == 3))
                        if f == 1:
                            ins.then_inc(s_yh, 1)
                    ins.then_inc(s_y, 1)

                def turn(n, fresh, before):
                    if not fresh:
                        pe.wait_ge(s_gtc, 2 * n)
                    gate_up(n, 0)
                    if before:
                        give_back(n - 1)
                    turn_hidden(n, 0)
                    for b in range(2):
                        for i, (at, r) in enumerate(ROWS):
                            ins = pe.transpose(bank[WB[b]][:, at:at + r], give[0:r, i, b, :, :].rearrange("p a s -> p (a s)"),
                                               k.ident[0:r, 0:r])
                        ins.then_inc(s_gt, 1)
                    if not fresh:
                        pe.wait_ge(s_cc, 16 * n)
                    down(n, 0)
                    gate_up(n, 1)
                    pick(n + 1, False)
                    turn_hidden(n, 1)
                    pe.wait_ge(s_xc, 4 * n + 8)
                    down(n, 1)
                pick(0, True)
                both(pe, turn, lambda pairs: give_back(pairs - 1))

            @block.scalar
            def _(act):
                def picked(m):
                    for q in range(4):
                        act.wait_ge(s_x, 4 * m + q + 1)
                        act.copy(x[:, 4 * q:4 * q + 4, :], bank[XB[q % 2]][:, :].rearrange("p (a s) -> p a s", a=4))\
                           .then_inc(s_xc, 1)

                def turn(n, fresh, before):
                    for b in range(2):
                        act.wait_ge(s_gu, 2 * n + b + 1)
                        if not fresh:
                            act.wait_ge(s_ht, 2 * n - 1 + b)
                        act.activation(h[:, b, :], bank[b][:, 0:256], ACT.Silu).then_inc(s_silu, 1)
                        if b == 1:
                            picked(n + 1)
                        elif not fresh:
                            act.wait_ge(s_c, 8 * n)
                        if b == 0:
                            for w in range(2):
                                act.wait_ge(s_gt, 2 * n + w + 1)
                                act.copy(giveT[:, w, :], bank[WB[w]][:, 0:NT]).then_inc(s_gtc, 1)
                        act.wait_ge(s_y, 2 * n + b + 1)
                        for j in range(2):
                            act.copy(y[:, b, j * 512:(j + 1) * 512], bank[YB[b][j]][:, :]).then_inc(s_yc, 1)
                picked(0)
                both(act, turn)

            @block.vector
            def _(dve):
                def select(n):
                    for b in range(2):
                        col = 2 * n + b
                        for i, (_, r) in enumerate(ROWS):
                            slot = k.slot[0:r, i, bass.ds(col, 1)]
                            wt = k.weight[0:r, i, bass.ds(col, 1)]
                            dve.tensor_scalar(sel[0:r, i, b, :], k.slots[0:r, :], slot, None, ALU.is_equal)
                            for d in range(2):
                                ins = dve.tensor_scalar(give[0:r, i, b, d, :], k.slots[0:r, :], slot, wt, ALU.is_equal,
                                                        ALU.mult)
                    ins.then_inc(s_sel, 1)

                def add(n):
                    for s in range(8):
                        dve.wait_ge(s_c, 8 * n + s + 1)
                        for dh in range(2):
                            a = k.acc[:, 8 * dh + s, :]
                            dve.tensor_tensor(a, a, bank[GB[s % 2][dh]][:, 0:NT], ALU.add).then_inc(s_cc, 1)

                def turn(n, fresh, before):
                    for b in range(2):
                        dve.wait_ge(s_silu, 2 * n + b + 1)
                        dve.tensor_tensor(h[:, b, :], h[:, b, :], bank[b][:, 256:512], ALU.mult).then_inc(s_h, 1)
                        if b == 0 and before:
                            add(n - 1)
                        dve.wait_ge(s_ht, 2 * n + b + 1)
                        if not fresh:
                            dve.wait_ge(s_y, 2 * n - 1 + b)
                        dve.tensor_copy(hT[:, b, :, :], bank[2][:, b * 256:(b + 1) * 256].rearrange("p (a s) -> p a s", a=2))\
                           .then_inc(s_htc, 1)
                        if b == 0:
                            dve.wait_ge(s_gt, 2 * n + 2)
                            select(n + 1)
                select(0)
                both(dve, turn, lambda pairs: add(pairs - 1))


def phase_final(k, A):
    nc = k.nc
    with ExitStack() as c:
        sb = lambda name, shape, dt=F32: k.sb(name, shape, dt, c)
        sq, part = sb("f_squares", [P, KT, NT]), sb("f_gated", [P, 2, NS])
        rstd, sd = sb("f_rstd", [P, NT]), sb("f_root", [P, NT])
        rows = sb("f_rows", [P, NTT, D])
        s_q, s_s, s_sd, s_n = k.sem("f_squared"), k.sem("f_summed"), k.sem("f_rooted"), k.sem("f_normed")
        s_t, s_o = k.sem("f_transposed"), k.sem("f_out")
        s_r = [k.sem("f_rows_act"), k.sem("f_rows_dve")]
        with nc.Block() as block:
            def copies(eng, copy, parity):
                for n in range(parity, 4 * NTT, 2):
                    i, q = divmod(n, 4)
                    r = ROWS[i][1]
                    eng.wait_ge(s_t, n + 1)
                    copy(rows[0:r, i, q * 512:(q + 1) * 512], k.bank[1 + n % 4][0:r, :]).then_inc(s_r[parity], 1)

            @block.vector
            def _(dve):
                step = k.steps.chain(dve)
                for m in range(KT):
                    step(add_gated(k, dve, step, m, k.acc[:, m, 0:TP], k.acc[:, m, TP:NT], 80, part[:, m % 2, :]))
                    dve.tensor_tensor(sq[:, m, :], k.xT[:, m, :], k.xT[:, m, :], ALU.mult).then_inc(s_q, 1)
                dve.wait_ge(s_sd, 1)
                step(dve.reciprocal(rstd[:, :], sd[:, :]))
                for m in range(KT):
                    dve.scalar_tensor_tensor(out=k.acc[:, m, :], in0=k.xT[:, m, :], scalar=k.par[:, C_NORMF + m:C_NORMF + m + 1],
                                             in1=rstd[:, :], op0=ALU.mult, op1=ALU.mult).then_inc(s_n, 1)
                copies(dve, dve.tensor_copy, 1)

            @block.tensor
            def _(pe):
                for t in range(KT):
                    pe.wait_ge(s_q, t + 1)
                    ins = pe.matmul(k.bank[0][:, 0:NT], k.ones[:, :], sq[:, t, :], start=(t == 0), stop=(t == KT - 1))
                ins.then_inc(s_s, 1)
                for n in range(4 * NTT):
                    i, q = divmod(n, 4)
                    at, r = ROWS[i]
                    if n < 4:
                        pe.wait_ge(s_n, 4 * (n + 1))
                    else:
                        pe.wait_ge(s_r[n % 2], n // 2 - 1)
                    for j in range(4):
                        ins = pe.transpose(k.bank[1 + n % 4][0:r, j * P:(j + 1) * P], k.acc[:, 4 * q + j, at:at + r],
                                           k.ident[:, :])
                    ins.then_inc(s_t, 1)

            @block.scalar
            def _(act):
                act.wait_ge(s_s, 1)
                act.activation(sd[:, :], k.bank[0][:, 0:NT], ACT.Sqrt, bias=k.eps[:, 0:1], scale=1.0 / D)\
                   .then_inc(s_sd, 1)
                copies(act, act.copy, 0)

            @block.sync
            def _(sp):
                out = (A["y_prompt"][0, 0:P, :], A["y_prompt"][0, P:TP, :], A["y_sample"].rearrange("b t d -> (b t) d"))
                for i, (_, r) in enumerate(ROWS):
                    for p in range(2):
                        sp.wait_ge(s_r[p], 2 * (i + 1))
                    sp.dma_start(out[i], rows[0:r, i, :]).then_inc(s_o, 16)
                sp.wait_ge(s_o, 16 * NTT)


def phase_clear(k):
    s = k.sem("acc_cleared")
    with k.nc.Block() as block:
        @block.gpsimd
        def _(pool):
            pool.memset(k.acc[:, :, :], 0.0).then_inc(s, 1)
            pool.wait_ge(s, 1)


def step_kernel(nc, A):
    with ExitStack() as ctx:
        k = persistent(nc, ctx)
        k.kc_dram = nc.dram_tensor("kc_scratch", [P, NB, 2 * NCS], F32, kind="Internal")
        k.vc_dram = nc.dram_tensor("vc_scratch", [NCS, NB, KVW], F32, kind="Internal")
        phase_start(k, A)
        k.bonus, k.y = k.mixT[:, RT:KT, :], k.mixT[:, 0:RT, :]
        with ExitStack() as mid:
            k.pT = k.sb("pT", [P, RKV_TILE, NX], F32, mid)
            k.gates = k.sb("gates", [P, len(ROWS), 24], F32, mid)
            k.sgates = k.sb("sample_gates", [NS, NB, 3], F32, mid)
            k.gate_dram = nc.dram_tensor("gate_scratch", [NS, 24], F32, kind="Internal")
            rw = mid.enter_context(ExitStack())
            k.rkvT = k.sb("rkvT", [P, 3 * RT, NX], F32, rw)
            with ExitStack() as hh:
                k.hT = hh.enter_context(nc.sbuf_tensor("sb_hT", [P, KT, NX], F32, side="right"))
                phase_norm1(k, A)
                phase_in(k, A)
                k.dec, k.a, k.g = (k.sb(n, [P, RT, NT], F32, rw) for n in ("dec", "a_rate", "g_gate"))
                phase_lora(k, A)
            k.kk = k.sb("kk", [P, RT, NT], F32, rw)
            phase_rkv(k, A)
            phase_scan(k, A)
            phase_groupnorm(k, A)
            rw.close()
            with ExitStack() as own:
                k.kcTp, k.vcp = k.sb("kcT_prompt", [P, 2 * NCP], F32, own), k.sb("vc_prompt", [NCP, KVW], F32, own)
                k.kvrows = k.sb("kvrows", [P, len(ROWS), 3 * ROW], F32, own)
                k.zero_rows = k.sb("zero_rows", [P, ROW], F32, own)
                k.cp_w1, k.cp_w2 = k.sb("cp_w1", [P, 2, CB, P], F32, own), k.sb("cp_w2", [P, 2, P], F32, own)
                phase_rows(k, A)
                phase_compress_prompt(k, A)
                phase_attend_prompt(k, A)
            phase_attend_samples(k, A)
        phase_out(k, A)
        k.h2rows = k.sb("h2rows", [P, NTT, D])
        k.slot, k.weight = k.sb("slot", [P, NTT, N_BLK + 2]), k.sb("weight", [P, NTT, N_BLK + 2])
        k.slots, k.expert = k.sb("slots", [P, SLOTS]), k.sb("expert", [1, N_BLK + 1], I32)
        with ExitStack() as c:
            k.h2T = k.sb("h2T", [P, KT, NT], F32, c)
            norm_block(k, "g", k.xT, k.h2T, C_NORM2, 48, 64)
            phase_route(k, A)
        k.acc = k.mixT
        phase_clear(k)
        phase_moe(k, A)
        phase_final(k, A)


_INS = (
    "x_prompt", "x_sample", "c_prompt", "c_sample", "cache_cmp_kv", "cache_slc_kv", "page_table",
    "state_win_kv", "state_wkv", "state_shift", "w_ada", "b_ada", "norm1", "w_in", "cmp_k_w1", "cmp_k_pe",
    "cmp_k_w2", "cmp_v_w1", "cmp_v_pe", "cmp_v_w2", "mu_rkv", "mu_wag", "decay_w0", "decay_w1", "decay_w2",
    "iclr_a0", "iclr_a1", "iclr_a2", "gate_g1", "gate_g2", "k_k", "k_a", "r_k", "ln_x_w", "ln_x_b", "w_out",
    "norm2", "w_router_group", "b_router_group", "w_router_expert", "b_router_expert", "w_gate", "w_up",
    "w_down", "norm_f",
)
_OUTS = (
    ("y_prompt", (1, 256, 2048)),
    ("y_sample", (8, 4, 2048)),
    ("cmp_kv_prompt", (1, 1, 256, 2, 2, 128)),
    ("cmp_kv_sample", (1, 8, 4, 2, 2, 128)),
    ("slc_kv_prompt", (1, 1, 256, 2, 2, 128)),
    ("slc_kv_sample", (1, 8, 4, 2, 2, 128)),
    ("win_kv_prompt", (1, 1, 512, 2, 2, 128)),
    ("win_kv_sample", (1, 8, 512, 2, 2, 128)),
    ("wkv_prompt", (1, 1, 16, 64, 64)),
    ("wkv_sample", (1, 8, 16, 64, 64)),
    ("shift_prompt", (1, 1, 2048)),
    ("shift_sample", (1, 8, 2048)),
)


def kernel(**inputs):
    import numpy as _np
    import concourse.bacc as _bacc
    from concourse import mybir as _mybir
    from concourse.bass_utils import run_bass_kernel_spmd as _run

    nc = _bacc.Bacc("TRN2", target_bir_lowering=False, num_devices=1)
    arrays, args = {}, {}
    for name in _INS:
        a = _np.ascontiguousarray(inputs[name])
        arrays[f"in_{name}_dram"] = a
        args[name] = nc.dram_tensor(f"in_{name}_dram", a.shape, _mybir.dt.from_np(a.dtype), kind="ExternalInput").ap()
    for name, shape in _OUTS:
        args[name] = nc.dram_tensor(f"out_{name}_dram", shape, _mybir.dt.float32, kind="ExternalOutput").ap()
    step_kernel(nc, args)
    r = _run(nc, [arrays], core_ids=[0])
    return tuple(r.results[0][f"out_{name}_dram"] for name, _ in _OUTS)
```

```python
from contextlib import ExitStack

import concourse.bass as bass
from concourse import mybir

F32 = mybir.dt.float32
I32 = mybir.dt.int32
ALU = mybir.AluOpType
ACT = mybir.ActivationFunctionType
AX = mybir.AxisListType

P = 128
D = 2048
KT = D // P
TP = 256
NB = 8
TS = 4
NS = NB * TS
NT = TP + NS
NX = NT + NB
ROWS = ((0, 128), (128, 128), (256, NS))
IN_W = 5656
IN_TILES = 44
GATE_OFF = IN_TILES * P
HEADS, GROUPS, HPG = 8, 2, 4
RKV_TILE = 20
RT = 8
NC = 1 + NB
EPS = 1e-6
NEG = -1.0e30
SCALE = 128.0 ** -0.5

(C_NORM1, C_NORM2, C_MUWAG, C_MURKV, C_W0, C_A0, C_KK, C_KA, C_RK, C_LNW, C_LNB, C_NORMF, C_BADA) = (
    0, 16, 32, 80, 104, 112, 120, 128, 136, 144, 152, 160, 176)
N_PAR = C_BADA + 96


class Step:
    pass


class Steps:

    def __init__(self, sem):
        self.sem, self.last = sem, None

    def chain(self, eng):
        self.last = Chain(eng, self.sem, self.last.base + self.last.n if self.last else 0)
        return self.last


class Chain:

    def __init__(self, eng, sem, base=0):
        self.eng, self.sem, self.base, self.n = eng, sem, base, 0

    def __call__(self, ins):
        ins.then_inc(self.sem, 1)
        self.n += 1
        self.eng.wait_ge(self.sem, self.base + self.n)

    def enter(self, i, per):
        assert self.n == 0
        self.start, self.per = self.base, per
        self.base = self.start + i * per

    def leave(self, count):
        assert self.n == self.per, self.n
        self.base, self.n = self.start + count * self.per, 0

    def settle(self):
        self.base, self.n = self.base + self.n, 0


def persistent(nc, ctx):
    k = Step()
    k.nc = nc
    k.sb = lambda name, shape, dt=F32, c=ctx: c.enter_context(nc.sbuf_tensor("sb_" + name, shape, dt))
    k.sem = lambda name: ctx.enter_context(nc.semaphore(name))
    k.bank = [ctx.enter_context(nc.psum_tensor(f"bank{i}", [P, 512], F32)) for i in range(8)]
    k.steps = Steps(k.sem("dve_step"))
    k.s_norm, k.norms = [k.sem("norm_" + n) for n in ("squared", "summed", "rooted")], 0
    k.ident = k.sb("ident", [P, P])
    k.ones = k.sb("ones", [P, P])
    k.stack = k.sb("stack", [P, 32])
    k.headones = k.sb("headones", [P, P])
    k.par = k.sb("par", [P, N_PAR])
    k.eps = k.sb("eps", [P, 4])
    k.mod = k.sb("mod", [P, 96, NC])
    k.xT = k.sb("xT", [P, KT, NT])
    k.mixT = k.sb("mixT", [P, KT, NT])
    k.peb = k.sb("pe_bias", [P, 2])
    return k


def phase_start(k, A):
    nc = k.nc
    CH = 512
    HK = KT // 2
    RING = 3
    PER = 6 * D // CH // NB
    PG = 4
    with ExitStack() as c:
        sb = lambda name, shape, dt=F32: k.sb(name, shape, dt, c)
        xf, mf = (v[:, :, :].rearrange("p a n -> p (a n)") for v in (k.xT, k.mixT))
        c_rows, c_act = xf[0:NC, 0:D], mf[0:NC, 0:D]
        stage = [xf[:, D + i * P:D + (i + 1) * P] for i in range(3)]
        sil = mf[:, D:D + 4 * NCS].rearrange("p (i n) -> p i n", i=2)
        at = D + 4 * NCS
        cT = mf[:, at:at + KT * 32].rearrange("p (t m) -> p t m", t=KT)
        w = [sb(f"w_ada{i}", [P, HK, CH]) for i in range(RING)]
        mrows = sb("mod_rows", [P, CH])
        w1, w2 = sb("cmp_w1", [P, 2, CB, P]), sb("cmp_w2", [P, 2, P])
        pe_rows, peT = sb("pe_rows", [CB, 2, P]), sb("peT", [P, 2, CB])
        raw = [sb(f"cmp_raw{i}", [P, PG, ROW]) for i in range(N_PAGES // PG)]
        xt = sb("cmp_xT", [P, 4, PAST])
        table = sb("cmp_table", [1, NB * N_PAGES], I32)
        kcT, vc = sb("kcT_made", [P, NB, 2 * NCS]), sb("vc_made", [P, NB, KVW])
        s_const = k.sem("a_const")
        s_par = k.sem("a_par_rows")
        s_c = k.sem("a_c_rows")
        s_w = [k.sem(f"a_w_landed{i}") for i in range(RING)]
        s_silu = k.sem("a_silu")
        s_parT = k.sem("a_par_transposed")
        s_cT = k.sem("a_c_transposed")
        s_ready = k.sem("a_operands_ready")
        s_half = k.sem("a_half_multiplied")
        s_rows = k.sem("a_chunk_copied")
        s_tr = k.sem("a_chunk_transposed")
        s_mod = k.sem("a_chunk_done")
        s_wl, s_tab = k.sem("l_weights"), k.sem("l_table")
        s_raw = [k.sem(f"l_pages{i}") for i in range(len(raw))]
        s_t = k.sem("l_page_transposed")
        s_pc = [k.sem("l_even_page_copied"), k.sem("l_odd_page_copied")]
        s_pre, s_sil, s_out, s_kv = (k.sem(n) for n in ("l_pre", "l_silu", "l_multiplied", "l_done"))
        s_pe0, s_pe1 = k.sem("l_pe_stage"), k.sem("l_pe_copied")

        w_view = A["w_ada"][0].rearrange("(k p) n -> p k n", p=P)
        with nc.Block() as block:
            @block.sync
            def _(sp):
                sp.dma_start(c_rows[0:1, :], A["c_prompt"]).then_inc(s_c, 16)
                sp.dma_start(c_rows[1:NC, :], A["c_sample"]).then_inc(s_c, 16)
                sp.dma_start(table[:, :], A["page_table"].rearrange("b n -> (b n)").rearrange("(o n) -> o n", o=1))\
                    .then_inc(s_tab, 16)
                sp.wait_ge(s_tab, 16)

                def turn(b, first):
                    def ada(i):
                        n = b * 2 * PER + i
                        if not (first and i < RING):
                            sp.wait_ge(s_half, n - RING + 1)
                        hf = i % 2
                        col = (b * PER + i // 2) * CH
                        sp.dma_start(w[i % RING][:, :, :], w_view[:, hf * HK:(hf + 1) * HK, bass.ds(col, CH)])\
                            .then_inc(s_w[i % RING], 16)

                    def pages(r):
                        if not first:
                            sp.wait_ge(s_t, (b - 1) * N_PAGES + PG * (r + 1))
                        for j in range(PG):
                            page = sp.value_load(table[0:1, bass.ds(b * N_PAGES + r * PG + j, 1)], min_val=0,
                                                 max_val=A["cache_cmp_kv"].shape[1] - 1)
                            sp.dma_start(raw[r][:, j, :], A["cache_cmp_kv"][0, bass.ds(page, 1)]
                                         .rearrange("o s kv g d -> (o s) (kv g d)")).then_inc(s_raw[r], 16)
                    ada(0)
                    pages(0)
                    pages(1)
                    ada(1)
                    ada(2)
                    pages(2)
                    pages(3)
                    ada(3)
                    ada(4)
                    ada(5)
                turn(0, True)
                with sp.Fori(1, NB) as b:
                    turn(b, False)
                sp.wait_ge(s_kv, 2 * NB)
                sp.dma_start(k.kc_dram[:, :, :], kcT[:, :, :]).then_inc(s_tab, 16)
                sp.dma_start(k.vc_dram[:, :, :], vc[0:NCS, :, :]).then_inc(s_tab, 16)
                sp.wait_ge(s_tab, 48)

            def copies(eng, copy, parity, b, lo, hi):
                for pg in range(lo + parity, hi, 2):
                    eng.wait_ge(s_t, b * N_PAGES + pg + 1)
                    copy(xt[:, :, pg * PAGE:(pg + 1) * PAGE], k.bank[2 + parity][:, :].rearrange("p (j s) -> p j s", j=4))\
                        .then_inc(s_pc[parity], 1)

            @block.scalar
            def _(act):
                def rows(tile, at, n, src):
                    act.dma_start(tile[at:at + n, :], src).then_inc(s_par, 16)
                r1 = lambda v: v.rearrange("a (r p) -> (a r) p", p=P)
                rows(stage[0], C_NORM1, 16, r1(A["norm1"]))
                rows(stage[0], C_NORM2, 16, r1(A["norm2"]))
                rows(stage[0], C_MUWAG, 48, A["mu_wag"][0].rearrange("a (r p) -> (a r) p", p=P))
                rows(stage[0], C_MURKV, 24, r1(A["mu_rkv"]))
                for col, v in ((C_W0, A["decay_w0"]), (C_A0, A["iclr_a0"]), (C_KK, A["k_k"]), (C_KA, A["k_a"]),
                               (C_RK, A["r_k"].rearrange("a h d -> a (h d)")), (C_LNW, A["ln_x_w"]),
                               (C_LNB, A["ln_x_b"])):
                    rows(stage[1], col - C_W0, 8, r1(v))
                rows(stage[1], C_NORMF - C_W0, 16, A["norm_f"].rearrange("(r p) -> r p", p=P))
                rows(stage[2], 0, 96, r1(A["b_ada"]))
                for i, (a, b2, pe_) in enumerate(((A["cmp_k_w1"], A["cmp_k_w2"], A["cmp_k_pe"]),
                                                  (A["cmp_v_w1"], A["cmp_v_w2"], A["cmp_v_pe"]))):
                    act.dma_start(pe_rows[:, i, :], pe_[0]).then_inc(s_wl, 16)
                    act.dma_start(w1[:, i, :, :], a[0].rearrange("s d e -> d s e")).then_inc(s_wl, 16)
                    act.dma_start(w2[:, i, :], b2[0]).then_inc(s_wl, 16)
                act.wait_ge(s_c, 32)
                act.activation(c_act[:, :], c_rows[:, :], ACT.Silu).then_inc(s_silu, 1)
                act.wait_ge(s_pe1, 2)
                with act.Fori(0, NB) as b:
                    copies(act, act.copy, 0, b, 0, N_PAGES)
                    for i in range(2):
                        act.wait_ge(s_pre, 2 * b + 1 + i)
                        act.activation(sil[:, i, :], k.bank[4 + i][:, 0:2 * NCS], ACT.Silu, bias=k.peb[:, i:i + 1])\
                            .then_inc(s_sil, 1)

            @block.gpsimd
            def _(pool):
                pool.memset(k.ident[:, :], 0.0).then_inc(s_const, 1)
                pool.memset(k.ones[:, :], 1.0).then_inc(s_const, 1)
                pool.memset(k.headones[:, :], 1.0).then_inc(s_const, 1)
                pool.memset(k.eps[:, 0:1], EPS).then_inc(s_const, 1)
                pool.memset(k.eps[:, 1:2], 64e-5).then_inc(s_const, 1)
                pool.memset(k.eps[:, 2:4], 0.0).then_inc(s_const, 1)
                pool.memset(cT[:, :, :], 0.0).then_inc(s_const, 1)
                pool.wait_ge(s_const, 7)
                pool.affine_select(out=k.ident[:, :], in_=k.ident[:, :], compare_op=ALU.not_equal, fill=1.0,
                                   base=0, pattern=[[-1, P]], channel_multiplier=1).then_inc(s_const, 1)
                pool.affine_select(out=k.headones[:, 0:64], in_=k.headones[:, 0:64], compare_op=ALU.is_ge, fill=0.0,
                                   base=63, pattern=[[0, 64]], channel_multiplier=-1).then_inc(s_const, 1)
                pool.affine_select(out=k.headones[:, 64:128], in_=k.headones[:, 64:128], compare_op=ALU.is_ge,
                                   fill=0.0, base=-64, pattern=[[0, 64]], channel_multiplier=1).then_inc(s_const, 1)

            @block.tensor
            def _(pe):
                pe.wait_ge(s_const, 10)
                pe.wait_ge(s_par, 16 * 13)
                pe.transpose(k.bank[0][:, 0:104], stage[0][0:104, :], k.ident[0:104, 0:104])
                pe.transpose(k.bank[0][:, 104:176], stage[1][0:72, :], k.ident[0:72, 0:72])
                pe.transpose(k.bank[0][:, 176:272], stage[2][0:96, :], k.ident[0:96, 0:96]).then_inc(s_parT, 1)
                pe.wait_ge(s_silu, 1)
                for t in range(KT):
                    ins = pe.transpose(k.bank[1][:, t * NC:(t + 1) * NC], c_act[:, t * P:(t + 1) * P],
                                       k.ident[0:NC, 0:NC])
                ins.then_inc(s_cT, 1)
                pe.wait_ge(s_wl, 16 * 6)
                for i in range(2):
                    ins = pe.transpose(k.bank[6][:, i * CB:(i + 1) * CB], pe_rows[:, i, :], k.ident[0:CB, 0:CB])
                ins.then_inc(s_pe0, 1)
                pe.wait_ge(s_pe1, 1)
                for i in range(2):
                    for s in range(CB):
                        ins = pe.matmul(k.bank[7][:, i:i + 1], w1[:, i, s, :], peT[:, i, s:s + 1], start=(s == 0),
                                        stop=(s == CB - 1))
                ins.then_inc(s_pe0, 1)
                pe.wait_ge(s_ready, 3)
                pe.wait_ge(s_pe1, 2)

                def chunk(b, r):
                    for hf in range(2):
                        i = 2 * r + hf
                        pe.wait_ge(s_w[i % RING], (b * 2 + i // RING + 1) * 16)
                        for t in range(HK):
                            j = t % 4
                            ins = pe.matmul(k.bank[0][32 * j:32 * j + 32, :], cT[:, hf * HK + t, :], w[i % RING][:, t, :],
                                            start=(hf == 0 and t < 4), stop=(hf == 1 and t >= HK - 4))
                        ins.then_inc(s_half, 1)

                def turned(b, r):
                    pe.wait_ge(s_rows, b * PER + r + 1)
                    for j in range(4):
                        ins = pe.matmul(k.bank[1][:, 32 * j:32 * j + 32], mrows[:, j * P:(j + 1) * P], k.stack[:, :],
                                        start=True, stop=True)
                    ins.then_inc(s_tr, 1)

                def pages(b, lo, hi):
                    for pg in range(lo, hi):
                        if pg % PG == 0:
                            pe.wait_ge(s_raw[pg // PG], (b + 1) * 16 * PG)
                        if pg >= 2:
                            pe.wait_ge(s_pc[pg % 2], b * (N_PAGES // 2) + pg // 2)
                        for j in range(4):
                            ins = pe.transpose(k.bank[2 + pg % 2][:, j * P:(j + 1) * P],
                                               raw[pg // PG][:, pg % PG, j * P:(j + 1) * P], k.ident[:, :])
                        ins.then_inc(s_t, 1)

                def turn(b, first, last):
                    chunk(b, 0)
                    pages(b, 3, 8)
                    turned(b, 0)
                    chunk(b, 1)
                    pages(b, 8, 12)
                    turned(b, 1)
                    pages(b, 12, N_PAGES)
                    for i in range(2):
                        pe.wait_ge(s_pc[i], (b + 1) * (N_PAGES // 2))
                    if not first:
                        pe.wait_ge(s_kv, 2 * b)
                    past = lambda i, s: xt[:, 2 * i:2 * i + 2, s:s + CS * (NCS - 1) + 1:CS]
                    compress_hidden(k, pe, NCS, w1, past, s_pre, (0,))
                    chunk(b, 2)
                    compress_hidden(k, pe, NCS, w1, past, s_pre, (1,))
                    turned(b, 2)
                    if not last:
                        pages(b + 1, 0, 3)
                    pe.wait_ge(s_sil, 2 * b + 2)
                    compress_out(k, pe, NCS, w2, sil, s_out)
                pages(0, 0, 3)
                turn(0, True, False)
                with pe.Fori(1, NB - 1) as b:
                    turn(b, False, False)
                turn(NB - 1, False, True)

            @block.vector
            def _(dve):
                dve.wait_ge(s_const, 10)
                dve.wait_ge(s_parT, 1)
                dve.tensor_copy(k.par[:, :], k.bank[0][:, 0:N_PAR]).then_inc(s_ready, 1)
                dve.wait_ge(s_cT, 1)
                dve.tensor_copy(cT[:, :, 0:NC], k.bank[1][:, 0:KT * NC].rearrange("p (t m) -> p t m", m=NC))\
                   .then_inc(s_ready, 1)
                dve.wait_ge(s_pe0, 1)
                dve.tensor_copy(peT[:, :, :], k.bank[6][:, 0:2 * CB].rearrange("p (i s) -> p i s", i=2)).then_inc(s_pe1, 1)
                dve.wait_ge(s_pe0, 2)
                dve.tensor_copy(k.peb[:, :], k.bank[7][:, 0:2]).then_inc(s_pe1, 1)
                dve.wait_ge(s_ready, 2)
                dve.tensor_reduce(k.stack[:, :], k.ident[:, :].rearrange("p (j m) -> p m j", j=4), AX.X, ALU.add).then_inc(s_ready, 1)

                def rows(b, r):
                    dve.wait_ge(s_half, (b * PER + r) * 2 + 2)
                    dve.tensor_copy(mrows[:, :], k.bank[0][:, :]).then_inc(s_rows, 1)

                def done(b, r):
                    n = b * PER + r
                    dve.wait_ge(s_tr, n + 1)
                    bada = k.par[:, bass.ds(C_BADA + 4 * n, 4)].unsqueeze(2).to_broadcast([P, 4, NC])
                    dve.tensor_tensor(k.mod[:, bass.ds(4 * n, 4), :],
                                      k.bank[1][:, 0:P].rearrange("p (j m) -> p j m", m=32)[:, :, 0:NC],
                                      bada, ALU.add).then_inc(s_mod, 1)

                with dve.Fori(0, NB) as b:
                    copies(dve, dve.tensor_copy, 1, b, 0, 2)
                    rows(b, 0)
                    copies(dve, dve.tensor_copy, 1, b, 2, 8)
                    done(b, 0)
                    rows(b, 1)
                    copies(dve, dve.tensor_copy, 1, b, 8, 12)
                    done(b, 1)
                    copies(dve, dve.tensor_copy, 1, b, 12, N_PAGES)
                    rows(b, 2)
                    done(b, 2)
                    dve.wait_ge(s_out, b + 1)
                    dve.tensor_scalar(kcT[:, bass.ds(b, 1), :].rearrange("p o n -> p (o n)"), k.bank[6][:, 0:2 * NCS], 1.0,
                                      None, ALU.mult).then_inc(s_kv, 1)
                    dve.tensor_scalar(vc[0:NCS, bass.ds(b, 1), :].rearrange("p o n -> p (o n)"),
                                      k.bank[7][0:NCS, 0:KVW], 1.0, None, ALU.mult).then_inc(s_kv, 1)


def compress_hidden(k, pe, n, w1, rhs, s_pre, kinds=(0, 1)):
    for i in kinds:
        for s in range(CB):
            ins = pe.matmul(k.bank[4 + i][:, 0:2 * n].rearrange("p (g c) -> p g c", g=2), w1[:, i, s, :],
                            rhs(i, s), start=(s == 0), stop=(s == CB - 1))
        ins.then_inc(s_pre, 1)


def compress_out(k, pe, n, w2, sil, s_out):
    pe.matmul(k.bank[6][:, 0:2 * n], w2[:, 0, :], sil[:, 0, 0:2 * n], start=True, stop=True)
    for g in range(2):
        ins = pe.matmul(k.bank[7][0:n, g * P:(g + 1) * P], sil[:, 1, g * n:(g + 1) * n], w2[:, 1, :],
                        start=True, stop=True)
    ins.then_inc(s_out, 1)


def phase_norm1(k, A):
    nc = k.nc
    with ExitStack() as c:
        sb = lambda name, shape, dt=F32: k.sb(name, shape, dt, c)
        rows = [sb("x_rows0", [P, D]), sb("x_rows1", [P, D]), sb("x_rows2", [NS, D])]
        rows.append(k.mixT[0:NB, :, :].rearrange("p a n -> p (a n)")[:, 0:D])
        s_x = [k.sem(f"b_rows_landed{i}") for i in range(4)]
        s_t = k.sem("b_tile_transposed")
        s_c = k.sem("b_tile_copied")
        with nc.Block() as block:
            @block.sync
            def _(sp):
                sp.dma_start(rows[0][:, :], A["x_prompt"][0, 0:128, :]).then_inc(s_x[0], 16)
                sp.dma_start(rows[1][:, :], A["x_prompt"][0, 128:256, :]).then_inc(s_x[1], 16)
                sp.dma_start(rows[2][:, :], A["x_sample"].rearrange("b t d -> (b t) d")).then_inc(s_x[2], 16)
                sp.dma_start(rows[3][:, :], A["state_shift"][0]).then_inc(s_x[3], 16)
                for r in range(2):
                    sp.dma_start(k.w_in[r][:, :, :], A["w_in"][0].rearrange("(k p) n -> p k n", p=P)
                                 [:, :, r * 512:(r + 1) * 512]).then_inc(k.s_w_in[r], 16)

            @block.tensor
            def _(pe):
                for i in range(4):
                    pe.wait_ge(s_x[i], 16)
                for t in range(KT):
                    if t >= 4:
                        pe.wait_ge(s_c, 2 * (t - 3))
                    for i, (at, n) in enumerate(ROWS + ((NT, NB),)):
                        ins = pe.transpose(k.bank[t % 4][:, at:at + n], rows[i][0:n, t * P:(t + 1) * P],
                                           k.ident[0:n, 0:n])
                    ins.then_inc(s_t, 1)

            @block.scalar
            def _(act):
                for t in range(KT):
                    act.wait_ge(s_t, t + 1)
                    act.copy(k.xT[:, t, :], k.bank[t % 4][:, 0:NT]).then_inc(s_c, 1)
                    act.copy(k.hT[:, t, NT:NX], k.bank[t % 4][:, NT:NX]).then_inc(s_c, 1)
    norm_block(k, "b1", k.xT, k.hT, C_NORM1, 0, 16)
    with ExitStack() as c:
        last = k.sb("last_cols", [P, KT, NC], F32, c)
        last_rows = k.sb("last_rows", [NC, D], F32, c)
        s_l, s_t, s_r, s_o = k.sem("b_last_cols"), k.sem("b_last_transposed"), k.sem("b_last_rows"), k.sem("b_last_out")
        with nc.Block() as block:
            @block.vector
            def _(dve):
                dve.tensor_copy(last[:, :, 0:1], k.hT[:, :, TP - 1:TP]).then_inc(s_l, 1)
                dve.tensor_copy(last[:, :, 1:NC], k.hT[:, :, TP + TS - 1:NT:TS]).then_inc(s_l, 1)
                for q in range(4):
                    dve.wait_ge(s_t, q + 1)
                    dve.tensor_copy(last_rows[:, q * 512:(q + 1) * 512], k.bank[q][0:NC, :]).then_inc(s_r, 1)

            @block.tensor
            def _(pe):
                pe.wait_ge(s_l, 2)
                for t in range(KT):
                    ins = pe.transpose(k.bank[t // 4][0:NC, (t % 4) * P:(t % 4 + 1) * P], last[:, t, :], k.ident[:, :])
                    if t % 4 == 3:
                        ins.then_inc(s_t, 1)

            @block.sync
            def _(sp):
                sp.wait_ge(s_r, 4)
                sp.dma_start(A["shift_prompt"][0], last_rows[0:1, :]).then_inc(s_o, 16)
                sp.dma_start(A["shift_sample"][0], last_rows[1:NC, :]).then_inc(s_o, 16)
                sp.wait_ge(s_o, 32)


def norm_block(k, pfx, src, dst, gain_col, shift, scale):
    nc = k.nc
    with ExitStack() as c:
        sb = lambda name, shape: k.sb(pfx + name, shape, F32, c)
        tmp, rstd, sd, g = sb("tmp", [P, KT, NT]), sb("rstd", [P, NT]), sb("sd", [P, NT]), sb("gain", [P, KT, NC])
        s_q, s_s, s_sd = k.s_norm
        before = k.norms
        k.norms += 1
        with nc.Block() as block:
            @block.vector
            def _(dve):
                step = k.steps.chain(dve)
                for t in range(KT):
                    dve.tensor_tensor(tmp[:, t, :], src[:, t, :], src[:, t, :], ALU.mult).then_inc(s_q, 1)
                gain = k.par[:, gain_col:gain_col + KT].unsqueeze(2).to_broadcast([P, KT, NC])
                step(dve.scalar_tensor_tensor(out=g[:, :, :], in0=k.mod[:, scale:scale + KT, :], scalar=1.0, in1=gain,
                                              op0=ALU.add, op1=ALU.mult))
                dve.wait_ge(s_sd, before + 1)
                step(dve.reciprocal(rstd[:, :], sd[:, :]))
                step(dve.tensor_tensor(tmp[:, :, :], src[:, :, 0:NT], rstd[:, :].unsqueeze(1).to_broadcast([P, KT, NT]),
                                       ALU.mult))
                for t in range(KT):
                    dve.tensor_scalar(dst[:, t, 0:TP], tmp[:, t, 0:TP], g[:, t, 0:1], k.mod[:, shift + t, 0:1],
                                      ALU.mult, ALU.add)
                by_t = lambda v: v.unsqueeze(3).to_broadcast([P, KT, NB, TS])
                samples = lambda v: v[:, :, TP:NT].rearrange("p k (b t) -> p k b t", t=TS)
                step(dve.tensor_tensor(samples(tmp), samples(tmp), by_t(g[:, :, 1:NC]), ALU.mult))
                step(dve.tensor_tensor(samples(dst), samples(tmp), by_t(k.mod[:, shift:shift + KT, 1:NC]), ALU.add))

            @block.tensor
            def _(pe):
                for t in range(KT):
                    pe.wait_ge(s_q, before * KT + t + 1)
                    ins = pe.matmul(k.bank[0][:, 0:NT], k.ones[:, :], tmp[:, t, :], start=(t == 0), stop=(t == KT - 1))
                ins.then_inc(s_s, 1)

            @block.scalar
            def _(act):
                act.wait_ge(s_s, before + 1)
                act.activation(sd[:, :], k.bank[0][:, 0:NT], ACT.Sqrt, bias=k.eps[:, 0:1], scale=1.0 / D)\
                   .then_inc(s_sd, 1)


def phase_in(k, A):
    nc = k.nc
    CH, N_CH, RING = 512, IN_TILES * P // 512, 2
    NG = 24
    with ExitStack() as c:
        sb = lambda name, shape, dt=F32: k.sb(name, shape, dt, c)
        w = k.w_in
        wg = sb("w_in_gate", [P, KT, NG])
        s_w = k.s_w_in
        s_wg = k.sem("c_wg_landed")
        s_tile = k.sem("c_tile_multiplied")
        s_copy = [k.sem("c_even_copied"), k.sem("c_odd_copied")]
        s_g = k.sem("c_gates_multiplied")
        s_gc = k.sem("c_gates_done")
        w_view = A["w_in"][0].rearrange("(k p) n -> p k n", p=P)
        FULL = N_CH // RING

        with nc.Block() as block:
            @block.sync
            def _(sp):
                def load(r, n, used):
                    sp.wait_ge(s_tile, used)
                    sp.dma_start(w[r][:, :, :], w_view[:, :, bass.ds(n * CH, CH)]).then_inc(s_w[r], 16)
                sp.dma_start(wg[:, :, :], w_view[:, :, GATE_OFF:IN_W]).then_inc(s_wg, 16)
                with sp.Fori(1, FULL) as it:
                    for r in range(RING):
                        load(r, it * RING + r, (it * RING + r - RING + 1) * 4)
                load(0, FULL * RING, (FULL * RING - RING + 1) * 4)

            @block.tensor
            def _(pe):
                def chunk(r, n, landed, first=False):
                    pe.wait_ge(s_w[r], landed)
                    for m in range(4):
                        if not first:
                            pe.wait_ge(s_copy[m % 2], 2 * n - 1 + m // 2)
                        for t in range(KT):
                            ins = pe.matmul(k.bank[m][:, 0:NX], w[r][:, t, m * P:(m + 1) * P], k.hT[:, t, :],
                                            start=(t == 0), stop=(t == KT - 1))
                        ins.then_inc(s_tile, 1)
                chunk(0, 0, 16, True)
                chunk(1, 1, 16)
                with pe.Fori(1, FULL) as it:
                    for r in range(RING):
                        chunk(r, it * RING + r, (it + 1) * 16)
                chunk(0, FULL * RING, (FULL + 1) * 16)
                pe.wait_ge(s_wg, 16)
                for i, (at, n) in enumerate(ROWS):
                    for t in range(KT):
                        ins = pe.matmul(k.bank[4 + i][0:n, 0:NG], k.hT[:, t, at:at + n], wg[:, t, :],
                                        start=(t == 0), stop=(t == KT - 1))
                    ins.then_inc(s_g, 1)

            def copies(eng, copy, parity):
                def chunk(n, dst, first):
                    for h in range(2):
                        m = 2 * h + parity
                        eng.wait_ge(s_tile, 4 * n + m + 1)
                        copy(dst[:, bass.ds(4 * n + m - first, 1), :].rearrange("p a n -> p (a n)"), k.bank[m][:, 0:NX])\
                            .then_inc(s_copy[parity], 1)
                with eng.Fori(0, RKV_TILE // 4) as n:
                    chunk(n, k.pT, 0)
                with eng.Fori(RKV_TILE // 4, N_CH) as n:
                    chunk(n, k.rkvT, RKV_TILE)

            @block.scalar
            def _(act):
                copies(act, act.copy, 0)
                for i, (at, n) in enumerate(ROWS):
                    act.wait_ge(s_g, i + 1)
                    act.activation(k.gates[0:n, i, :], k.bank[4 + i][0:n, 0:NG], ACT.Sigmoid).then_inc(s_gc, 1)

            @block.vector
            def _(dve):
                copies(dve, lambda out, in_: dve.tensor_scalar(out, in_, 1.0, None, ALU.mult), 1)


HT = 16
CL = 32
N_CHUNK = TP // CL
LW, LA, LG = 64, 64, 128


def shift_differences(dve, step, out, cur, tiles):
    samples = lambda v: v[:, :, TP:NT].rearrange("p k (b t) -> p k b t", t=TS)
    dve.tensor_tensor(out[:, :, 1:TP], cur[:, tiles, 0:TP - 1], cur[:, tiles, 1:TP], ALU.subtract)
    dve.tensor_scalar(out[:, :, 0:1], cur[:, tiles, 0:1], -1.0, None, ALU.mult)
    c = cur[:, tiles, :]
    dve.tensor_tensor(samples(out)[:, :, :, 1:TS], samples(c)[:, :, :, 0:TS - 1], samples(c)[:, :, :, 1:TS], ALU.subtract)
    step(dve.tensor_tensor(out[:, :, TP:NT:TS], c[:, :, NT:NX], c[:, :, TP:NT:TS], ALU.subtract))


def phase_lora(k, A):
    nc = k.nc
    with ExitStack() as c:
        sb = lambda name, shape, dt=F32: k.sb(name, shape, dt, c)
        w1 = [sb("lora_w1", [P, KT, LW]), sb("lora_a1", [P, KT, LA]), sb("lora_g1", [P, KT, LG])]
        w2 = [sb("lora_w2", [LW, RT * P]), sb("lora_a2", [LA, RT * P]), sb("lora_g2", [LG, RT * P])]
        dx = sb("dx", [P, KT, NT])
        XR = 8
        xm = sb("xm", [P, XR, NT])
        low = [sb("low_w", [LW, NT]), sb("low_a", [LA, NT]), sb("low_g", [LG, NT])]
        s_w, s_v, s_x = k.sem("f_lora_weights"), k.sem("f_lora_dve"), k.sem("f_mixed_input")
        s_used, s_act, s_hi, s_out = k.sem("f_tile_used"), k.sem("f_low_activated"), k.sem("f_high"), k.sem("f_high_done")
        dst = [k.dec, k.a, k.g]
        with nc.Block() as block:
            @block.sync
            def _(sp):
                for w, src in ((w1, (A["decay_w1"], A["iclr_a1"], A["gate_g1"])),):
                    for tile, s in zip(w, src):
                        sp.dma_start(tile[:, :, :], s[0].rearrange("(k p) n -> p k n", p=P)).then_inc(s_w, 16)
                for tile, s in zip(w2, (A["decay_w2"], A["iclr_a2"], A["gate_g2"])):
                    sp.dma_start(tile[:, :], s[0]).then_inc(s_w, 16)

            @block.vector
            def _(dve):
                step = Chain(dve, s_v)
                shift_differences(dve, step, dx, k.hT, slice(0, KT))
                for i in range(3):
                    for t in range(KT):
                        m = i * KT + t
                        if m >= XR:
                            dve.wait_ge(s_used, m - XR + 1)
                        mu = k.par[:, C_MUWAG + i * KT + t:C_MUWAG + i * KT + t + 1]
                        dve.scalar_tensor_tensor(out=xm[:, m % XR, :], in0=dx[:, t, :], scalar=mu, in1=k.hT[:, t, 0:NT],
                                                 op0=ALU.mult, op1=ALU.add).then_inc(s_x, 1)

            @block.tensor
            def _(pe):
                pe.wait_ge(s_w, 16 * 6)
                for i in range(3):
                    n = (LW, LA, LG)[i]
                    for t in range(KT):
                        pe.wait_ge(s_x, i * KT + t + 1)
                        ins = pe.matmul(k.bank[i][0:n, 0:NT], w1[i][:, t, :], xm[:, t % XR, :], start=(t == 0),
                                        stop=(t == KT - 1))
                        ins.then_inc(s_used, 1)
                for i in range(3):
                    pe.wait_ge(s_act, i + 1)
                    for t in range(RT):
                        m = i * RT + t
                        if m >= 4:
                            pe.wait_ge(s_out, m - 3)
                        pe.matmul(k.bank[4 + m % 4][:, 0:NT], w2[i][:, t * P:(t + 1) * P], low[i][:, :], start=True,
                                  stop=True).then_inc(s_hi, 1)

            @block.scalar
            def _(act):
                for i, fn in enumerate((ACT.Tanh, ACT.Copy, ACT.Sigmoid)):
                    n = (LW, LA, LG)[i]
                    act.wait_ge(s_used, (i + 1) * KT)
                    act.activation(low[i][:, :], k.bank[i][0:n, 0:NT], fn).then_inc(s_act, 1)
                for m in range(3 * RT):
                    i, t = m // RT, m % RT
                    act.wait_ge(s_hi, m + 1)
                    ps = k.bank[4 + m % 4][:, 0:NT]
                    if i == 2:
                        act.copy(dst[i][:, t, :], ps).then_inc(s_out, 1)
                    else:
                        col = (C_W0, C_A0)[i] + t
                        act.activation(dst[i][:, t, :], ps, ACT.Sigmoid, bias=k.par[:, col:col + 1]).then_inc(s_out, 1)
                act.wait_ge(s_out, 3 * RT)
                act.activation(k.dec[:, :, :], k.dec[:, :, :], ACT.Exp, scale=-0.6065306597126334).then_inc(s_out, 1)


def phase_rkv(k, A):
    nc = k.nc
    r, kx, v = (slice(i * RT, (i + 1) * RT) for i in range(3))
    with ExitStack() as c:
        sb = lambda name, shape, dt=F32: k.sb(name, shape, dt, c)
        d = sb("rkv_diff", [P, 3 * RT, NT])
        t1 = d[:, 0:RT, :]
        t2 = d[:, RT:2 * RT, :]
        one = sb("one_minus_ka", [P, RT])
        s_v, s_q, s_n, s_r = k.sem("g_dve"), k.sem("g_squares"), k.sem("g_head_sums"), k.sem("g_roots")
        with nc.Block() as block:
            @block.vector
            def _(dve):
                step = Chain(dve, s_v)
                shift_differences(dve, step, d, k.rkvT, slice(0, 3 * RT))
                for t in range(3 * RT):
                    mu = k.par[:, C_MURKV + t:C_MURKV + t + 1]
                    cur = k.rkvT[:, t, 0:NT]
                    ins = dve.scalar_tensor_tensor(out=cur, in0=d[:, t, :], scalar=mu, in1=cur, op0=ALU.mult,
                                                   op1=ALU.add)
                step(ins)
                bc = lambda col: k.par[:, col:col + RT].unsqueeze(2).to_broadcast([P, RT, NT])
                R, K, V = (k.rkvT[:, s, 0:NT] for s in (r, kx, v))
                step(dve.tensor_tensor(k.kk[:, :, :], K, bc(C_KK), ALU.mult))
                dve.tensor_tensor(t1, k.kk[:, :, :], k.kk[:, :, :], ALU.mult).then_inc(s_q, 1)
                step(dve.tensor_scalar(one[:, :], k.par[:, C_KA:C_KA + RT], -1.0, 1.0, ALU.mult, ALU.add))
                step(dve.tensor_tensor(t2, k.a[:, :, :], bc(C_KA), ALU.mult))
                step(dve.tensor_tensor(t2, t2, one[:, :].unsqueeze(2).to_broadcast([P, RT, NT]), ALU.add))
                step(dve.tensor_tensor(K, K, t2, ALU.mult))
                for t in range(RT):
                    dve.wait_ge(s_n, t + 1)
                    step(dve.tensor_scalar(t2[:, t, :], k.bank[t % 4][:, 0:NT], 1e-24, None, ALU.max))
                step(dve.tensor_tensor(k.bonus[:, :, :], R, K, ALU.mult))
                dve.tensor_tensor(k.bonus[:, :, :], k.bonus[:, :, :], bc(C_RK), ALU.mult).then_inc(s_q, 1)
                dve.wait_ge(s_r, 1)
                step(dve.reciprocal(t1, t2))
                step(dve.tensor_tensor(k.kk[:, :, :], k.kk[:, :, :], t1, ALU.mult))
                step(dve.tensor_tensor(k.a[:, :, :], k.a[:, :, :], k.kk[:, :, :], ALU.mult))
                for t in range(RT):
                    dve.wait_ge(s_n, RT + t + 1)
                    step(dve.tensor_tensor(k.bonus[:, t, :], k.bank[4 + t % 4][:, 0:NT], V[:, t, :], ALU.mult))

            @block.tensor
            def _(pe):
                BEFORE = 7
                pe.wait_ge(s_q, 1)
                for t in range(RT):
                    if t >= 4:
                        pe.wait_ge(s_v, BEFORE + t - 3)
                    pe.matmul(k.bank[t % 4][:, 0:NT], k.headones[:, :], t1[:, t, :], start=True, stop=True)\
                        .then_inc(s_n, 1)
                pe.wait_ge(s_q, 2)
                for t in range(RT):
                    if t >= 4:
                        pe.wait_ge(s_v, BEFORE + RT + 1 + 3 + t - 3)
                    pe.matmul(k.bank[4 + t % 4][:, 0:NT], k.headones[:, :], k.bonus[:, t, :], start=True, stop=True)\
                        .then_inc(s_n, 1)

            @block.scalar
            def _(act):
                act.wait_ge(s_v, 7 + RT)
                act.activation(t2, t2, ACT.Sqrt).then_inc(s_r, 1)


def phase_scan(k, A):
    nc = k.nc
    with ExitStack() as c:
        sb = lambda name, shape, dt=F32: k.sb(name, shape, dt, c)
        Q = HT // 4
        masks = []
        for name in ("prompt", "sample"):
            m = Step()
            m.up, m.low, m.incl4 = (sb(f"m_{what}_{name}", [P, 4, CL]) for what in ("up", "low", "incl4"))
            m.incl = sb("m_incl_" + name, [P, CL])
            masks.append(m)
        rowb4 = sb("m_row4", [P, 4, NB])
        rowb = sb("m_row", [P, NB])
        colb = sb("m_col", [P, NB, CL])
        d0, d1, pc = sb("decay_in", [P, RT, CL]), sb("decay_first", [P, RT, CL]), sb("decay_prod", [P, RT, CL])
        pinv, pprev = sb("decay_inv", [P, RT, CL]), sb("decay_prev", [P, RT, CL])
        bh, kh, vc = sb("bhat", [P, RT, CL]), sb("khat", [P, RT, CL]), sb("v_chunk", [P, RT, CL])
        lt = sb("LT", [P, Q, P])
        a_ = [sb("pow0", [P, Q, P]), sb("pow1", [P, Q, P])]
        at = [lt, sb("powT1", [P, Q, P])]
        sets = []
        for i in range(2):
            u = Step()
            u.ar = sb(f"ahat_rhat{i}", [P, 2, RT, CL])
            u.mk, u.pt = sb(f"MK{i}", [P, Q, P]), sb(f"invT{i}", [P, Q, P])
            u.rbk, u.rows = sb(f"RBK{i}", [P, Q, 2, CL]), sb(f"bkv_rows{i}", [P, 3, Q, 64])
            u.pend = sb(f"decay_end{i}", [P, RT])
            sets.append(u)
        x, sa = sb("X", [P, Q, 64]), sb("SA", [P, Q, 64])
        st = sb("state", [P, RT, 64])
        s0 = sb("sample_state", [P, RT, NB, 64])
        ahm = sb("ahat_by_sample", [P, RT, NB, CL])
        flat = lambda tile: k.rkvT[:, tile:tile + 7, :].rearrange("p a n -> p (a n)")[:, 0:Q * NB * 64]\
            .rearrange("p (q b i) -> p q b i", q=Q, b=NB)
        sam, vm = flat(0), flat(RT)
        s_m, s_st = k.sem("h_masks"), k.sem("h_states_landed")
        s_pe, s_v, s_o = k.sem("h_pe_stage"), k.sem("h_dve_stage"), k.sem("h_states_written")
        VST = 12
        s_rd = k.sem("h_operands_ready")
        s_fp, s_fv, s_bp, s_bv = (k.sem("h_" + n) for n in ("front_pe", "front_dve", "back_pe", "back_dve"))
        FP, FV, BP, BV = 6, 7, 3, 4
        pend_now = sb("decay_end", [P, RT])
        bank = k.bank

        def head(h):
            pb, rb = 64 * (h % 2), 64 * (h % 2) + 32 * (h // 2 % 2)
            return h // 2, slice(pb, pb + 64), h // 4, slice(rb, rb + 32)

        def pe_products(pe, u):
            g = bank[0][:, :].rearrange("p (q m a t) -> p q m a t", q=Q, m=2, a=2)
            for h in range(HT):
                t, pb, q, rb = head(h)
                pe.matmul(bank[1][rb, P + q * 64:P + (q + 1) * 64], vc[:, t, :], k.ident[:, pb], start=True, stop=True)
            for h in range(HT):
                t, pb, q, rb = head(h)
                pe.matmul(g[rb, q, 0, :, :], bh[pb, t, :], u.ar[pb, :, t, :], start=True, stop=True)
                pe.matmul(g[rb, q, 1, :, :], kh[pb, t, :], u.ar[pb, :, t, :], start=True, stop=True)
                pe.matmul(bank[1][rb, q * CL:(q + 1) * CL], u.ar[pb, 0, t, :], bh[pb, t, :], start=True, stop=True)
            for h in range(HT):
                t, pb, q, rb = head(h)
                for i, src in enumerate((bh, kh)):
                    ins = pe.matmul(bank[2][rb, i * 256 + q * 64:i * 256 + (q + 1) * 64], src[pb, t, :], k.ident[pb, pb],
                                    start=True, stop=True)
            return ins

        def pe_x(pe, u, sample):
            for q in range(Q):
                pe.matmul(bank[6][:, q * 64:(q + 1) * 64], u.mk[:, q, :], u.rows[:, 2, q, :], start=True, stop=False)
                for h in range(4 * q, 4 * q + 4):
                    t, pb, _, rb = head(h)
                    out = bank[6][rb, q * 64:(q + 1) * 64]
                    if sample:
                        for b in range(NB):
                            ins = pe.matmul(out, ahm[pb, t, b, :], s0[pb, t, b, :], start=False,
                                            stop=(b == NB - 1))
                    else:
                        ins = pe.matmul(out, u.ar[pb, 0, t, :], st[pb, t, :], start=False, stop=True)
            return ins

        def pe_level(pe, u, level):
            dst = level % 2
            for q in range(Q):
                cols = slice(q * P, (q + 1) * P)
                if level < 4:
                    ins = pe.matmul(bank[3][:, cols], at[dst][:, q, :], a_[dst][:, q, :], start=True, stop=True)
                    if level < 3:
                        ins = pe.matmul(bank[4][:, cols], a_[dst][:, q, :], at[dst][:, q, :], start=True, stop=True)
                if level > 0:
                    ins = pe.matmul(bank[5][:, cols], a_[dst][:, q, :], u.pt[:, q, :], start=True, stop=True)
            return ins

        def pe_sa(pe, u):
            for q in range(Q):
                ins = pe.matmul(bank[6][:, 256 + q * 64:256 + (q + 1) * 64], u.pt[:, q, :], x[:, q, :], start=True,
                                stop=True)
            return ins

        def pe_y(pe, u, sample, banks):
            for h in range(HT):
                t, pb, q, rb = head(h)
                y_bank, at_ = bank[banks[t % 2]], t // 2 * CL
                out = y_bank[pb, at_:at_ + CL]
                pe.matmul(out, sa[rb, q, :], u.rbk[rb, q, 0, :], start=True, stop=False)
                pe.matmul(out, u.rows[rb, 2, q, :], u.rbk[rb, q, 1, :], start=False, stop=sample)
                if sample:
                    for b in range(NB):
                        ins = pe.matmul(y_bank[pb, at_ + b * TS:at_ + (b + 1) * TS], s0[pb, t, b, :],
                                        u.ar[pb, 1, t, b * TS:(b + 1) * TS], start=False, stop=True,
                                        skip_group_check=True)
                else:
                    ins = pe.matmul(out, st[pb, t, :], u.ar[pb, 1, t, :], start=False, stop=True)
            return ins

        def pe_state(pe, u, heads):
            for h in heads:
                t, pb, q, rb = head(h)
                at_ = P + t // 2 * 64
                out = bank[6 + t % 2][pb, at_:at_ + 64]
                pe.matmul(out, u.rows[rb, 0, q, :], sa[rb, q, :], start=True, stop=False)
                ins = pe.matmul(out, u.rows[rb, 1, q, :], u.rows[rb, 2, q, :], start=False, stop=True)
            return ins

        def pe_sample_chunk(pe, u):
            v = lambda i: pe.wait_ge(s_v, i)
            v(1)
            pe_products(pe, u).then_inc(s_pe, 1)
            v(3)
            pe_x(pe, u, True).then_inc(s_pe, 1)
            for level in range(5):
                if level > 0:
                    v(4 + level)
                pe_level(pe, u, level).then_inc(s_pe, 1)
            v(9)
            pe_sa(pe, u).then_inc(s_pe, 1)
            v(10)
            pe_y(pe, u, True, (3, 4)).then_inc(s_pe, 1)

        def dve_hats(dve, inner, u, cols, first_step):
            K, V = (k.rkvT[:, i * RT:(i + 1) * RT, cols] for i in (1, 2))
            seg = slice(0, CL, first_step)
            inner(dve.tensor_scalar(d0[:, :, :], k.dec[:, :, cols], 1.0, None, ALU.mult))
            dve.tensor_scalar(d1[:, :, seg], k.dec[:, :, cols][:, :, seg], 1.0, None, ALU.mult)
            inner(dve.memset(d0[:, :, seg], 0.0))
            fl = lambda v: v[:, :, :].rearrange("p k t -> p (k t)")
            inner(dve.tensor_tensor_scan(fl(pc), fl(d0), fl(d1), 0.0, ALU.mult, ALU.add))
            inner(dve.tensor_copy(fl(pprev)[:, 1:RT * CL], fl(pc)[:, 0:RT * CL - 1]))
            inner(dve.memset(pprev[:, :, seg], 1.0))
            inner(dve.reciprocal(pinv[:, :, :], pc[:, :, :]))
            dve.tensor_copy(u.pend[:, :], pc[:, :, CL - 1:CL].rearrange("p k o -> p (k o)"))
            dve.tensor_tensor(bh[:, :, :], k.a[:, :, cols], pinv[:, :, :], ALU.mult)
            dve.tensor_tensor(kh[:, :, :], K, pinv[:, :, :], ALU.mult)
            return dve.tensor_scalar(vc[:, :, :], V, 1.0, None, ALU.mult)

        def dve_ar(dve, u, cols):
            dve.scalar_tensor_tensor(out=u.ar[:, 0, :, :], in0=k.kk[:, :, cols], scalar=-1.0, in1=pprev[:, :, :],
                                     op0=ALU.mult, op1=ALU.mult)
            return dve.tensor_tensor(u.ar[:, 1, :, :], k.rkvT[:, 0:RT, cols], pc[:, :, :], ALU.mult)

        def dve_masks(dve, step, u, mask):
            g = bank[0][:, :].rearrange("p (q m a t) -> p q m a t", q=Q, m=2, a=2)
            spread = lambda v: v.unsqueeze(2).to_broadcast([P, Q, 4, CL])
            over_q = lambda m: m[:, :, :].unsqueeze(1).to_broadcast([P, Q, 4, CL])
            out4 = lambda v: v[:, :, :].rearrange("p q (h t) -> p q h t", t=CL)
            dve.tensor_tensor(out4(a_[0]), spread(bank[1][:, 0:P].rearrange("p (q t) -> p q t", q=Q)), over_q(mask.low),
                              ALU.mult)
            step(dve.tensor_tensor(out4(lt), spread(g[:, :, 0, 0, :]), over_q(mask.up), ALU.mult))
            dve.tensor_tensor(out4(u.mk), spread(g[:, :, 1, 0, :]), over_q(mask.up), ALU.mult)
            dve.tensor_tensor(u.pt[:, :, :], lt[:, :, :], k.ident[:, :].unsqueeze(1).to_broadcast([P, Q, P]), ALU.add)
            for i in range(2):
                dve.tensor_tensor(u.rbk[:, :, i, :], g[:, :, i, 1, :],
                                  mask.incl[:, :].unsqueeze(1).to_broadcast([P, Q, CL]), ALU.mult)
            fr = u.rows[:, :, :, :].rearrange("p m q i -> p (m q i)")
            dve.tensor_copy(fr[:, 0:512], bank[2][:, :])
            step(dve.tensor_copy(fr[:, 512:768], bank[1][:, P:P + 256]))

        full = lambda v: v[:, :, :].rearrange("p q i -> p (q i)")

        def dve_level(dve, u, level):
            dst = (level + 1) % 2
            if level > 0:
                ins = dve.tensor_tensor(full(u.pt), full(u.pt), bank[5][:, :], ALU.add)
            if level < 4:
                if level < 3:
                    dve.tensor_copy(full(at[dst]), bank[4][:, :])
                ins = dve.tensor_copy(full(a_[dst]), bank[3][:, :])
            return ins

        def dve_y(dve, banks, cols):
            for i in range(2):
                ins = dve.tensor_scalar(k.y[:, i:RT:2, cols],
                                        bank[banks[i]][:, 0:RT // 2 * CL].rearrange("p (k t) -> p k t", t=CL), 1.0, None,
                                        ALU.mult)
            return ins

        def dve_sample_chunk(dve, step, inner, u):
            p = lambda i: dve.wait_ge(s_pe, i)
            cols = slice(TP, NT)
            dve_hats(dve, inner, u, cols, TS)
            inner(dve_ar(dve, u, cols))
            for t in range(RT):
                ins = dve.tensor_tensor(ahm[:, t, :, :], u.ar[:, 0, t, :].unsqueeze(1).to_broadcast([P, NB, CL]),
                                        colb[:, :, :], ALU.mult)
            step(ins)
            p(1)
            dve_masks(dve, step, u, masks[1])
            p(2)
            step(dve.tensor_copy(full(x), bank[6][:, 0:256]))
            for level in range(5):
                p(3 + level)
                step(dve_level(dve, u, level))
            p(8)
            step(dve.tensor_copy(full(sa), bank[6][:, 256:512]))
            p(9)
            step(dve_y(dve, (3, 4), cols))

        s_in = k.sem("h_dve_inner")
        s_sp, s_sv = k.sem("h_state_pe"), k.sem("h_state_dve")
        raw = sb("state_rows", [P, RT * P])
        x_rows = sb("prompt_state_rows", [64, RT * P])
        with nc.Block() as block:
            @block.gpsimd
            def _(pool):
                n = [0]

                def select(m, in_, op, base, pattern, cm):
                    pool.affine_select(out=m, in_=in_, compare_op=op, fill=0.0, base=base, pattern=pattern,
                                       channel_multiplier=cm).then_inc(s_m, 1)
                    n[0] += 1
                    pool.wait_ge(s_m, n[0])
                for i, m in enumerate(masks):
                    w = CL if i == 0 else TS
                    blk = [P // w, w]
                    for tile, op, s in ((m.up, ALU.is_gt, 1), (m.low, ALU.is_gt, -1), (m.incl4, ALU.is_ge, 1)):
                        t = tile[:, :, :].rearrange("p a t -> p (a t)")
                        one = k.ones[:, :]
                        select(t, one, op, 0, [[s, P]], -s)
                        tb = t.rearrange("p (a t) -> p a t", t=w)
                        if s == 1:
                            select(tb, tb, ALU.is_ge, 0, [[-w, blk[0]], [0, w]], 1)
                        else:
                            select(tb, tb, ALU.is_ge, w - 1, [[w, blk[0]], [0, w]], -1)
                r4 = rowb4[:, :, :].rearrange("p a b -> p (a b)")
                select(r4, k.ones[:, 0:32], ALU.is_ge, 0, [[-TS, 32]], 1)
                select(r4, r4, ALU.is_ge, TS - 1, [[TS, 32]], -1)
                select(colb[:, :, :], k.ones[:, 0:CL].unsqueeze(1).to_broadcast([P, NB, CL]), ALU.is_ge, 0, [[-TS, NB], [1, CL]], 0)
                select(colb[:, :, :], colb[:, :, :], ALU.is_ge, TS - 1, [[TS, NB], [-1, CL]], 0)

            @block.sync
            def _(sp):
                for pair in range(NB // 2):
                    if pair > 0:
                        sp.wait_ge(s_sp, pair)
                    for b in range(2):
                        sp.dma_start(raw[64 * b:64 * b + 64, :].rearrange("i (h j) -> i h j", j=64),
                                     A["state_wkv"][0, 2 * pair + b].rearrange("h i j -> i h j")).then_inc(s_st, 16)

            @block.tensor
            def _(pe):
                for pair in range(NB // 2):
                    pe.wait_ge(s_st, 32 * (pair + 1))
                    if pair > 0:
                        pe.wait_ge(s_sv, 2 * pair)
                    for t in range(RT):
                        ins = pe.transpose(bank[t // 4][:, (t % 4) * P:(t % 4 + 1) * P], raw[:, t * P:(t + 1) * P],
                                           k.ident[:, :])
                    ins.then_inc(s_sp, 1)

            @block.vector
            def _(dve):
                dve.wait_ge(s_m, 16)
                for m in masks:
                    dve.tensor_reduce(m.incl[:, :], m.incl4[:, :, :].rearrange("p a t -> p t a"), AX.X, ALU.add)
                dve.tensor_reduce(rowb[:, :], rowb4[:, :, :].rearrange("p a b -> p b a"), AX.X, ALU.add)
                dve.memset(st[:, :, :], 0.0)
                dve.memset(d1[:, :, :], 0.0)
                for pair in range(NB // 2):
                    dve.wait_ge(s_sp, pair + 1)
                    for i in range(2):
                        dve.tensor_copy(s0[:, 4 * i:4 * i + 4, 2 * pair:2 * pair + 2, :].rearrange("p t b i -> p t (b i)"),
                                        bank[i][:, :].rearrange("p (t n) -> p t n", t=4)).then_inc(s_sv, 1)
        with nc.Block() as block:
            @block.tensor
            def _(pe):
                def products(n):
                    pe.wait_ge(s_rd, n + 1)
                    pe_products(pe, u_of(n)).then_inc(s_fp, 1)

                def level(n, i):
                    pe.wait_ge(s_fv, n * FV + 2 + i)
                    pe_level(pe, u_of(n), i).then_inc(s_fp, 1)

                def turn(n, par, front, first=False):
                    u, w = sets[par], sets[1 - par]

                    def lev(i):
                        if front:
                            pe.wait_ge(s_fv, (n + 1) * FV + 2 + i)
                            pe_level(pe, w, i).then_inc(s_fp, 1)
                    if not first:
                        pe.wait_ge(s_bv, n * BV)
                    pe_x(pe, u, False).then_inc(s_bp, 1)
                    if front:
                        pe.wait_ge(s_rd, n + 2)
                        pe_products(pe, w).then_inc(s_fp, 1)
                    pe.wait_ge(s_fv, n * FV + FV)
                    pe.wait_ge(s_bv, n * BV + 1)
                    pe_sa(pe, u).then_inc(s_bp, 1)
                    lev(0)
                    pe.wait_ge(s_bv, n * BV + 2)
                    pe_y(pe, u, False, (6, 7))
                    lev(1)
                    pe_state(pe, u, range(HT // 2))
                    lev(2)
                    pe_state(pe, u, range(HT // 2, HT)).then_inc(s_bp, 1)
                    lev(3)
                    lev(4)
                u_of = lambda n: sets[n % 2]
                pe.wait_ge(s_st, 16 * NB)
                products(0)
                for i in range(5):
                    level(0, i)
                turn(0, 0, True, first=True)
                turn(1, 1, True)
                with pe.Fori(1, N_CHUNK // 2 - 1) as it:
                    for par in range(2):
                        turn(it * 2 + par, par, True)
                turn(N_CHUNK - 2, 0, True)
                turn(N_CHUNK - 1, 1, False)
                pe_sample_chunk(pe, sets[0])
                pe.wait_ge(s_v, VST)
                for t in range(RT):
                    if t >= 2:
                        pe.wait_ge(s_sv, NB + t - 1)
                    for h in (2 * t, 2 * t + 1):
                        _, pb, q, rb = head(h)
                        fold = lambda v: v[rb, q, :, :].rearrange("p b i -> p (b i)")
                        pe.matmul(bank[t % 2][pb, :], sets[0].rows[rb, 0, q, :], fold(sam), start=True, stop=False)
                        ins = pe.matmul(bank[t % 2][pb, :], sets[0].rows[rb, 1, q, :], fold(vm), start=False, stop=True)
                    ins.then_inc(s_sp, 1)
                for t in range(RT):
                    ins = pe.transpose(bank[2 + t // 4][0:64, (t % 4) * P:(t % 4 + 1) * P], st[:, t, :], k.ident[:, :])
                ins.then_inc(s_sp, 1)
                pe.wait_ge(s_sv, NB + RT)
                for pair in range(NB // 2):
                    if pair > 0:
                        pe.wait_ge(s_sv, NB + RT + 2 + 2 * pair)
                    for t in range(RT):
                        ins = pe.transpose(bank[4 + t // 4][:, (t % 4) * P:(t % 4 + 1) * P],
                                           s0[:, t, 2 * pair:2 * pair + 2, :].rearrange("p b i -> p (b i)"), k.ident[:, :])
                    ins.then_inc(s_sp, 1)

            @block.vector
            def _(dve):
                step, inner = Chain(dve, s_v), Chain(dve, s_in)
                front, back = Chain(dve, s_fv), Chain(dve, s_bv)
                cols = lambda n: bass.ds(n * CL, CL)

                def turn(n, par, has_front, has_prep):
                    u, w = sets[par], sets[1 - par]

                    def lev(i):
                        if has_front:
                            dve.wait_ge(s_fp, (n + 1) * FP + 2 + i)
                            front(dve_level(dve, w, i))
                    dve.wait_ge(s_bp, n * BP + 1)
                    back(dve.tensor_copy(full(x), bank[6][:, 0:256]))
                    if has_front:
                        dve.wait_ge(s_fp, (n + 1) * FP + 1)
                        dve_masks(dve, front, w, masks[0])
                    dve.wait_ge(s_bp, n * BP + 2)
                    back(dve.tensor_copy(full(sa), bank[6][:, 256:512]))
                    lev(0)
                    if has_prep:
                        dve.tensor_copy(pend_now[:, :], u.pend[:, :])
                        inner(dve_hats(dve, inner, u, cols(n + 2), CL))
                    pend = pend_now if has_prep else u.pend
                    lev(1)
                    lev(2)
                    dve.wait_ge(s_bp, n * BP + 3)
                    back(dve_y(dve, (6, 7), cols(n)))
                    for i in range(2):
                        ins = dve.tensor_tensor(st[:, i:RT:2, :], st[:, i:RT:2, :],
                                                bank[6 + i][:, P:P + RT // 2 * 64].rearrange("p (k i) -> p k i", i=64), ALU.add)
                    inner(ins)
                    back(dve.tensor_tensor(st[:, :, :], st[:, :, :], pend[:, :].unsqueeze(2).to_broadcast([P, RT, 64]),
                                           ALU.mult))
                    if has_prep:
                        dve_ar(dve, u, cols(n + 2)).then_inc(s_rd, 1)
                    lev(3)
                    lev(4)
                for n in range(2):
                    if n == 1:
                        dve.wait_ge(s_fp, 1)
                    inner(dve_hats(dve, inner, sets[n], slice(n * CL, (n + 1) * CL), CL))
                    dve_ar(dve, sets[n], slice(n * CL, (n + 1) * CL)).then_inc(s_rd, 1)
                    if n == 0:
                        dve.wait_ge(s_fp, 1)
                        dve_masks(dve, front, sets[0], masks[0])
                for i in range(5):
                    dve.wait_ge(s_fp, 2 + i)
                    front(dve_level(dve, sets[0], i))
                for c_ in (front, back, inner):
                    c_.settle()
                with dve.Fori(0, N_CHUNK // 2 - 1) as it:
                    front.enter(it, 2 * FV)
                    back.enter(it, 2 * BV)
                    inner.enter(it, 16)
                    for par in range(2):
                        turn(it * 2 + par, par, True, True)
                for c_ in (front, back, inner):
                    c_.leave(N_CHUNK // 2 - 1)
                turn(N_CHUNK - 2, 0, True, False)
                turn(N_CHUNK - 1, 1, False, False)
                dve_sample_chunk(dve, step, inner, sets[0])
                for src, dst in ((sa, sam), (sets[0].rows[:, 2, :, :], vm)):
                    for q in range(Q):
                        ins = dve.tensor_tensor(dst[:, q, :, :], src[:, q, :].unsqueeze(1).to_broadcast([P, NB, 64]),
                                                rowb[:, :].unsqueeze(2).to_broadcast([P, NB, 64]), ALU.mult)
                step(ins)
                for t in range(RT):
                    dve.wait_ge(s_sp, NB // 2 + t + 1)
                    s0t = s0[:, t, :, :].rearrange("p b i -> p (b i)")
                    step(dve.tensor_tensor(s0t, s0t, bank[t % 2][:, :], ALU.add))
                    dve.tensor_tensor(s0[:, t, :, :], s0[:, t, :, :], pc[:, t, TS - 1:CL:TS].unsqueeze(2)
                                      .to_broadcast([P, NB, 64]), ALU.mult).then_inc(s_sv, 1)
                dve.wait_ge(s_sp, NB // 2 + RT + 1)
                for i in range(2):
                    dve.tensor_copy(x_rows[0:64, i * 512:(i + 1) * 512], bank[2 + i][0:64, :]).then_inc(s_sv, 1)
                for pair in range(NB // 2):
                    dve.wait_ge(s_sp, NB // 2 + RT + 2 + pair)
                    if pair > 0:
                        dve.wait_ge(s_o, 16 + 32 * pair)
                    for i in range(2):
                        dve.tensor_copy(raw[:, i * 512:(i + 1) * 512], bank[4 + i][:, :]).then_inc(s_sv, 1)

            @block.sync
            def _(sp):
                sp.wait_ge(s_sv, NB + RT + 2)
                sp.dma_start(A["wkv_prompt"][0, 0].rearrange("h i j -> i h j"),
                             x_rows[0:64, :].rearrange("i (h j) -> i h j", j=64)).then_inc(s_o, 16)
                for pair in range(NB // 2):
                    sp.wait_ge(s_sv, NB + RT + 4 + 2 * pair)
                    for b in range(2):
                        sp.dma_start(A["wkv_sample"][0, 2 * pair + b].rearrange("h i j -> i h j"),
                                     raw[64 * b:64 * b + 64, :].rearrange("i (h j) -> i h j", j=64)).then_inc(s_o, 16)
                sp.wait_ge(s_o, 16 + 32 * (NB // 2))


def phase_groupnorm(k, A):
    nc = k.nc
    with ExitStack() as c:
        sb = lambda name, shape, dt=F32: k.sb(name, shape, dt, c)
        sq, sd = sb("gn_square", [P, RT, NT]), sb("gn_root", [P, RT, NT])
        s_m, s_c, s_q, s_n, s_r, s_v = (k.sem(n) for n in ("i_means", "i_centred", "i_squared", "i_variances",
                                                            "i_roots", "i_dve"))
        with nc.Block() as block:
            @block.tensor
            def _(pe):
                for t in range(RT):
                    if t >= 4:
                        pe.wait_ge(s_c, t - 3)
                    pe.matmul(k.bank[t % 4][:, 0:NT], k.headones[:, :], k.y[:, t, :], start=True, stop=True)\
                        .then_inc(s_m, 1)
                for t in range(RT):
                    pe.wait_ge(s_q, t + 1)
                    if t >= 4:
                        pe.wait_ge(s_r, t - 3)
                    pe.matmul(k.bank[4 + t % 4][:, 0:NT], k.headones[:, :], sq[:, t, :], start=True, stop=True)\
                        .then_inc(s_n, 1)

            @block.scalar
            def _(act):
                for t in range(RT):
                    act.wait_ge(s_n, t + 1)
                    act.activation(sd[:, t, :], k.bank[4 + t % 4][:, 0:NT], ACT.Sqrt, bias=k.eps[:, 1:2],
                                   scale=1.0 / 64).then_inc(s_r, 1)

            @block.vector
            def _(dve):
                step = Chain(dve, s_v)
                for t in range(RT):
                    dve.wait_ge(s_m, t + 1)
                    dve.scalar_tensor_tensor(out=k.y[:, t, :], in0=k.bank[t % 4][:, 0:NT], scalar=-1.0 / 64,
                                             in1=k.y[:, t, :], op0=ALU.mult, op1=ALU.add).then_inc(s_c, 1)
                    dve.wait_ge(s_c, t + 1)
                    dve.tensor_tensor(sq[:, t, :], k.y[:, t, :], k.y[:, t, :], ALU.mult).then_inc(s_q, 1)
                dve.wait_ge(s_r, RT)
                step(dve.reciprocal(sd[:, :, :], sd[:, :, :]))
                step(dve.tensor_tensor(k.y, k.y, sd[:, :, :], ALU.mult))
                for t in range(RT):
                    ins = dve.tensor_scalar(k.y[:, t, :], k.y[:, t, :], k.par[:, C_LNW + t:C_LNW + t + 1],
                                            k.par[:, C_LNB + t:C_LNB + t + 1], ALU.mult, ALU.add)
                step(ins)
                step(dve.tensor_tensor(k.y, k.y, k.bonus, ALU.add))
                step(dve.tensor_tensor(k.mixT[:, RT:KT, :], k.y, k.g[:, :, :], ALU.mult))


CB, CS = 32, 16
PAST, PAGE = 2048, 128
N_PAGES = PAST // PAGE
NCP = TP // CS - 1
NCS = PAST // CS - 1
CMP_T, SLC_T, WIN_T = 8, 12, 16
SELB, TOPK = 64, 16
NSEL = PAST // SELB + 1
WINL = 512
ROW = 512
KVW = 256
FAR = 1.0e33


def phase_rows(k, A):
    nc = k.nc
    with ExitStack() as c:
        zero = k.zero_rows
        s_t, s_c, s_z, s_o = k.sem("j_transposed"), k.sem("j_copied"), k.sem("j_zero"), k.sem("j_written")
        s_gate = k.sem("j_gates_written")
        k.rows_written = s_o
        k.s_cw = k.sem("q_weights")
        n_out = [0]
        with nc.Block() as block:
            @block.gpsimd
            def _(pool):
                pool.memset(zero[:, :], 0.0).then_inc(s_z, 1)

            @block.scalar
            def _(act):
                for i, (a, b) in enumerate(((A["cmp_k_w1"], A["cmp_k_w2"]), (A["cmp_v_w1"], A["cmp_v_w2"]))):
                    act.dma_start(k.cp_w1[:, i, :, :], a[0].rearrange("s d e -> d s e")).then_inc(k.s_cw, 16)
                    act.dma_start(k.cp_w2[:, i, :], b[0]).then_inc(k.s_cw, 16)

            @block.tensor
            def _(pe):
                for i, (at, n) in enumerate(ROWS):
                    for q in range(3):
                        m = 3 * i + q
                        if m >= 6:
                            pe.wait_ge(s_c, m - 5)
                        for j in range(4):
                            ins = pe.transpose(k.bank[m % 6][0:n, j * P:(j + 1) * P],
                                               k.pT[:, CMP_T + 4 * q + j, at:at + n], k.ident[:, :])
                        ins.then_inc(s_t, 1)

            @block.vector
            def _(dve):
                for i, (at, n) in enumerate(ROWS):
                    for q in range(3):
                        m = 3 * i + q
                        dve.wait_ge(s_t, m + 1)
                        dve.tensor_copy(k.kvrows[0:n, i, q * ROW:(q + 1) * ROW], k.bank[m % 6][0:n, :]).then_inc(s_c, 1)

            @block.sync
            def _(sp):
                def out(dst, src, **how):
                    sp.dma_start(dst, src, **how).then_inc(s_o, 16)
                    n_out[0] += 1
                r = lambda v: v.rearrange("s kv g d -> s (kv g d)")
                sp.dma_start(k.gate_dram[:, :], k.gates[0:NS, 2, :]).then_inc(s_gate, 16)
                sp.wait_ge(s_gate, 16)
                for h in range(HEADS):
                    for j in range(3):
                        out(k.sgates[TS * h:TS * h + TS, :, j],
                            k.gate_dram[:, j * HEADS + h].rearrange("(b t) -> t b", t=TS),
                            allow_slow_non_contiguous=True)
                out(A["win_kv_sample"][0, :, 0:WINL - TS].rearrange("b s kv g d -> b (s kv g d)"),
                    A["state_win_kv"][0, :, TS:WINL].rearrange("b s kv g d -> b (s kv g d)"))
                sp.wait_ge(s_z, 1)
                for i in range(2):
                    out(r(A["win_kv_prompt"][0, 0, i * P:(i + 1) * P]), zero[:, :])
                sp.wait_ge(s_c, 9)
                for i in range(2):
                    out(r(A["cmp_kv_prompt"][0, 0, i * P:(i + 1) * P]), k.kvrows[:, i, 0:ROW])
                    out(r(A["slc_kv_prompt"][0, 0, i * P:(i + 1) * P]), k.kvrows[:, i, ROW:2 * ROW])
                    out(r(A["win_kv_prompt"][0, 0, TP + i * P:TP + (i + 1) * P]), k.kvrows[:, i, 2 * ROW:3 * ROW])
                out(A["cmp_kv_sample"][0].rearrange("b t kv g d -> (b t) (kv g d)"), k.kvrows[0:NS, 2, 0:ROW])
                out(A["slc_kv_sample"][0].rearrange("b t kv g d -> (b t) (kv g d)"), k.kvrows[0:NS, 2, ROW:2 * ROW])
                for b in range(NB):
                    out(r(A["win_kv_sample"][0, b, WINL - TS:WINL]), k.kvrows[TS * b:TS * b + TS, 2, 2 * ROW:3 * ROW])
        k.n_rows_written = 16 * n_out[0]


def phase_compress_prompt(k, A):
    nc = k.nc
    with ExitStack() as c:
        sb = lambda name, shape: k.sb(name, shape, F32, c)
        w1, w2, sil = k.cp_w1, k.cp_w2, sb("cp_silu", [P, 2, 2 * NCP])
        s_w = k.s_cw
        s_pre, s_sil, s_out, s_kv = (k.sem(n) for n in ("q_pre", "q_silu", "q_multiplied", "q_done"))
        with nc.Block() as block:
            @block.tensor
            def _(pe):
                pe.wait_ge(s_w, 64)
                compress_hidden(k, pe, NCP, w1,
                                lambda i, s: k.pT[:, CMP_T + 2 * i:CMP_T + 2 * i + 2, s:s + CS * (NCP - 1) + 1:CS], s_pre)
                pe.wait_ge(s_sil, 2)
                compress_out(k, pe, NCP, w2, sil, s_out)

            @block.scalar
            def _(act):
                for i in range(2):
                    act.wait_ge(s_pre, i + 1)
                    act.activation(sil[:, i, :], k.bank[4 + i][:, 0:2 * NCP], ACT.Silu, bias=k.peb[:, i:i + 1])\
                        .then_inc(s_sil, 1)

            @block.vector
            def _(dve):
                dve.wait_ge(s_out, 1)
                dve.tensor_copy(k.kcTp[:, :], k.bank[6][:, 0:2 * NCP]).then_inc(s_kv, 1)
                dve.tensor_copy(k.vcp[0:NCP, :], k.bank[7][0:NCP, 0:KVW]).then_inc(s_kv, 1)


def phase_attend_prompt(k, A):
    nc = k.nc
    with ExitStack() as c:
        sb = lambda name, shape, dt=F32: k.sb(name, shape, dt, c)
        dtok, dcmp = sb("d_tok", [P, TP]), sb("d_cmp", [P, 2, NCP])
        far = sb("d_far", [P, TP])
        slope = sb("neg_slopes", [P, HEADS])
        rowok = sb("row_has_block", [P, 1])
        q = sb("q_head", [P, TP])
        NK = (P, TP)
        s_ = [sb(f"scores{i}", [P, 16 + 2 * NK[i]]) for i in range(2)]
        mx, sm, fac = sb("neg_max", [P, 2, 3]), sb("exp_sums", [P, 2, 3]), sb("factors", [P, 2, 3])
        pt = [sb(f"probsT{i}", [P, 2 * NK[i]]) for i in range(2)]
        ptc = sb("probsT_cmp", [16, 2, P])
        s_i, s_v, s_p, s_a, s_in = (k.sem(n) for n in ("m_iota", "m_dve_stage", "m_pe_stage", "m_exp_stage",
                                                       "m_dve_inner"))
        VST, PST, AST, IN = 8, 5, 2, 6
        with nc.Block() as block:
            @block.gpsimd
            def _(pool):
                pool.iota(dtok[:, :], pattern=[[-1, TP]], base=P, channel_multiplier=1,
                          allow_small_or_imprecise_dtypes=True).then_inc(s_i, 1)
                pool.iota(dcmp[:, :, :], pattern=[[P, 2], [-CS, NCP]], base=-(CB - 1), channel_multiplier=1,
                          allow_small_or_imprecise_dtypes=True).then_inc(s_i, 1)
                for h in range(HEADS):
                    ins = pool.memset(slope[:, h:h + 1], -2.0 ** (-8.0 * (h + 1) / HEADS))
                ins.then_inc(s_i, 1)
                pool.affine_select(out=rowok[:, :], in_=k.ones[:, 0:1], compare_op=ALU.is_ge, fill=0.0, base=-(CB - 1),
                                   pattern=[[0, 1]], channel_multiplier=1).then_inc(s_i, 1)

            @block.vector
            def _(dve):
                dve.wait_ge(s_i, 4)
                step = k.steps.chain(dve)
                step(dve.tensor_scalar(far[:, :], dtok[:, :], 0.0, FAR, ALU.is_lt, ALU.mult))
                step(dve.tensor_tensor(dtok[:, :], dtok[:, :], far[:, :], ALU.add))
                fl = dcmp[:, :, :].rearrange("p a b -> p (a b)")
                step(dve.tensor_scalar(far[:, 0:2 * NCP], fl, 0.0, FAR, ALU.is_lt, ALU.mult))
                step(dve.tensor_tensor(fl, fl, far[:, 0:2 * NCP], ALU.add))
        with nc.Block() as block:
            @block.sync
            def _(sp):
                sp.wait_ge(k.rows_written, k.n_rows_written)

            def each_head(eng, body):
                for g in range(GROUPS):
                    with eng.Fori(0, HPG) as hh:
                        body(g, hh, hh + HPG * g)

            @block.tensor
            def _(pe):
                def body(g, hh, n):
                    v = lambda i: pe.wait_ge(s_v, n * VST + i)
                    v(1)
                    for t in range(2):
                        qt = q[:, t * P:(t + 1) * P]
                        pe.matmul(k.bank[t][:, TP:TP + NCP], qt, k.kcTp[:, g * NCP:(g + 1) * NCP], start=True, stop=True)
                        pe.matmul(k.bank[t][:, 0:NK[t]], qt, k.pT[:, SLC_T + g, 0:NK[t]], start=True, stop=True)
                        pe.matmul(k.bank[2 + t][:, 0:NK[t]], qt, k.pT[:, WIN_T + g, 0:NK[t]], start=True, stop=True)\
                            .then_inc(s_p, 1)
                    for t in range(2):
                        v(4 + t)
                        out_c = (k.bank[4][0:NCP, 2 * P:3 * P], k.bank[7][0:NCP, 0:P])[t]
                        pe.transpose(out_c, s_[t][:, 0:NCP], k.ident[:, :])
                        for j in range(2 * NK[t] // P):
                            ins = pe.transpose(k.bank[4 + t][:, j * P:(j + 1) * P], s_[t][:, 16 + j * P:16 + (j + 1) * P],
                                               k.ident[:, :])
                        ins.then_inc(s_p, 1)
                    for t in range(2):
                        v(6 + t)
                        out = k.bank[6][:, t * P:(t + 1) * P]
                        pe.matmul(out, k.vcp[0:NCP, g * P:(g + 1) * P], ptc[0:NCP, t, :], start=True, stop=False)
                        for j in range(2 * NK[t] // P):
                            per = NK[t] // P
                            col = (1 + j // per) * ROW + KVW + g * P
                            ins = pe.matmul(out, k.kvrows[:, j % per, col:col + P], pt[t][:, j * P:(j + 1) * P],
                                            start=False, stop=(j == 2 * per - 1))
                    ins.then_inc(s_p, 1)
                each_head(pe, body)

            @block.scalar
            def _(act):
                def body(g, hh, n):
                    for t in range(2):
                        act.wait_ge(s_v, n * VST + 2 + t)
                        for i, (a, b) in enumerate(((0, NCP), (16, 16 + NK[t]), (16 + NK[t], 16 + 2 * NK[t]))):
                            ins = act.activation(s_[t][:, a:b], s_[t][:, a:b], ACT.Exp, bias=mx[:, t, i:i + 1],
                                                 accum_out=sm[:, t, i:i + 1])
                        ins.then_inc(s_a, 1)
                each_head(act, body)

            @block.vector
            def _(dve):
                def body(g, hh, n):
                    step = Chain(dve, s_v, n * VST)
                    inner = Chain(dve, s_in, n * IN)
                    p = lambda i: dve.wait_ge(s_p, n * PST + i)
                    step(dve.tensor_scalar(q[:, :], k.pT[:, bass.ds(n, 1), 0:TP].rearrange("p o n -> p (o n)"), SCALE,
                                           None, ALU.mult))
                    sl = slope[:, bass.ds(n, 1)]
                    for t in range(2):
                        p(1 + t)
                        nk = NK[t]
                        dist = dtok[:, TP - nk:TP]
                        for o, ps, dd in ((0, k.bank[t][:, TP:TP + NCP], dcmp[:, t, :]), (16, k.bank[t][:, 0:nk], dist),
                                          (16 + nk, k.bank[2 + t][:, 0:nk], dist)):
                            w = NCP if o == 0 else nk
                            ins = dve.scalar_tensor_tensor(out=s_[t][:, o:o + w], in0=dd, scalar=sl, in1=ps, op0=ALU.mult,
                                                           op1=ALU.add)
                        inner(ins)
                        dve.tensor_reduce(mx[:, t, 0:1], s_[t][:, 0:NCP], AX.X, ALU.max, negate=True)
                        step(dve.tensor_reduce(mx[:, t, 1:3], s_[t][:, 16:16 + 2 * nk].rearrange("p (a n) -> p a n", a=2),
                                               AX.X, ALU.max, negate=True))
                    for t in range(2):
                        nk = NK[t]
                        dve.wait_ge(s_a, n * AST + 1 + t)
                        inner(dve.reciprocal(fac[:, t, :], sm[:, t, :]))
                        gate = k.gates[:, t, :].rearrange("p (r h) -> p r h", h=HEADS)[:, :, bass.ds(n, 1)]\
                            .rearrange("p r o -> p (r o)")
                        ins = dve.tensor_tensor(fac[:, t, :], fac[:, t, :], gate, ALU.mult)
                        inner(ins)
                        if t == 0:
                            dve.tensor_scalar(s_[t][:, 0:NCP], s_[t][:, 0:NCP], fac[:, t, 0:1], rowok[:, :], ALU.mult, ALU.mult)
                        else:
                            dve.tensor_scalar(s_[t][:, 0:NCP], s_[t][:, 0:NCP], fac[:, t, 0:1], None, ALU.mult)
                        for i in range(2):
                            part = s_[t][:, 16 + i * nk:16 + (i + 1) * nk]
                            ins = dve.tensor_scalar(part, part, fac[:, t, 1 + i:2 + i], None, ALU.mult)
                        step(ins)
                    for t in range(2):
                        p(3 + t)
                        dve.tensor_copy(ptc[0:NCP, t, :], (k.bank[4][0:NCP, 2 * P:3 * P], k.bank[7][0:NCP, 0:P])[t])
                        step(dve.tensor_copy(pt[t][:, :], k.bank[4 + t][:, 0:2 * NK[t]]))
                    p(5)
                    step(dve.tensor_scalar(k.mixT[:, bass.ds(n, 1), 0:TP].rearrange("p o n -> p (o n)"),
                                           k.bank[6][:, 0:TP], 1.0, None, ALU.mult))
                    assert step.n == VST and inner.n == IN, (step.n, inner.n)
                each_head(dve, body)


def phase_attend_samples(k, A):
    nc = k.nc
    R = HEADS * TS
    with ExitStack() as c:
        sb = lambda name, shape, dt=F32: k.sb(name, shape, dt, c)
        kcs, vcs = [sb(f"kc_sample{i}", [P, 2 * NCS]) for i in range(2)], [sb(f"vc_sample{i}", [NCS, KVW]) for i in range(2)]
        PG = 4
        NQ = N_PAGES // PG
        kraw = [sb(f"slc_k{i}", [P, PG, KVW]) for i in range(NQ)]
        vraw = [sb(f"slc_v{i}", [P, N_PAGES, KVW]) for i in range(2)]
        wraw = [sb(f"win_raw{i}", [P, WINL // P, ROW]) for i in range(2)]
        vnew = [sb(f"v_new{i}", [TS, 2, KVW]) for i in range(2)]
        kt = [sb(f"slc_kT{i}", [P, GROUPS, PAST]) for i in range(2)]
        wt = [sb(f"win_kT{i}", [P, GROUPS, WINL]) for i in range(2)]
        orow = sb("out_rows", [P, KVW])
        qz = sb("q_padded", [P, GROUPS, R])
        S, W = PAST + TS, WINL + TS
        s_s, s_w, s_c = sb("s_slc", [R, S]), sb("s_win", [R, W]), sb("s_cmp", [R, NCS + 1])
        p_c = sb("p_cmp", [R, NCS + 1])
        b_s, b_new = k.pT[0:R, 0:HEADS, 0:TP], sb("bias_new", [R, TS])
        b_w, b_c = sb("bias_win", [R, W]), sb("bias_cmp", [R, NCS + 1])
        cmpx = sb("compare", [R, NSEL, NSEL])
        cmpe = sb("compare_eq", [R, NSEL, NSEL])
        before = k.pT[0:R, CMP_T:CMP_T + 4, :].rearrange("p a n -> p (a n)")[:, 0:NSEL * NSEL]\
            .rearrange("p (i j) -> p i j", i=NSEL)
        imp, drop = sb("importance", [R, NSEL]), sb("dropped", [R, NSEL])
        forced = sb("forced", [R, NSEL])
        over = sb("overlap", [NCS, NSEL])
        mx, sm, fac = sb("s_negmax", [R, 3]), sb("s_sums", [R, 3]), sb("s_factors", [R, 3])
        rowi, tstep, nslope = sb("row_index", [R, 4], I32), sb("row_step", [R, 1]), sb("row_slope", [R, 1])
        pts = sb("s_probsT", [P, N_PAGES, R])
        pto = sb("s_probsT_rest", [P, 8, R])
        psg, psb = sb("p_group", [P, 8]), sb("p_group_rows", [P, GROUPS, HPG, TS])
        table = sb("slc_table", [1, NB * N_PAGES], I32)
        s_i, s_tab = k.sem("n_iota"), k.sem("n_table")
        s_k = [k.sem(f"n_k_pages{i}") for i in range(NQ)]
        s_vr = [k.sem(f"n_v_pages{i}") for i in range(2)]
        s_wr = [k.sem(f"n_window{i}") for i in range(2)]
        s_v, s_p, s_a, s_in = k.sem("n_dve_stage"), k.sem("n_pe_stage"), k.sem("n_exp_stage"), k.sem("n_dve_inner")
        s_kt = k.sem("n_k_transposed")
        s_kc = k.sem("n_k_copied")
        NKT = N_PAGES // 2 + 2
        with nc.Block() as block:
            @block.gpsimd
            def _(pool):
                f = dict(allow_small_or_imprecise_dtypes=True)
                pool.iota(b_s, pattern=[[-TP, HEADS], [-1, TP]], base=PAST, channel_multiplier=0, **f).then_inc(s_i, 1)
                pool.iota(b_new[:, :], pattern=[[-1, TS]], base=0, channel_multiplier=0, **f).then_inc(s_i, 1)
                pool.iota(b_w[:, :], pattern=[[-1, W]], base=WINL, channel_multiplier=0, **f).then_inc(s_i, 1)
                pool.iota(b_c[:, 0:NCS], pattern=[[-CS, NCS]], base=PAST - (CB - 1), channel_multiplier=0, **f).then_inc(s_i, 1)
                pool.iota(rowi[:, 0:1], pattern=[[0, 1]], base=0, channel_multiplier=1).then_inc(s_i, 1)
                pool.memset(qz[:, :, :], 0.0).then_inc(s_i, 1)
                pool.memset(forced[:, :], 0.0).then_inc(s_i, 1)
                pool.wait_ge(s_i, 7)
                pool.memset(forced[:, 0:1], 1.0e4).then_inc(s_i, 1)
                pool.memset(forced[:, NSEL - 2:NSEL], 1.0e4).then_inc(s_i, 1)
                pool.affine_select(out=before[:, :, :], in_=k.ones[0:R, 0:1].unsqueeze(2).to_broadcast([R, NSEL, NSEL]),
                                   compare_op=ALU.is_gt, fill=0.0, base=0, pattern=[[1, NSEL], [-1, NSEL]],
                                   channel_multiplier=0).then_inc(s_i, 1)
                pool.affine_select(out=over[:, :], in_=k.ones[0:NCS, 0:NSEL], compare_op=ALU.is_ge, fill=0.0,
                                   base=SELB - 1, pattern=[[SELB, NSEL]], channel_multiplier=-CS).then_inc(s_i, 1)
                pool.wait_ge(s_i, 11)
                pool.affine_select(out=over[:, :], in_=over[:, :], compare_op=ALU.is_ge, fill=0.0, base=CB - 1,
                                   pattern=[[-SELB, NSEL]], channel_multiplier=CS).then_inc(s_i, 1)

            @block.vector
            def _(dve):
                step = k.steps.chain(dve)
                dve.wait_ge(s_i, 12)
                step(dve.tensor_scalar(rowi[:, 1:2], rowi[:, 0:1], TS - 1, None, ALU.bitwise_and))
                step(dve.tensor_scalar(rowi[:, 2:3], rowi[:, 0:1], 2, None, ALU.logical_shift_right))
                step(dve.tensor_copy(tstep[:, :], rowi[:, 1:2]))
                step(dve.tensor_scalar(rowi[:, 3:4], rowi[:, 2:3], -1.0, 126.0, ALU.mult, ALU.add))
                step(dve.tensor_scalar(rowi[:, 0:1], rowi[:, 3:4], 23, None, ALU.logical_shift_left))
                step(dve.tensor_scalar(nslope[:, :], rowi[:, 0:1].bitcast(F32), -1.0, None, ALU.mult))
                step(dve.tensor_scalar(b_s, b_s, tstep[:, 0:1], None, ALU.add))
                for tile, lo in ((b_new, 0), (b_w, WINL)):
                    step(dve.tensor_scalar(tile[:, :], tile[:, :], tstep[:, 0:1], None, ALU.add))
                    new = tile[:, lo:lo + TS]
                    step(dve.tensor_scalar(cmpx[:, 0, 0:TS], new, 0.0, FAR, ALU.is_lt, ALU.mult))
                    step(dve.tensor_tensor(new, new, cmpx[:, 0, 0:TS], ALU.add))
                old = b_w[:, 0:TS]
                step(dve.tensor_scalar(cmpx[:, 0, 0:TS], old, float(WINL), FAR, ALU.is_ge, ALU.mult))
                step(dve.tensor_tensor(old, old, cmpx[:, 0, 0:TS], ALU.add))
                step(dve.tensor_scalar(b_c[:, 0:NCS], b_c[:, 0:NCS], tstep[:, 0:1], None, ALU.add))
                for tile in (b_s, b_new[:, :], b_w[:, :], b_c[:, 0:NCS]):
                    step(dve.tensor_scalar(tile, tile, nslope[:, 0:1], None, ALU.mult))

            @block.sync
            def _(sp):
                sp.dma_start(table[:, :], A["page_table"].rearrange("b n -> (b n)").rearrange("(o n) -> o n", o=1))\
                    .then_inc(s_tab, 16)
                sp.wait_ge(s_tab, 16)

        VST, PST, AST, IN = 13, 8, 3, 14
        with nc.Block() as block:
            @block.sync
            def _(sp):
                def load(b, u, keys_used, buffers_used):
                    one = lambda v: v[:, bass.ds(b, 1), :].rearrange("p o n -> p (o n)")
                    row = lambda v: v.rearrange("o t kv g d -> (o t) (kv g d)")

                    def page(r, j):
                        n = sp.value_load(table[0:1, bass.ds(b * N_PAGES + r * PG + j, 1)], min_val=0,
                                          max_val=A["cache_slc_kv"].shape[1] - 1)
                        return row(A["cache_slc_kv"][0, bass.ds(n, 1)])
                    for r in range(NQ):
                        if keys_used:
                            sp.wait_ge(s_kt, (b - 1) * NKT + 2 * (r + 1))
                        for j in range(PG):
                            sp.dma_start(kraw[r][:, j, :], page(r, j)[:, 0:KVW]).then_inc(s_k[r], 16)
                    if buffers_used:
                        sp.wait_ge(s_p, (b - 1) * PST)
                    sp.dma_start(wraw[u][:, :, :], A["state_win_kv"][0, bass.ds(b, 1)]
                                 .rearrange("o (n p) kv g d -> p (o n) (kv g d)", p=P)).then_inc(s_wr[u], 16)
                    sp.dma_start(kcs[u][:, :], one(k.kc_dram)).then_inc(s_wr[u], 16)
                    sp.dma_start(vcs[u][:, :], one(k.vc_dram)).then_inc(s_wr[u], 16)
                    sp.dma_start(vnew[u][:, 0, :], row(A["slc_kv_sample"][0, bass.ds(b, 1)])[:, KVW:]).then_inc(s_wr[u], 16)
                    sp.dma_start(vnew[u][:, 1, :], row(A["win_kv_sample"][0, bass.ds(b, 1), WINL - TS:WINL])[:, KVW:])\
                        .then_inc(s_wr[u], 16)
                    for r in range(NQ):
                        for j in range(PG):
                            sp.dma_start(vraw[u][:, r * PG + j, :], page(r, j)[:, KVW:]).then_inc(s_vr[u], 16)
                load(0, 0, False, False)
                load(1, 1, True, False)
                with sp.Fori(1, NB // 2) as it:
                    for u in range(2):
                        load(it * 2 + u, u, True, True)

            @block.tensor
            def _(pe):
                def turned(b, m, tiles):
                    if m >= 2:
                        pe.wait_ge(s_kc, b * NKT + m - 1)
                    for j, src in enumerate(tiles):
                        ins = pe.transpose(k.bank[1 + m % 2][:, j * P:(j + 1) * P], src, k.ident[:, :])
                    ins.then_inc(s_kt, 1)

                def turn_keys(b, u, turn):
                    for m in range(N_PAGES // 2):
                        r = m // 2
                        if m % 2 == 0:
                            pe.wait_ge(s_k[r], (b + 1) * 16 * PG)
                        turned(b, m, [kraw[r][:, (2 * m + i) % PG, g * P:(g + 1) * P] for g in range(2) for i in range(2)])
                    pe.wait_ge(s_wr[u], turn * 80)
                    for m in range(2):
                        turned(b, N_PAGES // 2 + m, [wraw[u][:, 2 * m + i, g * P:(g + 1) * P] for g in range(2)
                                                     for i in range(2)])

                def body(b, u, it, last=False):
                    v = lambda i: pe.wait_ge(s_v, b * VST + i)
                    v(1)
                    for g in range(2):
                        ins = pe.matmul(k.bank[0][0:R, 0:NCS], qz[:, g, :], kcs[u][:, g * NCS:(g + 1) * NCS], start=(g == 0), stop=(g == 1))
                    for br in range(2):
                        for g in range(2):
                            ins = pe.matmul(k.bank[0][0:R, 128 + TS * br:128 + TS * (br + 1)], qz[:, g, :],
                                            knew(b, (SLC_T, WIN_T)[br] + g), start=(g == 0), stop=(g == 1))
                    ins.then_inc(s_p, 1)

                    pe.wait_ge(s_kc, (b + 1) * NKT)
                    for ch in range(4):
                        if ch >= 2:
                            v(3 + ch - 2)
                        for g in range(2):
                            ins = pe.matmul(k.bank[3 + ch % 2][0:R, :], qz[:, g, :], kt[u][:, g, ch * 512:(ch + 1) * 512],
                                            start=(g == 0), stop=(g == 1))
                        if ch == 1:
                            for g in range(2):
                                ins = pe.matmul(k.bank[5][0:R, :], qz[:, g, :], wt[u][:, g, :], start=(g == 0), stop=(g == 1))
                            ins.then_inc(s_p, 1)
                        if ch == 3:
                            ins.then_inc(s_p, 1)
                    if not last:
                        turn_keys(b + 1, 1 - u, it + 1 + u)
                    v(7)
                    pe.matmul(k.bank[7][0:NCS, 0:R], p_c[:, 0:NCS], k.ident[0:R, 0:R], start=True, stop=True)
                    pe.transpose(k.bank[7][0:NCS, R:2 * R], s_c[:, 0:NCS], k.ident[0:R, 0:R]).then_inc(s_p, 1)
                    v(8)
                    pe.matmul(k.bank[0][0:R, 160:160 + NSEL], psb[0:NCS, :, :, :].rearrange("p g h t -> p (g h t)"),
                              over[:, :], start=True, stop=True).then_inc(s_p, 1)
                    v(10)
                    pe.matmul(k.bank[6][:, 0:R], s_s[:, 0:P], k.ident[0:R, 0:R], start=True, stop=True)
                    for j in range(1, N_PAGES):
                        pe.transpose(k.bank[6][:, j * R:(j + 1) * R], s_s[:, j * P:(j + 1) * P], k.ident[0:R, 0:R])
                    pe.transpose(k.bank[7][0:TS, 2 * R:3 * R], s_s[:, PAST:S], k.ident[0:R, 0:R])
                    pe.transpose(k.bank[7][0:TS, 3 * R:4 * R], s_w[:, WINL:W], k.ident[0:R, 0:R])
                    for j in range(WINL // P):
                        ins = pe.transpose(k.bank[7][:, (4 + j) * R:(5 + j) * R], s_w[:, j * P:(j + 1) * P], k.ident[0:R, 0:R])
                    ins.then_inc(s_p, 1)
                    pe.wait_ge(s_vr[u], (it + 1) * 16 * N_PAGES)
                    v(11)
                    tiles = [(pts[:, j, :], vraw[u][:, j, :]) for j in range(N_PAGES)]
                    tiles += [(pto[:, 4 + j, :], wraw[u][:, j, KVW:]) for j in range(WINL // P)]
                    tiles += [(pto[0:TS, 2 + br, :], vnew[u][:, br, :]) for br in range(2)]
                    tiles += [(pto[0:NCS, 1, :], vcs[u][:, :])]
                    for n, (probs, values) in enumerate(tiles):
                        ins = pe.matmul(k.bank[5][R * (n % 4):R * (n % 4) + R, 0:KVW], probs, values, start=(n < 4),
                                        stop=(n >= len(tiles) - 4))
                    ins.then_inc(s_p, 1)
                    v(12)
                    for g in range(2):
                        ins = pe.matmul(k.bank[6][:, g * R:(g + 1) * R], orow[:, g * P:(g + 1) * P], k.stack[:, :],
                                        start=True, stop=True)
                    ins.then_inc(s_p, 1)
                knew = lambda b, t: k.pT[:, t, bass.ds(TP + b * TS, TS)]
                turn_keys(0, 0, 1)
                with pe.Fori(0, NB // 2 - 1) as it:
                    for u in range(2):
                        body(it * 2 + u, u, it)
                for u in range(2):
                    body(NB - 2 + u, u, NB // 2 - 1, last=(u == 1))

            @block.scalar
            def _(act):
                def copy_keys(b, u):
                    for m in range(NKT):
                        act.wait_ge(s_kt, b * NKT + m + 1)
                        bank = k.bank[1 + m % 2][:, :].rearrange("p (g n) -> p g n", g=2)
                        dst = kt[u][:, :, m * 256:(m + 1) * 256] if m < N_PAGES // 2 else \
                            wt[u][:, :, (m - N_PAGES // 2) * 256:(m - N_PAGES // 2 + 1) * 256]
                        act.copy(dst, bank).then_inc(s_kc, 1)

                def body(b, u, last=False):
                    for i, (tile, n, at) in enumerate(((s_c, NCS, 2), (s_w, W, 6), (s_s, S, 9))):
                        act.wait_ge(s_v, b * VST + at)
                        act.activation(tile[:, 0:n], tile[:, 0:n], ACT.Exp, bias=mx[:, i:i + 1], accum_out=sm[:, i:i + 1])\
                            .then_inc(s_a, 1)
                        if i == 0 and not last:
                            copy_keys(b + 1, 1 - u)
                copy_keys(0, 0)
                with act.Fori(0, NB // 2 - 1) as it:
                    for u in range(2):
                        body(it * 2 + u, u)
                for u in range(2):
                    body(NB - 2 + u, u, last=(u == 1))

            @block.vector
            def _(dve):
                def body(b):
                    step = Chain(dve, s_v, b * VST)
                    inner = Chain(dve, s_in, b * IN)
                    p = lambda i: dve.wait_ge(s_p, b * PST + i)
                    for g in range(2):
                        ins = dve.tensor_scalar(qz[:, g, 16 * g:16 * g + 16].rearrange("p (h t) -> p h t", t=TS),
                                                k.pT[:, HPG * g:HPG * (g + 1), bass.ds(TP + b * TS, TS)], SCALE, None, ALU.mult)
                    step(ins)
                    p(1)
                    ps = k.bank[0][0:R, :]
                    dve.tensor_tensor(s_s[:, PAST:S], ps[:, 128:128 + TS], b_new[:, :], ALU.add)
                    dve.tensor_tensor(s_w[:, WINL:W], ps[:, 128 + TS:128 + 2 * TS], b_w[:, WINL:W], ALU.add)
                    inner(dve.tensor_tensor(s_c[:, 0:NCS], ps[:, 0:NCS], b_c[:, 0:NCS], ALU.add))
                    step(dve.tensor_reduce(mx[:, 0:1], s_c[:, 0:NCS], AX.X, ALU.max, negate=True))
                    p(2)
                    for ch in range(4):
                        if ch == 2:
                            p(3)
                        two = lambda v: v.rearrange("p (a n) -> p a n", n=TP)
                        ins = dve.tensor_tensor(two(s_s[:, ch * 512:(ch + 1) * 512]), two(k.bank[3 + ch % 2][0:R, :]),
                                                b_s[:, 2 * ch:2 * ch + 2, :], ALU.add)
                        if ch < 3:
                            step(ins)
                        else:
                            inner(dve.tensor_tensor(s_w[:, 0:WINL], k.bank[5][0:R, :], b_w[:, 0:WINL], ALU.add))
                            step(dve.tensor_reduce(mx[:, 1:2], s_w[:, :], AX.X, ALU.max, negate=True))
                    dve.wait_ge(s_a, b * 3 + 1)
                    inner(dve.reciprocal(fac[:, 0:1], sm[:, 0:1]))
                    inner(dve.tensor_scalar(p_c[:, 0:NCS], s_c[:, 0:NCS], fac[:, 0:1], None, ALU.mult))
                    gate = lambda r: k.sgates[:, bass.ds(b, 1), r:r + 1].rearrange("p o r -> p (o r)")
                    step(dve.tensor_scalar(s_c[:, 0:NCS], p_c[:, 0:NCS], gate(0), None, ALU.mult))
                    p(4)
                    inner(dve.tensor_copy(pto[0:NCS, 0:2, :].rearrange("p a r -> p (a r)"), k.bank[7][0:NCS, 0:2 * R]))
                    inner(dve.tensor_reduce(psg[0:NCS, :].rearrange("p (g t) -> p g t", g=2),
                                            pto[0:NCS, 0, :].rearrange("p (g h t) -> p g t h", g=2, h=HPG), AX.X, ALU.add))
                    step(dve.tensor_copy(psb[0:NCS, :, :, :], psg[0:NCS, :].rearrange("p (g t) -> p g t", g=2).unsqueeze(2)
                                         .to_broadcast([NCS, GROUPS, HPG, TS])))
                    p(5)
                    inner(dve.tensor_tensor(imp[:, :], ps[:, 160:160 + NSEL], forced[:, :], ALU.add))
                    mine = imp[:, :].unsqueeze(2).to_broadcast([R, NSEL, NSEL])
                    other = imp[:, :].unsqueeze(1).to_broadcast([R, NSEL, NSEL])
                    dve.tensor_tensor(cmpx[:, :, :], other, mine, ALU.is_gt)
                    inner(dve.tensor_tensor(cmpe[:, :, :], other, mine, ALU.is_equal))
                    inner(dve.tensor_tensor(cmpe[:, :, :], cmpe[:, :, :], before[:, :, :], ALU.mult))
                    inner(dve.tensor_tensor(cmpx[:, :, :], cmpx[:, :, :], cmpe[:, :, :], ALU.add))
                    inner(dve.tensor_reduce(drop[:, :], cmpx[:, :, :], AX.X, ALU.add))
                    inner(dve.tensor_scalar(drop[:, :], drop[:, :], TOPK - 0.5, NEG, ALU.is_gt, ALU.mult))
                    past = s_s[:, 0:PAST].rearrange("p (j s) -> p j s", s=SELB)
                    inner(dve.tensor_tensor(past, past, drop[:, 0:NSEL - 1].unsqueeze(2).to_broadcast([R, NSEL - 1, SELB]),
                                            ALU.add))
                    step(dve.tensor_reduce(mx[:, 2:3], s_s[:, :], AX.X, ALU.max, negate=True))
                    dve.wait_ge(s_a, b * 3 + 3)
                    dve.reciprocal(fac[:, 1:2], sm[:, 1:2])
                    inner(dve.reciprocal(fac[:, 2:3], sm[:, 2:3]))
                    dve.tensor_scalar(s_w[:, :], s_w[:, :], fac[:, 1:2], gate(2), ALU.mult, ALU.mult)
                    step(dve.tensor_scalar(s_s[:, :], s_s[:, :], fac[:, 2:3], gate(1), ALU.mult, ALU.mult))
                    p(6)
                    dve.tensor_copy(pts[:, :, :].rearrange("p j r -> p (j r)"), k.bank[6][:, :])
                    dve.tensor_copy(pto[0:TS, 2:4, :].rearrange("p a r -> p (a r)"), k.bank[7][0:TS, 2 * R:4 * R])
                    step(dve.tensor_copy(pto[:, 4:8, :].rearrange("p a r -> p (a r)"), k.bank[7][:, 4 * R:8 * R]))
                    p(7)
                    step(dve.tensor_copy(orow[:, :], k.bank[5][:, 0:KVW]))
                    p(8)
                    for g in range(2):
                        hd = slice(HPG * g, HPG * (g + 1))
                        ins = dve.tensor_scalar(k.mixT[:, hd, bass.ds(TP + b * TS, TS)],
                                                k.bank[6][:, g * R + 16 * g:g * R + 16 * g + 16]
                                                .rearrange("p (h t) -> p h t", t=TS), 1.0, None, ALU.mult)
                    step(ins)
                    assert (step.n, inner.n) == (VST, IN), (step.n, inner.n)
                with dve.Fori(0, NB) as b:
                    body(b)


def phase_out(k, A):
    nc = k.nc
    CH = 512
    N_CH = D // CH
    with ExitStack() as c:
        w = [k.sb(f"w_out{i}", [P, KT, CH], F32, c) for i in range(2)]
        part = k.sb("gated", [P, 2, NS], F32, c)
        s_w = [k.sem(f"o_w_landed{i}") for i in range(2)]
        s_tile = k.sem("o_tile_multiplied")
        s_add = k.sem("o_tile_added")
        w_view = A["w_out"][0].rearrange("(k p) n -> p k n", p=P)
        with nc.Block() as block:
            @block.sync
            def _(sp):
                for n in range(N_CH):
                    if n >= 2:
                        sp.wait_ge(s_tile, 4 * (n - 1))
                    sp.dma_start(w[n % 2][:, :, :], w_view[:, :, n * CH:(n + 1) * CH]).then_inc(s_w[n % 2], 16)

            @block.tensor
            def _(pe):
                for m in range(KT):
                    n = m // 4
                    if m % 4 == 0:
                        pe.wait_ge(s_w[n % 2], 16 * (n // 2 + 1))
                    if m >= 4:
                        pe.wait_ge(s_add, m - 3)
                    for t in range(KT):
                        ins = pe.matmul(k.bank[m % 4][:, 0:NT], w[n % 2][:, t, (m % 4) * P:(m % 4 + 1) * P],
                                        k.mixT[:, t, :], start=(t == 0), stop=(t == KT - 1))
                    ins.then_inc(s_tile, 1)

            @block.vector
            def _(dve):
                inner = k.steps.chain(dve)
                for m in range(KT):
                    dve.wait_ge(s_tile, m + 1)
                    ps = k.bank[m % 4]
                    add_gated(k, dve, inner, m, ps[:, 0:TP], ps[:, TP:NT], 32, part[:, m % 2, :]).then_inc(s_add, 1)


def add_gated(k, dve, inner, m, prompt, sample, gate, part):
    by_t = lambda v: v.rearrange("p (b t) -> p b t", t=TS)
    dve.scalar_tensor_tensor(out=k.xT[:, m, 0:TP], in0=prompt, scalar=k.mod[:, gate + m, 0:1], in1=k.xT[:, m, 0:TP],
                             op0=ALU.mult, op1=ALU.add)
    inner(dve.tensor_tensor(by_t(part), by_t(sample), k.mod[:, gate + m, 1:NC].unsqueeze(2).to_broadcast([P, NB, TS]),
                            ALU.mult))
    return dve.tensor_tensor(k.xT[:, m, TP:NT], k.xT[:, m, TP:NT], part, ALU.add)


NGRP, NEXP, EPG = 4, 32, 8
SLOTS = 64
N_OVER = 2 * NT // SLOTS - 1
N_BLK = NEXP + N_OVER
NTT = len(ROWS)


def phase_route(k, A):
    nc = k.nc
    NL = NGRP + NEXP
    with ExitStack() as c:
        sb = lambda name, shape, dt=F32: k.sb(name, shape, dt, c)
        w = sb("w_router", [P, KT, NL])
        bias = sb("router_bias", [P, NL])
        L = sb("logits", [P, NTT, NL])
        tri = sb("earlier", [P, P])
        im = sb("expert_minus_99", [P, NEXP])
        cand, oh, oh2 = sb("candidates", [P, NTT, NEXP]), sb("one_hot1", [P, NTT, NEXP]), sb("one_hot2", [P, NTT, NEXP])
        le, M = sb("expert_logits", [P, NTT, NEXP]), sb("chosen", [P, NTT, NEXP])
        gd, goh = sb("group_logits", [P, NTT, NGRP]), sb("group_one_hot", [P, NTT, NGRP])
        r1 = sb("route_scalars", [P, NTT, 8])
        rank, wt = sb("rank", [P, NTT, NEXP]), sb("route_weights", [P, NTT, NEXP])
        nb, cum, excl = sb("extra_blocks", [P, NEXP]), sb("extra_cum", [P, NEXP]), sb("extra_tmp", [P, NEXP])
        ind, pick = sb("extra_ind", [P, N_OVER, NEXP]), sb("extra_pick", [P, N_OVER, NEXP])
        ex, onum = sb("extra_scalars", [P, 4, N_OVER]), sb("extra_number", [P, N_OVER])
        ef = sb("expert_float", [P, N_BLK + 1])
        s_w, s_i, s_rows = k.sem("r_weights_landed"), k.sem("r_constants"), k.sem("r_rows_copied")
        s_l, s_e, s_rank, s_p = (k.sem("r_logits"), k.sem("r_exps"), k.sem("r_ranks"),
                                      k.sem("r_rows_transposed"))
        s_v1, s_v2, s_m = k.sem("r_group_max"), k.sem("r_best_two"), k.sem("r_chosen")
        with nc.Block() as block:
            @block.sync
            def _(sp):
                load_expert(k, A, sp, 0)
                with nc.allow_non_contiguous_dma(reason="small router weights"):
                    sp.dma_start(w[:, :, 0:NGRP], A["w_router_group"][0].rearrange("(k p) n -> p k n", p=P)).then_inc(s_w, 16)
                    sp.dma_start(w[:, :, NGRP:NL], A["w_router_expert"][0].rearrange("(k p) n -> p k n", p=P)).then_inc(s_w, 16)
                sp.wait_ge(s_i, 1)
                sp.dma_start(bias[0:1, 0:NGRP], A["b_router_group"]).then_inc(s_w, 16)
                sp.dma_start(bias[0:1, NGRP:NL], A["b_router_expert"]).then_inc(s_w, 16)

            @block.gpsimd
            def _(pool):
                f = dict(allow_small_or_imprecise_dtypes=True)
                pool.memset(bias[:, :], 0.0).then_inc(s_i, 1)
                pool.memset(L[:, :, :], 0.0).then_inc(s_i, 1)
                pool.memset(rank[:, :, :], 0.0).then_inc(s_i, 1)
                pool.memset(k.acc[:, :, :], 0.0).then_inc(s_i, 1)
                pool.memset(k.slot[:, :, N_BLK:N_BLK + 2], 0.0).then_inc(s_i, 1)
                pool.memset(k.weight[:, :, N_BLK:N_BLK + 2], 0.0).then_inc(s_i, 1)
                pool.iota(im[:, :], pattern=[[1, NEXP]], base=-99, channel_multiplier=0, **f).then_inc(s_i, 1)
                pool.iota(k.slots[:, :], pattern=[[1, SLOTS]], base=0, channel_multiplier=0, **f).then_inc(s_i, 1)
                pool.iota(onum[:, :], pattern=[[1, N_OVER]], base=0, channel_multiplier=0, **f).then_inc(s_i, 1)
                pool.iota(ef[:, 0:NEXP], pattern=[[1, NEXP]], base=0, channel_multiplier=0, **f).then_inc(s_i, 1)
                pool.affine_select(out=tri[:, :], in_=k.ones[:, :], compare_op=ALU.is_gt, fill=0.0, base=0,
                                   pattern=[[1, P]], channel_multiplier=-1).then_inc(s_i, 1)

            @block.tensor
            def _(pe):
                for n in range(4 * NTT):
                    i, q = divmod(n, 4)
                    at, r = ROWS[i]
                    if n >= 4:
                        pe.wait_ge(s_rows, n - 3)
                    for j in range(4):
                        ins = pe.transpose(k.bank[4 + n % 4][0:r, j * P:(j + 1) * P], k.h2T[:, 4 * q + j, at:at + r],
                                           k.ident[:, :])
                    ins.then_inc(s_p, 1)
                pe.wait_ge(s_w, 64)
                for i, (at, r) in enumerate(ROWS):
                    pe.matmul(k.bank[i][0:r, 0:NL], k.ones[:, 0:r], bias[:, :], start=True, stop=False)
                    for t in range(KT):
                        ins = pe.matmul(k.bank[i][0:r, 0:NL], k.h2T[:, t, at:at + r], w[:, t, :], start=False,
                                        stop=(t == KT - 1))
                    ins.then_inc(s_l, 1)
                pe.wait_ge(s_m, 1)
                for i, (_, r) in enumerate(ROWS):
                    out = k.bank[3][0:r, i * NEXP:(i + 1) * NEXP]
                    for j in range(i):
                        pe.matmul(out, k.ones[:, 0:r], M[:, j, :], start=(j == 0), stop=False)
                    pe.matmul(out, tri[0:r, 0:r], M[0:r, i, :], start=(i == 0), stop=True)
                for i, (_, r) in enumerate(ROWS):
                    ins = pe.matmul(k.bank[0][:, 64:64 + NEXP], k.ones[0:r, :], M[0:r, i, :], start=(i == 0),
                                    stop=(i == NTT - 1))
                ins.then_inc(s_rank, 1)

            @block.scalar
            def _(act):
                for n in range(4 * NTT):
                    i, q = divmod(n, 4)
                    r = ROWS[i][1]
                    act.wait_ge(s_p, n + 1)
                    act.copy(k.h2rows[0:r, i, q * 512:(q + 1) * 512], k.bank[4 + n % 4][0:r, :]).then_inc(s_rows, 1)
                act.wait_ge(s_v1, 1)
                act.activation(cand[:, :, 0:NGRP], gd[:, :, :], ACT.Exp).then_inc(s_e, 1)
                act.wait_ge(s_v2, 1)
                act.activation(r1[:, :, 4:5], r1[:, :, 3:4], ACT.Exp).then_inc(s_e, 1)

            @block.vector
            def _(dve):
                step = k.steps.chain(dve)
                tt = lambda out, a, b, op: step(dve.tensor_tensor(out, a, b, op))
                ts = lambda out, a, s1, s2, o1, o2=None: step(dve.tensor_scalar(out, a, s1, s2, o1, o2) if o2 else
                                                              dve.tensor_scalar(out, a, s1, s2, o1))
                red = lambda out, a, op: step(dve.tensor_reduce(out, a, AX.X, op))
                wide = lambda col, n: col.to_broadcast([P, NTT, n])
                imw = lambda n: im[:, 0:n].unsqueeze(1).to_broadcast([P, NTT, n])

                def first_best(src, out, n, best, at):
                    tt(out, src, wide(best, n), ALU.is_equal)
                    tt(out, out, imw(n), ALU.mult)
                    red(r1[:, :, at:at + 1], out, ALU.min)
                    tt(out, imw(n), wide(r1[:, :, at:at + 1], n), ALU.is_equal)
                dve.wait_ge(s_i, 11)
                for i, (_, r) in enumerate(ROWS):
                    dve.wait_ge(s_l, i + 1)
                    step(dve.tensor_copy(L[0:r, i, :], k.bank[i][0:r, 0:NL]))
                red(r1[:, :, 0:1], L[:, :, 0:NGRP], ALU.max)
                dve.tensor_tensor(gd[:, :, :], L[:, :, 0:NGRP], wide(r1[:, :, 0:1], NGRP), ALU.subtract).then_inc(s_v1, 1)
                first_best(L[:, :, 0:NGRP], goh[:, :, :], NGRP, r1[:, :, 0:1], 1)
                ts(goh[:, :, :], goh[:, :, :], -NEG, NEG, ALU.mult, ALU.add)
                for i in range(NTT):
                    tt(le[:, i, :].rearrange("p (g e) -> p g e", e=EPG), L[:, i, NGRP:NL].rearrange("p (g e) -> p g e", e=EPG),
                       goh[:, i, :].unsqueeze(2).to_broadcast([P, NGRP, EPG]), ALU.add)
                red(r1[:, :, 2:3], le[:, :, :], ALU.max)
                first_best(le[:, :, :], oh[:, :, :], NEXP, r1[:, :, 2:3], 1)
                step(dve.scalar_tensor_tensor(out=le[:, :, :], in0=oh[:, :, :], scalar=2.0 * NEG, in1=le[:, :, :],
                                              op0=ALU.mult, op1=ALU.add))
                red(r1[:, :, 3:4], le[:, :, :], ALU.max)
                first_best(le[:, :, :], oh2[:, :, :], NEXP, r1[:, :, 3:4], 1)
                dve.tensor_tensor(r1[:, :, 3:4], r1[:, :, 3:4], r1[:, :, 2:3], ALU.subtract).then_inc(s_v2, 1)
                dve.tensor_tensor(M[:, :, :], oh[:, :, :], oh2[:, :, :], ALU.add).then_inc(s_m, 1)
                dve.wait_ge(s_e, 2)
                red(r1[:, :, 5:6], cand[:, :, 0:NGRP], ALU.add)
                ts(r1[:, :, 6:7], r1[:, :, 4:5], 1.0, None, ALU.add)
                tt(r1[:, :, 5:6], r1[:, :, 5:6], r1[:, :, 6:7], ALU.mult)
                step(dve.reciprocal(r1[:, :, 6:7], r1[:, :, 5:6]))
                tt(r1[:, :, 7:8], r1[:, :, 6:7], r1[:, :, 4:5], ALU.mult)
                tt(oh[:, :, :], oh[:, :, :], wide(r1[:, :, 6:7], NEXP), ALU.mult)
                tt(oh2[:, :, :], oh2[:, :, :], wide(r1[:, :, 7:8], NEXP), ALU.mult)
                tt(wt[:, :, :], oh[:, :, :], oh2[:, :, :], ALU.add)
                dve.wait_ge(s_rank, 1)
                for i, (_, r) in enumerate(ROWS):
                    step(dve.scalar_tensor_tensor(out=rank[0:r, i, :], in0=k.bank[3][0:r, i * NEXP:(i + 1) * NEXP],
                                                  scalar=1.0, in1=M[0:r, i, :], op0=ALU.add, op1=ALU.mult))
                ts(rank[:, :, :], rank[:, :, :], 1.0, None, ALU.subtract)
                step(dve.tensor_copy(k.slot[:, :, 0:NEXP], rank[:, :, :]))
                step(dve.tensor_copy(k.weight[:, :, 0:NEXP], wt[:, :, :]))
                cnt = k.bank[0][:, 64:64 + NEXP]
                ts(nb[:, :], cnt, SLOTS + 0.5, None, ALU.is_gt)
                for j in range(2, (NT - 1) // SLOTS + 1):
                    step(dve.scalar_tensor_tensor(out=nb[:, :], in0=cnt, scalar=j * SLOTS + 0.5, in1=nb[:, :], op0=ALU.is_gt,
                                                  op1=ALU.add))
                step(dve.tensor_copy(cum[:, :], nb[:, :]))
                for s in (1, 2, 4, 8, 16):
                    step(dve.tensor_copy(excl[:, :], cum[:, :]))
                    tt(cum[:, s:NEXP], excl[:, s:NEXP], excl[:, 0:NEXP - s], ALU.add)
                step(dve.tensor_copy(ef[:, N_BLK:N_BLK + 1], cum[:, NEXP - 1:NEXP]))
                over = slice(NEXP, N_BLK)
                by_o = lambda v: v.unsqueeze(1).to_broadcast([P, N_OVER, NEXP])
                by_e = lambda v: v.unsqueeze(2).to_broadcast([P, N_OVER, NEXP])
                tt(ind[:, :, :], by_o(cum[:, :]), by_e(onum[:, :]), ALU.is_le)
                red(ex[:, 0, :], ind[:, :, :], ALU.add)
                tt(pick[:, :, :], ind[:, :, :], by_o(nb[:, :]), ALU.mult)
                red(ex[:, 1, :], pick[:, :, :], ALU.add)
                ts(ex[:, 2, :], ex[:, 0, :], NEXP - 0.5, 1.0e3, ALU.is_gt, ALU.mult)
                tt(ex[:, 3, :], onum[:, :], ex[:, 1, :], ALU.subtract)
                ts(ex[:, 3, :], ex[:, 3, :], float(SLOTS), float(SLOTS), ALU.mult, ALU.add)
                tt(ex[:, 3, :], ex[:, 3, :], ex[:, 2, :], ALU.add)
                ts(ef[:, over], ex[:, 0, :], float(NEXP - 1), None, ALU.min)
                tt(pick[:, :, :], by_o(ef[:, 0:NEXP]), by_e(ef[:, over]), ALU.is_equal)
                for i in range(NTT):
                    for table, dst in ((rank, k.slot), (wt, k.weight)):
                        tt(ind[:, :, :], pick[:, :, :], by_o(table[:, i, :]), ALU.mult)
                        red(dst[:, i, over], ind[:, :, :], ALU.add)
                tt(k.slot[:, :, over], k.slot[:, :, over], ex[:, 3, :].unsqueeze(1).to_broadcast([P, NTT, N_OVER]),
                   ALU.subtract)
                step(dve.tensor_copy(k.expert[:, :], ef[0:1, :]))


DE = 512
CK = 8


def expert_buffers(k, c):
    k.wg = [k.sb(f"gate_w{i}", [P, CK, DE], F32, c) for i in range(2)]
    k.wu = [k.sb(f"up_w{i}", [P, CK, DE], F32, c) for i in range(2)]
    k.wd = [k.sb(f"down_w{i}", [P, 2, D], F32, c) for i in range(2)]
    k.s_we = [k.sem(f"u_w_landed{i}") for i in range(6)]


def load_expert(k, A, sp, e, free=None):
    g_v, u_v, d_v = (v[0, bass.ds(e, 1)].rearrange("o (k p) n -> p (o k) n", p=P)
                     for v in (A["w_gate"], A["w_up"], A["w_down"]))
    for i in range(2):
        if free:
            free(i)
        sp.dma_start(k.wg[i][:, :, :], g_v[:, i * CK:(i + 1) * CK, :]).then_inc(k.s_we[2 * i], 16)
        sp.dma_start(k.wu[i][:, :, :], u_v[:, i * CK:(i + 1) * CK, :]).then_inc(k.s_we[2 * i + 1], 16)
    for i in range(2):
        if free:
            free(2 + i)
        sp.dma_start(k.wd[i][:, :, :], d_v[:, 2 * i:2 * i + 2, :]).then_inc(k.s_we[4 + i], 16)


def phase_moe(k, A):
    nc = k.nc
    with ExitStack() as c:
        sb = lambda name, shape, dt=F32: k.sb(name, shape, dt, c)
        wg, wu, wd, s_w = k.wg, k.wu, k.wd, k.s_we
        sel = sb("select", [P, NTT, 2, SLOTS])
        give = sb("give", [P, NTT, 2, 2, SLOTS])
        giveT = sb("giveT", [P, 2, NT])
        x = sb("x_picked", [P, KT, P])
        h = sb("hidden", [P, 2, 256])
        hT = sb("hiddenT", [P, 2, 2, P])
        y = sb("y_rows", [P, 2, D // 2])
        s_half = k.sem("u_half_gate_up")
        s_gu = k.sem("u_gate_up")
        s_yh = k.sem("u_half_y")
        s_y = k.sem("u_y_made")
        s_sel = k.sem("u_selected")
        s_x, s_xc = k.sem("u_x_picked"), k.sem("u_x_copied")
        s_silu, s_h = k.sem("u_silu"), k.sem("u_hidden")
        s_ht, s_htc = k.sem("u_hidden_transposed"), k.sem("u_hiddenT_copied")
        s_gt, s_gtc = k.sem("u_give_transposed"), k.sem("u_giveT_copied")
        s_yc = k.sem("u_y_copied")
        s_c, s_cc = k.sem("u_given_back"), k.sem("u_added")
        bank = k.bank
        XB = (7, 3)
        YB = ((5, 6), (3, 4))
        GB = ((5, 6), (3, 4))
        WB = (0, 7)

        def both(eng, turn, last=None):
            def run(lo, hi):
                turn(lo, lo == 0, False)
                with eng.Fori(lo + 1, hi) as n:
                    turn(n, False, True)
                if last:
                    last(hi)
            run(0, NEXP // 2)
            with eng.If(eng.value_load(k.expert[0:1, N_BLK:N_BLK + 1], min_val=0, max_val=N_OVER) > 0):
                run(NEXP // 2, N_BLK // 2)

        with nc.Block() as block:
            @block.sync
            def _(sp):
                def turn(n, fresh, before):
                    for b in range(2):
                        if fresh and b == 0:
                            continue
                        e = sp.value_load(k.expert[0:1, bass.ds(2 * n + b, 1)], min_val=0, max_val=NEXP - 1)
                        load_expert(k, A, sp, e, lambda i: sp.wait_ge((s_half, s_gu, s_yh, s_y)[i], 2 * n + b))
                both(sp, turn)

            @block.tensor
            def _(pe):
                def give_back(n):
                    pe.wait_ge(s_yc, 4 * n + 4)
                    for s in range(8):
                        if s >= 2:
                            pe.wait_ge(s_cc, 16 * n + 2 * (s - 1))
                        for b in range(2):
                            for dh in range(2):
                                rows = slice(64 * dh, 64 * dh + 64)
                                ins = pe.matmul(bank[GB[s % 2][dh]][:, 0:NT], y[rows, b, s * P:(s + 1) * P],
                                                giveT[rows, b, :], start=(b == 0), stop=(b == 1))
                        ins.then_inc(s_c, 1)

                def pick(m, fresh):
                    pe.wait_ge(s_sel, m + 1)
                    if not fresh:
                        pe.wait_ge(s_gtc, 2 * m)
                    for q in range(4):
                        if q >= 2:
                            pe.wait_ge(s_xc, 4 * m + q - 1)
                        for j in range(4):
                            t = 4 * q + j
                            for i, (_, r) in enumerate(ROWS):
                                ins = pe.matmul(bank[XB[q % 2]][:, j * P:(j + 1) * P], k.h2rows[0:r, i, t * P:(t + 1) * P],
                                                sel[0:r, i, :, :].rearrange("p b s -> p (b s)"), start=(i == 0),
                                                stop=(i == NTT - 1))
                        ins.then_inc(s_x, 1)

                def gate_up(n, b):
                    for t in range(KT):
                        i = t // CK
                        if b == 0 and t % 4 == 0:
                            pe.wait_ge(s_xc, 4 * n + t // 4 + 1)
                        if t % CK == 0:
                            for w in range(2):
                                pe.wait_ge(s_w[2 * i + w], 16 * (2 * n + b + 1))
                        for w, col in ((wg, 0), (wu, 256)):
                            for half in range(2):
                                ins = pe.matmul(bank[b][64 * half:64 * half + 64, col:col + 256],
                                                x[:, t, b * 64:b * 64 + 64],
                                                w[i][:, t % CK, half * 256:half * 256 + 256],
                                                start=(t == 0 and w is wg), stop=(t == KT - 1 and w is wu))
                        if t == CK - 1:
                            ins.then_inc(s_half, 1)
                        if t == KT - 1:
                            ins.then_inc(s_gu, 1)

                def turn_hidden(n, b):
                    pe.wait_ge(s_h, 2 * n + b + 1)
                    for cc in range(2):
                        ins = pe.transpose(bank[2][:, (2 * b + cc) * P:(2 * b + cc + 1) * P], h[:, b, cc * P:(cc + 1) * P],
                                           k.ident[:, :])
                    ins.then_inc(s_ht, 1)

                def down(n, b):
                    pe.wait_ge(s_htc, 2 * n + b + 1)
                    for f in range(4):
                        half, cc = divmod(f, 2)
                        if cc == 0:
                            pe.wait_ge(s_w[4 + half], 16 * (2 * n + b + 1))
                        for j in range(2):
                            for dh in range(2):
                                at = dh * (D // 2) + j * 512
                                ins = pe.matmul(bank[YB[b][j]][64 * dh:64 * dh + 64, :],
                                                hT[:, b, cc, half * 64:half * 64 + 64], wd[half][:, cc, at:at + 512],
                                                start=(f == 0), stop=(f == 3))
                        if f == 1:
                            ins.then_inc(s_yh, 1)
                    ins.then_inc(s_y, 1)

                def turn(n, fresh, before):
                    if not fresh:
                        pe.wait_ge(s_gtc, 2 * n)
                    gate_up(n, 0)
                    if before:
                        give_back(n - 1)
                    turn_hidden(n, 0)
                    for b in range(2):
                        for i, (at, r) in enumerate(ROWS):
                            ins = pe.transpose(bank[WB[b]][:, at:at + r], give[0:r, i, b, :, :].rearrange("p a s -> p (a s)"),
                                               k.ident[0:r, 0:r])
                        ins.then_inc(s_gt, 1)
                    if not fresh:
                        pe.wait_ge(s_cc, 16 * n)
                    down(n, 0)
                    gate_up(n, 1)
                    pick(n + 1, False)
                    turn_hidden(n, 1)
                    pe.wait_ge(s_xc, 4 * n + 8)
                    down(n, 1)
                pick(0, True)
                both(pe, turn, lambda pairs: give_back(pairs - 1))

            @block.scalar
            def _(act):
                def picked(m):
                    for q in range(4):
                        act.wait_ge(s_x, 4 * m + q + 1)
                        act.copy(x[:, 4 * q:4 * q + 4, :], bank[XB[q % 2]][:, :].rearrange("p (a s) -> p a s", a=4))\
                           .then_inc(s_xc, 1)

                def turn(n, fresh, before):
                    for b in range(2):
                        act.wait_ge(s_gu, 2 * n + b + 1)
                        if not fresh:
                            act.wait_ge(s_ht, 2 * n - 1 + b)
                        act.activation(h[:, b, :], bank[b][:, 0:256], ACT.Silu).then_inc(s_silu, 1)
                        if b == 1:
                            picked(n + 1)
                        elif not fresh:
                            act.wait_ge(s_c, 8 * n)
                        if b == 0:
                            for w in range(2):
                                act.wait_ge(s_gt, 2 * n + w + 1)
                                act.copy(giveT[:, w, :], bank[WB[w]][:, 0:NT]).then_inc(s_gtc, 1)
                        act.wait_ge(s_y, 2 * n + b + 1)
                        for j in range(2):
                            act.copy(y[:, b, j * 512:(j + 1) * 512], bank[YB[b][j]][:, :]).then_inc(s_yc, 1)
                picked(0)
                both(act, turn)

            @block.vector
            def _(dve):
                def select(n):
                    for b in range(2):
                        col = 2 * n + b
                        for i, (_, r) in enumerate(ROWS):
                            slot = k.slot[0:r, i, bass.ds(col, 1)]
                            wt = k.weight[0:r, i, bass.ds(col, 1)]
                            dve.tensor_scalar(sel[0:r, i, b, :], k.slots[0:r, :], slot, None, ALU.is_equal)
                            for d in range(2):
                                ins = dve.tensor_scalar(give[0:r, i, b, d, :], k.slots[0:r, :], slot, wt, ALU.is_equal,
                                                        ALU.mult)
                    ins.then_inc(s_sel, 1)

                def add(n):
                    for s in range(8):
                        dve.wait_ge(s_c, 8 * n + s + 1)
                        for dh in range(2):
                            a = k.acc[:, 8 * dh + s, :]
                            dve.tensor_tensor(a, a, bank[GB[s % 2][dh]][:, 0:NT], ALU.add).then_inc(s_cc, 1)

                def turn(n, fresh, before):
                    for b in range(2):
                        dve.wait_ge(s_silu, 2 * n + b + 1)
                        dve.tensor_tensor(h[:, b, :], h[:, b, :], bank[b][:, 256:512], ALU.mult).then_inc(s_h, 1)
                        if b == 0 and before:
                            add(n - 1)
                        dve.wait_ge(s_ht, 2 * n + b + 1)
                        if not fresh:
                            dve.wait_ge(s_y, 2 * n - 1 + b)
                        dve.tensor_copy(hT[:, b, :, :], bank[2][:, b * 256:(b + 1) * 256].rearrange("p (a s) -> p a s", a=2))\
                           .then_inc(s_htc, 1)
                        if b == 0:
                            dve.wait_ge(s_gt, 2 * n + 2)
                            select(n + 1)
                select(0)
                both(dve, turn, lambda pairs: add(pairs - 1))


def phase_final(k, A):
    nc = k.nc
    with ExitStack() as c:
        sb = lambda name, shape, dt=F32: k.sb(name, shape, dt, c)
        sq, part = sb("f_squares", [P, KT, NT]), sb("f_gated", [P, 2, NS])
        rstd, sd = sb("f_rstd", [P, NT]), sb("f_root", [P, NT])
        rows = k.h2rows
        s_q, s_s, s_sd = k.s_norm
        before = k.norms
        s_n = k.sem("f_normed")
        s_t, s_o = k.sem("f_transposed"), k.sem("f_out")
        s_r = [k.sem("f_rows_act"), k.sem("f_rows_dve")]
        with nc.Block() as block:
            def copies(eng, copy, parity):
                for n in range(parity, 4 * NTT, 2):
                    i, q = divmod(n, 4)
                    r = ROWS[i][1]
                    eng.wait_ge(s_t, n + 1)
                    copy(rows[0:r, i, q * 512:(q + 1) * 512], k.bank[1 + n % 4][0:r, :]).then_inc(s_r[parity], 1)

            @block.vector
            def _(dve):
                step = k.steps.chain(dve)
                for m in range(KT):
                    step(add_gated(k, dve, step, m, k.acc[:, m, 0:TP], k.acc[:, m, TP:NT], 80, part[:, m % 2, :]))
                    dve.tensor_tensor(sq[:, m, :], k.xT[:, m, :], k.xT[:, m, :], ALU.mult).then_inc(s_q, 1)
                dve.wait_ge(s_sd, before + 1)
                step(dve.reciprocal(rstd[:, :], sd[:, :]))
                for m in range(KT):
                    dve.scalar_tensor_tensor(out=k.acc[:, m, :], in0=k.xT[:, m, :], scalar=k.par[:, C_NORMF + m:C_NORMF + m + 1],
                                             in1=rstd[:, :], op0=ALU.mult, op1=ALU.mult).then_inc(s_n, 1)
                copies(dve, dve.tensor_copy, 1)

            @block.tensor
            def _(pe):
                for t in range(KT):
                    pe.wait_ge(s_q, before * KT + t + 1)
                    ins = pe.matmul(k.bank[0][:, 0:NT], k.ones[:, :], sq[:, t, :], start=(t == 0), stop=(t == KT - 1))
                ins.then_inc(s_s, 1)
                for n in range(4 * NTT):
                    i, q = divmod(n, 4)
                    at, r = ROWS[i]
                    if n < 4:
                        pe.wait_ge(s_n, 4 * (n + 1))
                    else:
                        pe.wait_ge(s_r[n % 2], n // 2 - 1)
                    for j in range(4):
                        ins = pe.transpose(k.bank[1 + n % 4][0:r, j * P:(j + 1) * P], k.acc[:, 4 * q + j, at:at + r],
                                           k.ident[:, :])
                    ins.then_inc(s_t, 1)

            @block.scalar
            def _(act):
                act.wait_ge(s_s, before + 1)
                act.activation(sd[:, :], k.bank[0][:, 0:NT], ACT.Sqrt, bias=k.eps[:, 0:1], scale=1.0 / D)\
                   .then_inc(s_sd, 1)
                copies(act, act.copy, 0)

            @block.sync
            def _(sp):
                out = (A["y_prompt"][0, 0:P, :], A["y_prompt"][0, P:TP, :], A["y_sample"].rearrange("b t d -> (b t) d"))
                for i, (_, r) in enumerate(ROWS):
                    for p in range(2):
                        sp.wait_ge(s_r[p], 2 * (i + 1))
                    sp.dma_start(out[i], rows[0:r, i, :]).then_inc(s_o, 16)
                sp.wait_ge(s_o, 16 * NTT)


def step_kernel(nc, A):
    with ExitStack() as ctx:
        k = persistent(nc, ctx)
        k.kc_dram = nc.dram_tensor("kc_scratch", [P, NB, 2 * NCS], F32, kind="Internal")
        k.vc_dram = nc.dram_tensor("vc_scratch", [NCS, NB, KVW], F32, kind="Internal")
        phase_start(k, A)
        k.bonus, k.y = k.mixT[:, RT:KT, :], k.mixT[:, 0:RT, :]
        with ExitStack() as mid:
            k.pT = k.sb("pT", [P, RKV_TILE, NX], F32, mid)
            k.gates = k.sb("gates", [P, len(ROWS), 24], F32, mid)
            k.sgates = k.sb("sample_gates", [NS, NB, 3], F32, mid)
            k.gate_dram = nc.dram_tensor("gate_scratch", [NS, 24], F32, kind="Internal")
            rw = mid.enter_context(ExitStack())
            k.rkvT = k.sb("rkvT", [P, 3 * RT, NX], F32, rw)
            with ExitStack() as hh:
                k.hT = hh.enter_context(nc.sbuf_tensor("sb_hT", [P, KT, NX], F32, side="right"))
                ahead = hh.enter_context(ExitStack())
                k.w_in = [k.sb(f"w_in{i}", [P, KT, 512], F32, ahead) for i in range(2)]
                k.s_w_in = [k.sem(f"c_w_landed{i}") for i in range(2)]
                phase_norm1(k, A)
                phase_in(k, A)
                ahead.close()
                k.dec, k.a, k.g = (k.sb(n, [P, RT, NT], F32, rw) for n in ("dec", "a_rate", "g_gate"))
                phase_lora(k, A)
            k.kk = k.sb("kk", [P, RT, NT], F32, rw)
            phase_rkv(k, A)
            phase_scan(k, A)
            phase_groupnorm(k, A)
            rw.close()
            with ExitStack() as own:
                k.kcTp, k.vcp = k.sb("kcT_prompt", [P, 2 * NCP], F32, own), k.sb("vc_prompt", [NCP, KVW], F32, own)
                k.kvrows = k.sb("kvrows", [P, len(ROWS), 3 * ROW], F32, own)
                k.zero_rows = k.sb("zero_rows", [P, ROW], F32, own)
                k.cp_w1, k.cp_w2 = k.sb("cp_w1", [P, 2, CB, P], F32, own), k.sb("cp_w2", [P, 2, P], F32, own)
                phase_rows(k, A)
                phase_compress_prompt(k, A)
                phase_attend_prompt(k, A)
            phase_attend_samples(k, A)
        phase_out(k, A)
        k.h2rows = k.sb("h2rows", [P, NTT, D])
        k.slot, k.weight = k.sb("slot", [P, NTT, N_BLK + 2]), k.sb("weight", [P, NTT, N_BLK + 2])
        k.slots, k.expert = k.sb("slots", [P, SLOTS]), k.sb("expert", [1, N_BLK + 1], I32)
        moe = ctx.enter_context(ExitStack())
        expert_buffers(k, moe)
        k.acc = k.mixT
        with ExitStack() as c:
            k.h2T = k.sb("h2T", [P, KT, NT], F32, c)
            norm_block(k, "g", k.xT, k.h2T, C_NORM2, 48, 64)
            phase_route(k, A)
        phase_moe(k, A)
        moe.close()
        phase_final(k, A)


_INS = (
    "x_prompt", "x_sample", "c_prompt", "c_sample", "cache_cmp_kv", "cache_slc_kv", "page_table",
    "state_win_kv", "state_wkv", "state_shift", "w_ada", "b_ada", "norm1", "w_in", "cmp_k_w1", "cmp_k_pe",
    "cmp_k_w2", "cmp_v_w1", "cmp_v_pe", "cmp_v_w2", "mu_rkv", "mu_wag", "decay_w0", "decay_w1", "decay_w2",
    "iclr_a0", "iclr_a1", "iclr_a2", "gate_g1", "gate_g2", "k_k", "k_a", "r_k", "ln_x_w", "ln_x_b", "w_out",
    "norm2", "w_router_group", "b_router_group", "w_router_expert", "b_router_expert", "w_gate", "w_up",
    "w_down", "norm_f",
)
_OUTS = (
    ("y_prompt", (1, 256, 2048)),
    ("y_sample", (8, 4, 2048)),
    ("cmp_kv_prompt", (1, 1, 256, 2, 2, 128)),
    ("cmp_kv_sample", (1, 8, 4, 2, 2, 128)),
    ("slc_kv_prompt", (1, 1, 256, 2, 2, 128)),
    ("slc_kv_sample", (1, 8, 4, 2, 2, 128)),
    ("win_kv_prompt", (1, 1, 512, 2, 2, 128)),
    ("win_kv_sample", (1, 8, 512, 2, 2, 128)),
    ("wkv_prompt", (1, 1, 16, 64, 64)),
    ("wkv_sample", (1, 8, 16, 64, 64)),
    ("shift_prompt", (1, 1, 2048)),
    ("shift_sample", (1, 8, 2048)),
)


def kernel(**inputs):
    import numpy as _np
    import concourse.bacc as _bacc
    from concourse import mybir as _mybir
    from concourse.bass_utils import run_bass_kernel_spmd as _run

    nc = _bacc.Bacc("TRN2", target_bir_lowering=False, num_devices=1)
    arrays, args = {}, {}
    for name in _INS:
        a = _np.ascontiguousarray(inputs[name])
        arrays[f"in_{name}_dram"] = a
        args[name] = nc.dram_tensor(f"in_{name}_dram", a.shape, _mybir.dt.from_np(a.dtype), kind="ExternalInput").ap()
    for name, shape in _OUTS:
        args[name] = nc.dram_tensor(f"out_{name}_dram", shape, _mybir.dt.float32, kind="ExternalOutput").ap()
    step_kernel(nc, args)
    r = _run(nc, [arrays], core_ids=[0])
    return tuple(r.results[0][f"out_{name}_dram"] for name, _ in _OUTS)
```
